# Optimizing a Trainium2 kernel written in Bass

```python
import jax
import jax.numpy as jnp
from jax import lax
import numpy as np
import math

D_MODEL = 1024
BATCH = 1
SEQ = 512
DEPTH = 1

CTX_LEN = 256
GRID_W = 64
N_MOD = 6
ADA_SCALE = 0.5
LN_EPS = 1e-5
DN_ALPHA = (2 * DEPTH) ** 0.25
DN_BETA = (8 * DEPTH) ** -0.25

SSD_HEADS = 8
SSD_HEAD_DIM = 64
SSD_INNER = SSD_HEADS * SSD_HEAD_DIM
SSD_GROUPS = 2
SSD_STATE = 128
SSD_CONV = 3
SSD_CHUNK = 128
SSD_XBC = SSD_INNER + 2 * SSD_GROUPS * SSD_STATE

RWKV_HEADS = 4
RWKV_HEAD_DIM = 64
RWKV_WIDTH = RWKV_HEADS * RWKV_HEAD_DIM
RWKV_DECAY_LORA = 64
RWKV_ICLR_LORA = 64
RWKV_GATE_LORA = 128
RWKV_COLS = 3 * RWKV_WIDTH + 2 * RWKV_DECAY_LORA + 2 * RWKV_ICLR_LORA + RWKV_GATE_LORA
RWKV_LNX_EPS = 64e-5

GLA_HEADS = 4
GLA_KEY_DIM = 32
GLA_VAL_DIM = 64
GLA_K_WIDTH = GLA_HEADS * GLA_KEY_DIM
GLA_V_WIDTH = GLA_HEADS * GLA_VAL_DIM
GLA_GATE_LORA = 16
GLA_GATE_NORMALIZER = 16.0
GLA_CHUNK = 16

MIX_WIDTH = SSD_INNER + RWKV_WIDTH + GLA_V_WIDTH
IN_WIDTHS = (SSD_INNER, SSD_XBC, 2 * SSD_HEADS, RWKV_COLS, GLA_K_WIDTH, GLA_K_WIDTH, GLA_V_WIDTH, 2 * GLA_GATE_LORA, GLA_V_WIDTH)
N_IN = SSD_INNER + SSD_XBC + 2 * SSD_HEADS + RWKV_COLS + 2 * GLA_K_WIDTH + 2 * GLA_V_WIDTH + 2 * GLA_GATE_LORA

N_EXPERTS = 64
TOP_K = 8
N_GROUPS = 8
TOPK_GROUPS = 4
EXPERT_DIM = 256
SHARED_DIM = 256
ROUTED_SCALE = 2.5
MOE_BLOCK = 128


def _split(z, widths):
    return jnp.split(z, [int(i) for i in np.cumsum(widths)[:-1]], axis=-1)

def _layernorm(x, w=None, b=None, eps=LN_EPS):
    xf = x.astype(jnp.float32)
    mu = jnp.mean(xf, -1, keepdims=True)
    var = jnp.mean(jnp.square(xf - mu), -1, keepdims=True)
    y = (xf - mu) * lax.rsqrt(var + eps)
    if w is not None:
        y = y * w.astype(jnp.float32) + b.astype(jnp.float32)
    return y.astype(x.dtype)

def _rmsnorm_groups(x, w, group, eps=1e-5):
    xf = x.astype(jnp.float32)
    shp = xf.shape
    g = xf.reshape(shp[:-1] + (shp[-1] // group, group))
    g = g * lax.rsqrt(jnp.mean(g * g, -1, keepdims=True) + eps)
    return (g.reshape(shp) * w.astype(jnp.float32)).astype(x.dtype)

def _seg_flip(z, n_ctx):
    return jnp.concatenate([jnp.flip(z[:, :n_ctx], 1), jnp.flip(z[:, n_ctx:], 1)], axis=1)

def _dwconv_centred(z, w, b):
    ch = z.shape[-1]
    pad = (SSD_CONV - 1) // 2
    y = lax.conv_general_dilated(z, w[:, None, :].astype(z.dtype), window_strides=(1,), padding=[(pad, pad)],
                                 dimension_numbers=('NWC', 'WIO', 'NWC'), feature_group_count=ch)
    return y + b

def _seq_shift_mix(z, mu_prev, mu_next):
    prev = jnp.pad(z, ((0, 0), (1, 0), (0, 0)))[:, :-1]
    nxt = jnp.pad(z, ((0, 0), (0, 1), (0, 0)))[:, 1:]
    return z + mu_prev * (prev - z) + mu_next * (nxt - z)

def _grid_shift_mix(z, mu):
    b, s, ch = z.shape
    rows = s // GRID_W
    g = z.reshape(b, rows, GRID_W, ch)
    left = jnp.pad(g, ((0, 0), (0, 0), (1, 0), (0, 0)))[:, :, :-1]
    right = jnp.pad(g, ((0, 0), (0, 0), (0, 1), (0, 0)))[:, :, 1:]
    up = jnp.pad(g, ((0, 0), (1, 0), (0, 0), (0, 0)))[:, :-1]
    down = jnp.pad(g, ((0, 0), (0, 1), (0, 0), (0, 0)))[:, 1:]
    out = g + mu[0] * (left - g) + mu[1] * (right - g) + mu[2] * (up - g) + mu[3] * (down - g)
    return out.reshape(b, s, ch)

def _ssd_chunked(x, dt, log_a, bm, cm):
    n, t, h, p = x.shape
    g, ds = bm.shape[2], bm.shape[3]
    q = SSD_CHUNK
    nc = t // q
    rep = h // g
    b_h = jnp.repeat(bm, rep, axis=2).reshape(n, nc, q, h, ds)
    c_h = jnp.repeat(cm, rep, axis=2).reshape(n, nc, q, h, ds)
    xdt = (x * dt[..., None]).reshape(n, nc, q, h, p)
    acs = jnp.cumsum(log_a.reshape(n, nc, q, h), axis=2)
    acs_h = jnp.moveaxis(acs, 3, 1)
    tril = jnp.tril(jnp.ones((q, q), dtype=bool))
    seg = acs_h[..., :, None] - acs_h[..., None, :]
    lmat = jnp.exp(jnp.where(tril, seg, -jnp.inf))
    scores = jnp.einsum('nclhd,ncshd->nhcls', c_h, b_h) * lmat
    y_diag = jnp.einsum('nhcls,ncshp->nclhp', scores, xdt)
    decay_end = jnp.exp(acs[:, :, -1:, :] - acs)
    states = jnp.einsum('nclhd,nclh,nclhp->nchpd', b_h, decay_end, xdt)
    chunk_decay = jnp.exp(acs[:, :, -1, :])

    def step(hprev, inp):
        st, dec = inp
        return hprev * dec[..., None, None] + st, hprev

    h0 = jnp.zeros((n, h, p, ds), x.dtype)
    _, h_in = lax.scan(step, h0, (jnp.moveaxis(states, 1, 0), jnp.moveaxis(chunk_decay, 1, 0)))
    h_in = jnp.moveaxis(h_in, 0, 1)
    y_off = jnp.einsum('nclhd,nchpd,nclh->nclhp', c_h, h_in, jnp.exp(acs))
    return (y_diag + y_off).reshape(n, t, h, p)

def _rwkv7_scan(r, w, k, v, kk, a):
    n, t, h, dk = r.shape

    def step(S, inp):
        r_t, w_t, k_t, v_t, kk_t, a_t = inp
        sa = -jnp.einsum('nhvk,nhk->nhv', S, kk_t)
        S = S * w_t[:, :, None, :] + sa[..., None] * (kk_t * a_t)[:, :, None, :] + v_t[..., None] * k_t[:, :, None, :]
        return S, jnp.einsum('nhvk,nhk->nhv', S, r_t)

    S0 = jnp.zeros((n, h, dk, dk), r.dtype)
    xs = (jnp.moveaxis(r, 1, 0), jnp.moveaxis(w, 1, 0), jnp.moveaxis(k, 1, 0),
          jnp.moveaxis(v, 1, 0), jnp.moveaxis(kk, 1, 0), jnp.moveaxis(a, 1, 0))
    _, y = lax.scan(step, S0, xs)
    return jnp.moveaxis(y, 0, 1)

def _gla_chunked(q, k, v, log_a):
    n, t, h, dk = q.shape
    dv = v.shape[-1]
    c = GLA_CHUNK
    nc = t // c
    q = q.reshape(n, nc, c, h, dk)
    k = k.reshape(n, nc, c, h, dk)
    v = v.reshape(n, nc, c, h, dv)
    acs = jnp.cumsum(log_a.reshape(n, nc, c, h, dk), axis=2)
    tril = jnp.tril(jnp.ones((c, c), dtype=bool))[:, :, None, None]
    seg = acs[:, :, :, None] - acs[:, :, None, :]
    decay = jnp.exp(jnp.where(tril, seg, -jnp.inf))
    scores = jnp.einsum('ncihd,ncjhd,ncijhd->nchij', q, k, decay)
    o_intra = jnp.einsum('nchij,ncjhv->ncihv', scores, v)
    q_dec = q * jnp.exp(acs)
    k_dec = k * jnp.exp(acs[:, :, -1:] - acs)
    states = jnp.einsum('ncjhd,ncjhv->nchdv', k_dec, v)
    chunk_decay = jnp.exp(acs[:, :, -1])

    def step(S, inp):
        st, dec = inp
        return S * dec[..., None] + st, S

    S0 = jnp.zeros((n, h, dk, dv), q.dtype)
    _, s_in = lax.scan(step, S0, (jnp.moveaxis(states, 1, 0), jnp.moveaxis(chunk_decay, 1, 0)))
    s_in = jnp.moveaxis(s_in, 0, 1)
    o_inter = jnp.einsum('ncihd,nchdv->ncihv', q_dec, s_in)
    return (o_intra + o_inter).reshape(n, t, h, dv)

def _token_mixer(u, n_ctx, w_in, ssd_conv_w, ssd_conv_b, ssd_dt_bias, ssd_a_log, ssd_d, ssd_norm_w,
                 rwkv_mu, rwkv_w0, rwkv_w2, rwkv_a0, rwkv_a2, rwkv_g2, rwkv_kk, rwkv_ka, rwkv_rk,
                 rwkv_lnx_w, rwkv_lnx_b, gla_gu, gla_gb, gla_norm_w, w_out):
    f32 = jnp.float32
    bsz, t, _ = u.shape
    flip = lambda zz: _seg_flip(zz, n_ctx)

    def both(fwd, bwd):
        s = jnp.stack([fwd, flip(bwd)])
        return s.reshape((2 * bsz,) + s.shape[2:])

    def unboth(y):
        y = y.reshape((2, bsz) + y.shape[1:])
        return y[0] + flip(y[1])

    z, xbc, dt, rw, gq, gk, gv, gd, og = _split(u @ w_in, IN_WIDTHS)

    xbc = jax.nn.silu(jnp.concatenate([_dwconv_centred(xbc[:, :n_ctx], ssd_conv_w, ssd_conv_b),
                                       _dwconv_centred(xbc[:, n_ctx:], ssd_conv_w, ssd_conv_b)], axis=1))
    xs, bm, cm = _split(xbc.astype(f32), (SSD_INNER, SSD_GROUPS * SSD_STATE, SSD_GROUPS * SSD_STATE))
    xs = xs.reshape(bsz, t, SSD_HEADS, SSD_HEAD_DIM)
    bm = bm.reshape(bsz, t, SSD_GROUPS, SSD_STATE)
    cm = cm.reshape(bsz, t, SSD_GROUPS, SSD_STATE)
    dt = jax.nn.softplus(dt.astype(f32).reshape(bsz, t, 2, SSD_HEADS) + ssd_dt_bias.astype(f32))
    neg_a = -jnp.exp(ssd_a_log.astype(f32))
    dt_f, dt_b = dt[:, :, 0], dt[:, :, 1]
    y = unboth(_ssd_chunked(both(xs, xs), both(dt_f, dt_b), both(dt_f * neg_a[0], dt_b * neg_a[1]),
                            both(bm, bm), both(cm, cm)))
    y = y + ssd_d.astype(f32)[:, None] * xs
    y_ssd = _rmsnorm_groups(y.reshape(bsz, t, SSD_INNER) * jax.nn.silu(z.astype(f32)), ssd_norm_w,
                            SSD_INNER // SSD_GROUPS)

    rw = jnp.concatenate([_seq_shift_mix(rw[:, :n_ctx], rwkv_mu[0], rwkv_mu[1]),
                          _grid_shift_mix(rw[:, n_ctx:], rwkv_mu)], axis=1)
    r, k, v, wd_f, wd_b, ad_f, ad_b, gd_r = _split(
        rw.astype(f32), (RWKV_WIDTH,) * 3 + (RWKV_DECAY_LORA,) * 2 + (RWKV_ICLR_LORA,) * 2 + (RWKV_GATE_LORA,))
    hd = lambda zz: zz.reshape(bsz, t, RWKV_HEADS, RWKV_HEAD_DIM)
    decay = lambda wd, i: jnp.exp(-jnp.exp(-jax.nn.softplus(-(rwkv_w0[i] + jnp.tanh(wd) @ rwkv_w2[i])) - 0.5))
    iclr = lambda ad, i: jax.nn.sigmoid(rwkv_a0[i] + ad @ rwkv_a2[i])
    w_f, w_b = hd(decay(wd_f, 0)), hd(decay(wd_b, 1))
    a_f, a_b = hd(iclr(ad_f, 0)), hd(iclr(ad_b, 1))
    r, k, v = hd(r), hd(k), hd(v)
    kk = k * rwkv_kk.reshape(RWKV_HEADS, RWKV_HEAD_DIM)
    kk = kk / jnp.maximum(jnp.sqrt(jnp.sum(kk * kk, -1, keepdims=True)), 1e-12)
    ka = rwkv_ka.reshape(RWKV_HEADS, RWKV_HEAD_DIM)
    k_f = k * (1.0 + (a_f - 1.0) * ka)
    k_b = k * (1.0 + (a_b - 1.0) * ka)
    y = unboth(_rwkv7_scan(both(r, r), both(w_f, w_b), both(k_f, k_b), both(v, v), both(kk, kk), both(a_f, a_b)))
    mu = jnp.mean(y, -1, keepdims=True)
    var = jnp.mean(jnp.square(y - mu), -1, keepdims=True)
    y = ((y - mu) * lax.rsqrt(var + RWKV_LNX_EPS)).reshape(bsz, t, RWKV_WIDTH) * rwkv_lnx_w + rwkv_lnx_b
    bonus = (jnp.sum(r * (k_f + k_b) * rwkv_rk, -1, keepdims=True) * v).reshape(bsz, t, RWKV_WIDTH)
    y_rwkv = (y + bonus) * (jax.nn.sigmoid(gd_r) @ rwkv_g2)

    gh = lambda zz, d: zz.reshape(bsz, t, GLA_HEADS, d)
    q = gh(gq.astype(f32), GLA_KEY_DIM) * GLA_KEY_DIM ** -0.5
    kg = gh(gk.astype(f32), GLA_KEY_DIM)
    vg = gh(gv.astype(f32), GLA_VAL_DIM)
    gd_f, gd_b = _split(gd.astype(f32), (GLA_GATE_LORA, GLA_GATE_LORA))
    la = lambda gg, i: gh(jax.nn.log_sigmoid(gg @ gla_gu[i] + gla_gb[i]) / GLA_GATE_NORMALIZER, GLA_KEY_DIM)
    o = unboth(_gla_chunked(both(q, q), both(kg, kg), both(vg, vg), both(la(gd_f, 0), la(gd_b, 1))))
    y_gla = _rmsnorm_groups(o.reshape(bsz, t, GLA_V_WIDTH), gla_norm_w, GLA_VAL_DIM) * jax.nn.silu(og.astype(f32))

    y_mix = jnp.concatenate([y_ssd, y_rwkv, y_gla], axis=-1).astype(u.dtype)
    return y_mix @ w_out

def _moe_ffn(h, router_w, router_b, w1, w3, w2, sw1, sw3, sw2):
    f32 = jnp.float32
    t = h.shape[0]
    per_group = N_EXPERTS // N_GROUPS
    scores = jax.nn.sigmoid((h @ router_w).astype(f32))
    sel = scores + router_b.astype(f32)
    grp_score = lax.top_k(sel.reshape(t, N_GROUPS, per_group), 2)[0].sum(-1)
    _, top_g = lax.top_k(grp_score, TOPK_GROUPS)
    gmask = jax.nn.one_hot(top_g, N_GROUPS, dtype=f32).sum(1) > 0
    sel = jnp.where(jnp.repeat(gmask, per_group, axis=1), sel, -jnp.inf)
    _, idx = lax.top_k(sel, TOP_K)
    wts = jnp.take_along_axis(scores, idx, axis=1)
    wts = wts / jnp.sum(wts, -1, keepdims=True) * ROUTED_SCALE

    n_assign = t * TOP_K
    flat_e = idx.reshape(-1)
    order = jnp.argsort(flat_e)
    sorted_e = flat_e[order]
    counts = jnp.bincount(flat_e, length=N_EXPERTS)
    padded = (counts + MOE_BLOCK - 1) // MOE_BLOCK * MOE_BLOCK
    pend = jnp.cumsum(padded)
    pstart = pend - padded
    sstart = jnp.cumsum(counts) - counts
    dest = pstart[sorted_e] + jnp.arange(n_assign, dtype=jnp.int32) - sstart[sorted_e]
    n_rows = -(-n_assign // MOE_BLOCK) * MOE_BLOCK + N_EXPERTS * MOE_BLOCK
    n_blocks = n_rows // MOE_BLOCK
    row_tok = jnp.zeros((n_rows,), jnp.int32).at[dest].set((order // TOP_K).astype(jnp.int32))
    row_w = jnp.zeros((n_rows,), f32).at[dest].set(wts.reshape(-1)[order])
    block_e = jnp.minimum(jnp.searchsorted(pend, jnp.arange(n_blocks, dtype=jnp.int32) * MOE_BLOCK, side='right'),
                          N_EXPERTS - 1)

    def body(acc, blk):
        tok, wt, e = blk
        xb = h[tok]
        hid = jax.nn.silu(xb @ w1[e]) * (xb @ w3[e])
        return acc.at[tok].add(wt[:, None] * (hid @ w2[e]).astype(f32)), None

    routed, _ = lax.scan(body, jnp.zeros(h.shape, f32),
                         (row_tok.reshape(n_blocks, MOE_BLOCK), row_w.reshape(n_blocks, MOE_BLOCK), block_e))
    shared = (jax.nn.silu(h @ sw1) * (h @ sw3)) @ sw2
    return routed.astype(h.dtype) + shared

def first_inputs(seed: int = 0) -> dict:
    key = jax.random.key(seed)
    ks = jax.random.split(key, 40)
    L, D, E, F, Fs = DEPTH, D_MODEL, N_EXPERTS, EXPERT_DIM, SHARED_DIM
    nrm = lambda k, shape, s: jax.random.normal(k, shape, jnp.float32) * s
    one = lambda k, shape: 1.0 + 0.1 * jax.random.normal(k, shape, jnp.float32)
    dt0 = jnp.exp(jax.random.uniform(ks[9], (L, 2, SSD_HEADS), jnp.float32, np.log(1e-3), np.log(1e-1)))
    return {
        'x': nrm(ks[0], (BATCH, SEQ, D), 1.0),
        'c': nrm(ks[1], (BATCH, D), 1.0),
        'ctx': nrm(ks[2], (BATCH, CTX_LEN, D), 1.0),
        'c_ctx': nrm(ks[3], (D,), 1.0),
        'ada_w': nrm(ks[4], (L, D, N_MOD * D), D ** -0.5 * ADA_SCALE),
        'ada_b': nrm(ks[5], (L, N_MOD * D), 0.02),
        'w_in': nrm(ks[6], (L, D, N_IN), D ** -0.5),
        'ssd_conv_w': nrm(ks[7], (L, SSD_CONV, SSD_XBC), SSD_CONV ** -0.5),
        'ssd_conv_b': nrm(ks[8], (L, SSD_XBC), 0.02),
        'ssd_dt_bias': dt0 + jnp.log(-jnp.expm1(-dt0)),
        'ssd_a_log': jnp.log(jax.random.uniform(ks[10], (L, 2, SSD_HEADS), jnp.float32, 1.0, 16.0)),
        'ssd_d': one(ks[11], (L, SSD_HEADS)),
        'ssd_norm_w': one(ks[12], (L, SSD_INNER)),
        'rwkv_mu': jax.random.uniform(ks[13], (L, 4, RWKV_COLS), jnp.float32, 0.0, 0.5),
        'rwkv_w0': jax.random.uniform(ks[14], (L, 2, RWKV_WIDTH), jnp.float32, -6.0, 1.0),
        'rwkv_w2': nrm(ks[15], (L, 2, RWKV_DECAY_LORA, RWKV_WIDTH), 0.1),
        'rwkv_a0': nrm(ks[16], (L, 2, RWKV_WIDTH), 0.1),
        'rwkv_a2': nrm(ks[17], (L, 2, RWKV_ICLR_LORA, RWKV_WIDTH), 0.1),
        'rwkv_g2': nrm(ks[18], (L, RWKV_GATE_LORA, RWKV_WIDTH), RWKV_GATE_LORA ** -0.5),
        'rwkv_kk': one(ks[19], (L, RWKV_WIDTH)),
        'rwkv_ka': one(ks[20], (L, RWKV_WIDTH)),
        'rwkv_rk': nrm(ks[21], (L, RWKV_HEADS, RWKV_HEAD_DIM), 0.1),
        'rwkv_lnx_w': one(ks[22], (L, RWKV_WIDTH)),
        'rwkv_lnx_b': nrm(ks[23], (L, RWKV_WIDTH), 0.02),
        'gla_gu': nrm(ks[24], (L, 2, GLA_GATE_LORA, GLA_K_WIDTH), GLA_GATE_LORA ** -0.5),
        'gla_gb': nrm(ks[25], (L, 2, GLA_K_WIDTH), 0.5),
        'gla_norm_w': one(ks[26], (L, GLA_V_WIDTH)),
        'w_out': nrm(ks[27], (L, MIX_WIDTH, D), MIX_WIDTH ** -0.5 * DN_BETA),
        'ln1_w': one(ks[28], (L, D)),
        'ln1_b': nrm(ks[29], (L, D), 0.02),
        'ln2_w': one(ks[30], (L, D)),
        'ln2_b': nrm(ks[31], (L, D), 0.02),
        'router_w': nrm(ks[32], (L, D, E), D ** -0.5),
        'router_b': nrm(ks[33], (L, E), 0.01),
        'exp_w1': nrm(ks[34], (L, E, D, F), D ** -0.5),
        'exp_w3': nrm(ks[35], (L, E, D, F), D ** -0.5),
        'exp_w2': nrm(ks[36], (L, E, F, D), F ** -0.5 * DN_BETA),
        'sh_w1': nrm(ks[37], (L, D, Fs), D ** -0.5),
        'sh_w3': nrm(ks[38], (L, D, Fs), D ** -0.5),
        'sh_w2': nrm(ks[39], (L, Fs, D), Fs ** -0.5 * DN_BETA),
    }

def first_block(x, c, ctx, c_ctx, ada_w, ada_b, w_in, ssd_conv_w, ssd_conv_b, ssd_dt_bias, ssd_a_log, ssd_d,
              ssd_norm_w, rwkv_mu, rwkv_w0, rwkv_w2, rwkv_a0, rwkv_a2, rwkv_g2, rwkv_kk, rwkv_ka, rwkv_rk,
              rwkv_lnx_w, rwkv_lnx_b, gla_gu, gla_gb, gla_norm_w, w_out, ln1_w, ln1_b, ln2_w, ln2_b,
              router_w, router_b, exp_w1, exp_w3, exp_w2, sh_w1, sh_w3, sh_w2):
    n_ctx = ctx.shape[1]
    xc = ctx
    for l in range(DEPTH):
        mod = jnp.split(jax.nn.silu(c) @ ada_w[l] + ada_b[l], N_MOD, axis=-1)
        modc = jnp.split(jax.nn.silu(c_ctx) @ ada_w[l] + ada_b[l], N_MOD, axis=-1)
        sh1, sc1, g1, sh2, sc2, g2 = [m[:, None, :] for m in mod]
        sh1c, sc1c, g1c, sh2c, sc2c, g2c = modc

        u = jnp.concatenate([_layernorm(xc) * (1.0 + sc1c) + sh1c,
                             _layernorm(x) * (1.0 + sc1) + sh1], axis=1)
        mix = _token_mixer(u, n_ctx, w_in[l], ssd_conv_w[l], ssd_conv_b[l], ssd_dt_bias[l], ssd_a_log[l], ssd_d[l],
                           ssd_norm_w[l], rwkv_mu[l], rwkv_w0[l], rwkv_w2[l], rwkv_a0[l], rwkv_a2[l], rwkv_g2[l],
                           rwkv_kk[l], rwkv_ka[l], rwkv_rk[l], rwkv_lnx_w[l], rwkv_lnx_b[l], gla_gu[l], gla_gb[l],
                           gla_norm_w[l], w_out[l])
        x = _layernorm(DN_ALPHA * x + g1 * mix[:, n_ctx:], ln1_w[l], ln1_b[l])
        xc = _layernorm(DN_ALPHA * xc + g1c * mix[:, :n_ctx], ln1_w[l], ln1_b[l])

        h = _layernorm(x) * (1.0 + sc2) + sh2
        moe_w = (router_w[l], router_b[l], exp_w1[l], exp_w3[l], exp_w2[l], sh_w1[l], sh_w3[l], sh_w2[l])
        if l < DEPTH - 1:
            hc = _layernorm(xc) * (1.0 + sc2c) + sh2c
            tok = jnp.concatenate([hc, h], axis=1)
            f = _moe_ffn(tok.reshape(-1, D_MODEL), *moe_w).reshape(tok.shape)
            xc = _layernorm(DN_ALPHA * xc + g2c * f[:, :n_ctx], ln2_w[l], ln2_b[l])
            f = f[:, n_ctx:]
        else:
            f = _moe_ffn(h.reshape(-1, D_MODEL), *moe_w).reshape(h.shape)
        x = _layernorm(DN_ALPHA * x + g2 * f, ln2_w[l], ln2_b[l])
    return x


DEPTH_2 = 2

CHUNK = 64
Q_BLOCK = 128
ROPE_THETA = 10000.0
RMS_EPS = 1e-6

A_HEADS = D_MODEL // 128
A_HEAD_DIM = 64
D_A = A_HEADS * A_HEAD_DIM
IDX_HEADS = 8
IDX_DIM = 32
TOPK_MAX = 256

B_HEADS = D_MODEL // 256
B_HEAD_DIM = 64
D_B = B_HEADS * 2 * B_HEAD_DIM

D_MIX = D_A + D_B
D_FF = -(-8 * D_MODEL // (3 * 256)) * 256

IN_SPLITS = (D_A, D_A, D_A, IDX_HEADS * IDX_DIM, IDX_DIM, IDX_HEADS, D_B, D_B, D_B)
D_IN = D_A * 3 + IDX_HEADS * IDX_DIM + IDX_DIM + IDX_HEADS + D_B * 3


def rms_norm(x, g):
    x32 = x.astype(jnp.float32)
    r = lax.rsqrt(jnp.mean(x32 * x32, axis=-1, keepdims=True) + RMS_EPS)
    return (x32 * r * g.astype(jnp.float32)).astype(x.dtype)

def rope_tables(seq_len, dim):
    pos = jnp.arange(seq_len, dtype=jnp.float32)
    inv = ROPE_THETA ** (-jnp.arange(0, dim, 2, dtype=jnp.float32) / dim)
    ang = pos[:, None] * inv[None, :]
    return jnp.cos(ang), jnp.sin(ang)

def apply_rope(x, cos, sin):
    half = x.shape[-1] // 2
    x32 = x.astype(jnp.float32)
    x1, x2 = x32[..., :half], x32[..., half:]
    c = cos[None, :, None, :]
    s = sin[None, :, None, :]
    return jnp.concatenate([x1 * c - x2 * s, x2 * c + x1 * s], axis=-1).astype(x.dtype)

def to_blocks(a):
    b, s = a.shape[:2]
    return jnp.swapaxes(a.reshape(b, s // Q_BLOCK, Q_BLOCK, *a.shape[2:]), 0, 1)

def from_blocks(a):
    nb, b = a.shape[:2]
    return jnp.swapaxes(a, 0, 1).reshape(b, nb * a.shape[2], *a.shape[3:])

def dsa_mixer(q, k, v, iq, ik, iw):
    s_len = q.shape[1]
    topk = min(TOPK_MAX, s_len // 4)
    key_chunk = jnp.arange(s_len) // CHUNK
    scale = A_HEAD_DIM ** -0.5
    gather = jax.vmap(lambda a, i: a[i])

    def block(args):
        bi, qb, iqb, iwb = args
        q_chunk = (bi * Q_BLOCK + jnp.arange(Q_BLOCK)) // CHUNK
        admissible = key_chunk[None, :] <= q_chunk[:, None]
        dots = jnp.einsum('bqhd,bsd->bqhs', iqb, ik,
                          preferred_element_type=jnp.float32) * (IDX_DIM ** -0.5)
        w = iwb.astype(jnp.float32) * (IDX_HEADS ** -0.5)
        score = jnp.einsum('bqhs,bqh->bqs', jax.nn.relu(dots), w)
        score = jnp.where(admissible[None], score, -jnp.inf)
        _, idx = lax.top_k(score, topk)
        k_sel = gather(k, idx)
        v_sel = gather(v, idx)
        valid = (idx // CHUNK) <= q_chunk[None, :, None]
        logits = jnp.einsum('bqhd,bqkhd->bhqk', qb, k_sel,
                            preferred_element_type=jnp.float32) * scale
        logits = jnp.where(valid[:, None], logits, -jnp.inf)
        p = jax.nn.softmax(logits, axis=-1)
        return jnp.einsum('bhqk,bqkhd->bqhd', p.astype(v.dtype), v_sel)

    nb = s_len // Q_BLOCK
    out = lax.map(block, (jnp.arange(nb), to_blocks(q), to_blocks(iq), to_blocks(iw)))
    return from_blocks(out)

def diff_mixer(q, k, v, lam, lam_init, g_subln):
    s_len = q.shape[1]
    key_chunk = jnp.arange(s_len) // CHUNK
    scale = B_HEAD_DIM ** -0.5

    def block(args):
        bi, qb = args
        q_chunk = (bi * Q_BLOCK + jnp.arange(Q_BLOCK)) // CHUNK
        admissible = key_chunk[None, :] <= q_chunk[:, None]
        logits = jnp.einsum('bqhcd,bshcd->bchqs', qb, k,
                            preferred_element_type=jnp.float32) * scale
        logits = jnp.where(admissible[None, None, None], logits, -jnp.inf)
        p = jax.nn.softmax(logits, axis=-1)
        attn = p[:, 0] - lam * p[:, 1]
        return jnp.einsum('bhqs,bshe->bqhe', attn.astype(v.dtype), v)

    nb = s_len // Q_BLOCK
    out = from_blocks(lax.map(block, (jnp.arange(nb), to_blocks(q))))
    return rms_norm(out, g_subln) * (1.0 - lam_init)

def second_inputs(seed: int = 0) -> dict:
    key = jax.random.key(seed)
    ks = jax.random.split(key, 14)
    f32 = jnp.float32
    nrm = lambda k, shape, fan_in: jax.random.normal(k, shape, f32) * (fan_in ** -0.5)
    gain = lambda k, shape: 1.0 + 0.02 * jax.random.normal(k, shape, f32)
    return {
        "x": jax.random.normal(ks[0], (BATCH, SEQ, D_MODEL), f32),
        "w_in": nrm(ks[1], (DEPTH_2, D_MODEL, D_IN), D_MODEL),
        "w_out": nrm(ks[2], (DEPTH_2, D_MIX, D_MODEL), D_MIX),
        "g_mix": gain(ks[3], (DEPTH_2, D_MODEL)),
        "lam_q1": 0.1 * jax.random.normal(ks[4], (DEPTH_2, B_HEAD_DIM), f32),
        "lam_k1": 0.1 * jax.random.normal(ks[5], (DEPTH_2, B_HEAD_DIM), f32),
        "lam_q2": 0.1 * jax.random.normal(ks[6], (DEPTH_2, B_HEAD_DIM), f32),
        "lam_k2": 0.1 * jax.random.normal(ks[7], (DEPTH_2, B_HEAD_DIM), f32),
        "g_subln": gain(ks[8], (DEPTH_2, 2 * B_HEAD_DIM)),
        "g_ffn": gain(ks[9], (DEPTH_2, D_MODEL)),
        "w_gate": nrm(ks[10], (DEPTH_2, D_MODEL, D_FF), D_MODEL),
        "w_up": nrm(ks[11], (DEPTH_2, D_MODEL, D_FF), D_MODEL),
        "w_down": nrm(ks[12], (DEPTH_2, D_FF, D_MODEL), D_FF),
        "g_final": gain(ks[13], (D_MODEL,)),
    }

def second_block(x, w_in, w_out, g_mix, lam_q1, lam_k1, lam_q2, lam_k2, g_subln,
              g_ffn, w_gate, w_up, w_down, g_final):
    b_, s_len, _ = x.shape
    cos_a, sin_a = rope_tables(s_len, A_HEAD_DIM)
    cos_i, sin_i = rope_tables(s_len, IDX_DIM)
    cos_b, sin_b = rope_tables(s_len, B_HEAD_DIM)
    split_points = [int(o) for o in np.cumsum(IN_SPLITS)[:-1]]

    for layer in range(DEPTH_2):
        h = rms_norm(x, g_mix[layer])
        proj = jnp.einsum('bsd,dc->bsc', h, w_in[layer])
        qa, ka, va, iq, ik, iw, qb, kb, vb = jnp.split(proj, split_points, axis=-1)

        qa = apply_rope(qa.reshape(b_, s_len, A_HEADS, A_HEAD_DIM), cos_a, sin_a)
        ka = apply_rope(ka.reshape(b_, s_len, A_HEADS, A_HEAD_DIM), cos_a, sin_a)
        va = va.reshape(b_, s_len, A_HEADS, A_HEAD_DIM)
        iq = apply_rope(iq.reshape(b_, s_len, IDX_HEADS, IDX_DIM), cos_i, sin_i)
        ik = apply_rope(ik[:, :, None, :], cos_i, sin_i)[:, :, 0, :]
        out_a = dsa_mixer(qa, ka, va, iq, ik, iw).reshape(b_, s_len, D_A)

        qb = apply_rope(qb.reshape(b_, s_len, 2 * B_HEADS, B_HEAD_DIM), cos_b, sin_b)
        kb = apply_rope(kb.reshape(b_, s_len, 2 * B_HEADS, B_HEAD_DIM), cos_b, sin_b)
        qb = qb.reshape(b_, s_len, B_HEADS, 2, B_HEAD_DIM)
        kb = kb.reshape(b_, s_len, B_HEADS, 2, B_HEAD_DIM)
        vb = vb.reshape(b_, s_len, B_HEADS, 2 * B_HEAD_DIM)
        lam_init = 0.8 - 0.6 * math.exp(-0.3 * layer)
        lam = (jnp.exp(jnp.sum(lam_q1[layer].astype(jnp.float32) * lam_k1[layer].astype(jnp.float32)))
               - jnp.exp(jnp.sum(lam_q2[layer].astype(jnp.float32) * lam_k2[layer].astype(jnp.float32)))
               + lam_init)
        out_b = diff_mixer(qb, kb, vb, lam, lam_init, g_subln[layer]).reshape(b_, s_len, D_B)

        mixed = jnp.concatenate([out_a, out_b], axis=-1)
        x = x + jnp.einsum('bsc,cd->bsd', mixed, w_out[layer])

        h2 = rms_norm(x, g_ffn[layer])
        gate = jnp.einsum('bsd,df->bsf', h2, w_gate[layer])
        up = jnp.einsum('bsd,df->bsf', h2, w_up[layer])
        x = x + jnp.einsum('bsf,fd->bsd', jax.nn.silu(gate) * up, w_down[layer])

    return rms_norm(x, g_final)


def setup_inputs(seed=0):
    out = dict(first_inputs(seed))
    for name, value in second_inputs(seed + 1).items():
        if name != "x":
            out[name + "_2"] = value
    return out


def reference(
    x, c, ctx, c_ctx, ada_w, ada_b, w_in, ssd_conv_w, ssd_conv_b, ssd_dt_bias, ssd_a_log, ssd_d,
    ssd_norm_w, rwkv_mu, rwkv_w0, rwkv_w2, rwkv_a0, rwkv_a2, rwkv_g2, rwkv_kk, rwkv_ka, rwkv_rk,
    rwkv_lnx_w, rwkv_lnx_b, gla_gu, gla_gb, gla_norm_w, w_out, ln1_w, ln1_b, ln2_w, ln2_b,
    router_w, router_b, exp_w1, exp_w3, exp_w2, sh_w1, sh_w3, sh_w2, w_in_2, w_out_2, g_mix_2,
    lam_q1_2, lam_k1_2, lam_q2_2, lam_k2_2, g_subln_2, g_ffn_2, w_gate_2, w_up_2, w_down_2,
    g_final_2,
):
    x = first_block(
        x, c, ctx, c_ctx, ada_w, ada_b, w_in, ssd_conv_w, ssd_conv_b, ssd_dt_bias, ssd_a_log,
        ssd_d, ssd_norm_w, rwkv_mu, rwkv_w0, rwkv_w2, rwkv_a0, rwkv_a2, rwkv_g2, rwkv_kk,
        rwkv_ka, rwkv_rk, rwkv_lnx_w, rwkv_lnx_b, gla_gu, gla_gb, gla_norm_w, w_out, ln1_w,
        ln1_b, ln2_w, ln2_b, router_w, router_b, exp_w1, exp_w3, exp_w2, sh_w1, sh_w3, sh_w2,
    )
    return second_block(
        x, w_in_2, w_out_2, g_mix_2, lam_q1_2, lam_k1_2, lam_q2_2, lam_k2_2, g_subln_2, g_ffn_2,
        w_gate_2, w_up_2, w_down_2, g_final_2,
    )


_drawn_inputs = setup_inputs


def setup_inputs(seed=0):
    import zlib

    import numpy as np

    out = dict(_drawn_inputs(seed))
    spreads = {}
    factors = {'ssd_conv_b': 3.512,
     'ssd_d': 3.195,
     'rwkv_w2': 3.695,
     'rwkv_a0': 6.4,
     'rwkv_kk': 2.67,
     'rwkv_lnx_w': 3.084,
     'rwkv_lnx_b': 4.662,
     'gla_norm_w': 2.88,
     'g_subln_2': 3.53,
     'g_ffn_2': 2.874,
     'g_final_2': 2.796}
    for name, (base, spread) in spreads.items():
        noise = np.random.default_rng([zlib.crc32(name.encode()), seed]).standard_normal(out[name].shape)
        drawn = base * np.exp(spread * noise) if base else spread * noise
        out[name] = jnp.asarray(drawn.astype(out[name].dtype))
    for name, factor in factors.items():
        out[name] = (out[name] * factor).astype(out[name].dtype)
    return out
```

```python
import numpy as np
import concourse.bass as bass
from concourse import mybir
from contextlib import ExitStack

F32 = mybir.dt.float32
I32 = mybir.dt.int32
ALU = mybir.AluOpType
ACT = mybir.ActivationFunctionType
AX = mybir.AxisListType

D = 1024
NIN = 3504
E05 = float(np.exp(-0.5))
ALPHA = float(2 ** 0.25)

def _const_mats():
    i = np.arange(128)
    s, t = i[:, None], i[None, :]
    m = {}
    for d in range(2):
        le = (s <= t) if d == 0 else (s >= t)
        lt = (s < t) if d == 0 else (s > t)
        gt = (s > t) if d == 0 else (s < t)
        b64 = s // 64 == t // 64
        b16 = s // 16 == t // 16
        m[f"i128_{d}"] = le
        m[f"g128_{d}"] = gt
        m[f"i64_{d}"] = le & b64
        m[f"e64_{d}"] = lt & b64
        half = (s % 16 < 8) if d == 0 else (s % 16 >= 8)
        m[f"q16_{d}"] = (le & b16).astype(np.float32) - (half & b16)
        m[f"i16_{d}"] = le & b16
        m[f"c16_{d}"] = s // 16 == np.arange(8)[None, :]
        m[f"x16_{d}"] = gt & b16
        for k in range(6):
            w = 1 << k
            blk = s // (2 * w) == t // (2 * w)
            sh, th = (s // w) % 2, (t // w) % 2
            m[f"l{k}_{d}"] = blk & ((sh == 0) & (th == 1) if d == 0 else (sh == 1) & (th == 0))
    m["ones"] = np.ones((128, 128))
    m["ident"] = np.eye(128)
    m["h64"] = s // 64 == t // 64
    m["ch64"] = s // 64 == np.arange(2)[None, :]
    m["bd"] = s // 32 == np.arange(256)[None, :] // 64
    m["sw64"] = (s // 64 == t // 64) & ((s % 64 + 32) % 64 == t % 64)
    m["sw32"] = (s // 32 == t // 32) & ((s % 32 + 16) % 32 == t % 32)
    r0 = np.zeros((128, 128))
    r0[0] = 1
    m["row0"] = r0
    out, at, parts = {}, 0, []
    for k, v in m.items():
        v = np.asarray(v, np.float32)
        out[k] = (at, v.shape[1])
        parts.append(v)
        at += v.shape[1]
    return out, np.ascontiguousarray(np.concatenate(parts, 1))


def _rope_tables():
    out = []
    for dim in (64, 32):
        half = dim // 2
        inv = 10000.0 ** (-np.arange(0, dim, 2, dtype=np.float32) / np.float32(dim))
        ang = np.arange(512, dtype=np.float32)[:, None] * inv.astype(np.float32)[None, :]
        c, s = np.cos(ang).T, np.sin(ang).T
        p = np.arange(128) % dim
        out.append(c[p % half])
        out.append(np.where((p < half)[:, None], -s[p % half], s[p % half]))
    return np.ascontiguousarray(np.stack(out, 1).astype(np.float32))


COLS = [("conv_w", 24), ("conv_b", 8), ("mu", 36), ("a0", 4), ("kk", 2), ("ka", 2), ("rk", 2),
        ("lnw", 2), ("lnb", 2), ("c", 8), ("cc", 8), ("g_mix", 16), ("g_ffn", 16), ("g_sub", 2),
        ("gla_w", 2), ("ssd_w", 4)]
ROWS = [("dtb", 16), ("alog", 16), ("ssd_d", 8), ("w0", 512), ("gb", 256), ("ln1w", 1024), ("ln1b", 1024),
        ("ln2w", 1024), ("ln2b", 1024), ("rb", 64), ("gfin", 1024), ("lam", 512)]


def _offsets(items):
    o, at = {}, 0
    for n, w in items:
        o[n] = (at, w)
        at += w
    return o, at


CO, CN = _offsets(COLS)
RO, RN = _offsets(ROWS)


class Queues:

    def __init__(self, nc, ctx):
        self.nc, self.ctx = nc, ctx
        self.q = {e: [] for e in ("pe", "act", "dve", "pool", "sp")}
        self.sem = {e: ctx.enter_context(nc.semaphore("s_" + e)) for e in ("pe", "act", "dve", "pool")}
        self.n = {e: 0 for e in self.sem}
        self.seen = {e: {} for e in self.q}
        self.dsem = [ctx.enter_context(nc.semaphore(f"s_dma{i}")) for i in range(48)]
        self.dn = [0] * 48
        self.dnext = 0

    def wait(self, e, *toks):
        for t in toks:
            if t is None:
                continue
            if isinstance(t, list):
                self.wait(e, *t)
                continue
            name, s, v = t
            if self.seen[e].get(name, 0) >= v:
                continue
            self.seen[e][name] = v
            self.q[e].append(lambda eng, s=s, v=v: eng.wait_ge(s, v))

    def op(self, e, fn, *toks, chain=None):
        self.wait(e, *toks)
        if (e != "pe" if chain is None else chain) and self.n[e]:
            self.wait(e, (e, self.sem[e], self.n[e]))
        self.n[e] += 1
        s = self.sem[e]
        self.q[e].append(lambda eng: fn(eng).then_inc(s, 1))
        return (e, s, self.n[e])

    def last(self, e):
        return (e, self.sem[e], self.n[e]) if self.n[e] else None

    def all(self):
        return [self.last(e) for e in self.sem]

    def dma(self, e, fn, *toks):
        i = self.dnext
        self.dnext = (i + 1) % 48
        s = self.dsem[i]
        if self.dn[i]:
            self.wait(e, (f"d{i}", s, self.dn[i]))
        self.wait(e, *toks)
        self.dn[i] += 16
        self.q[e].append(lambda eng: fn(eng).then_inc(s, 16))
        return (f"d{i}", s, self.dn[i])

    def barrier(self, engines=("pe", "act", "dve", "pool")):
        toks = self.all()
        for e in engines:
            self.wait(e, *toks)

    def emit(self):
        block = self.ctx.enter_context(self.nc.Block())
        for e, deco in (("sp", block.sync), ("act", block.scalar), ("dve", block.vector),
                        ("pool", block.gpsimd), ("pe", block.tensor)):
            lst = self.q[e]

            def body(eng, lst=lst):
                for f in lst:
                    f(eng)
            deco(body)


def run(*gens):
    gens = list(gens)
    while gens:
        for g in list(gens):
            try:
                next(g)
            except StopIteration:
                gens.remove(g)


class Ring:

    def __init__(self, K, buf, size):
        self.K, self.buf, self.size, self.pos, self.live = K, buf, size, 0, []

    def take(self, n):
        if self.pos + n > self.size:
            self.pos = 0
        a, b = self.pos, self.pos + n
        self.pos = b
        over = [x for x in self.live if x[0] < b and a < x[1]]
        self.live = [x for x in self.live if not (x[0] < b and a < x[1])]
        ent = [a, b, None]
        self.live.append(ent)
        for x in over:
            assert x[2] is not None, "ring slot still in use"
        return ent, self.buf[:, a:b], [x[2] for x in over]

    def load(self, srcs, n):
        ent, ap, over = self.take(n)
        toks = []
        for o, w, a, src in srcs:
            dst = ap[:, o:o + w]
            if a:
                dst = dst.rearrange("p (a b) -> p a b", a=a)
            toks.append(self.K.dma("sp", lambda e, dst=dst, src=src: e.dma_start(dst, src), over))
        return ent, ap, toks


def build(nc, A, out, DBG=None):
    ctx = ExitStack()
    with ctx:
        _program(nc, ctx, A, out, DBG)


def _program(nc, ctx, A, out, DBG):
    K = Queues(nc, ctx)
    op = K.op
    cmap, _ = _const_mats()

    def sb(name, shape, dt=F32, c=ctx):
        return c.enter_context(nc.sbuf_tensor(name, shape, dt))

    banks = [ctx.enter_context(nc.psum_tensor(f"ps{i}", [128, 512], F32)) for i in range(8)]
    free = [(b, None) for b in banks]

    def bank():
        b, tok = free.pop(0)
        K.wait("pe", tok)
        return b

    def give(b, *toks):
        free.append((b, list(toks)))

    def mm(o, l, r, *toks, start=True, stop=True, after=False):
        return op("pe", lambda e: e.matmul(o, l, r, start=start, stop=stop), *toks, chain=after)

    def tr(o, i, idn, *toks):
        return op("pe", lambda e: e.transpose(o, i, idn), *toks)

    def tt(o, a, b, alu, *toks, e="dve"):
        return op(e, lambda g: g.tensor_tensor(o, a, b, alu), *toks)

    def ts(o, a, s1, s2, o1, o2, *toks, e="dve"):
        if s2 is None:
            return op(e, lambda g: g.tensor_scalar(o, a, s1, None, o1), *toks)
        return op(e, lambda g: g.tensor_scalar(o, a, s1, s2, o1, o2), *toks)

    def stt(o, a, s, b, o1, o2, *toks):
        return op("dve", lambda g: g.scalar_tensor_tensor(out=o, in0=a, scalar=s, in1=b, op0=o1, op1=o2), *toks)

    def act(o, i, f, *toks, bias=None, scale=1.0, accum=None):
        kw = {"scale": scale}
        if bias is not None:
            kw["bias"] = bias
        if accum is not None:
            kw["accum_out"] = accum
        return op("act", lambda g: g.activation(o, i, f, **kw), *toks)

    def copy(o, i, *toks, e="dve"):
        if e == "act":
            return act(o, i, ACT.Copy, *toks)
        return op(e, lambda g: g.tensor_copy(o, i), *toks)

    def memset(o, v, *toks, e="pool"):
        return op(e, lambda g: g.memset(o, v), *toks)

    def recip(o, i, *toks):
        return op("dve", lambda g: g.reciprocal(o, i), *toks)

    def max8(o, i, *toks):
        return op("dve", lambda g: g.max(o, i), *toks)

    def strike(o, m, i, *toks):
        return op("dve", lambda g: g.match_replace(out=o, in_to_replace=m, in_values=i, imm_value=-3e38), *toks)

    def red(o, i, alu, *toks):
        return op("dve", lambda g: g.tensor_reduce(o, i, AX.X, alu), *toks)

    def dump(name, ap, *toks):
        if DBG is None or name not in DBG:
            return
        K.wait("sp", K.all())
        t = K.dma("sp", lambda e: e.dma_start(DBG[name], ap))
        for e in ("pe", "act", "dve", "pool"):
            K.wait(e, t)

    def bc(ap, n):
        return ap.unsqueeze(2).to_broadcast([ap.shape[0], ap.shape[1], n])

    def bcm(ap, n):
        return ap.unsqueeze(1).to_broadcast([ap.shape[0], n, ap.shape[1]])

    csb = sb("csb", [128, A["cst"].shape[1]])
    col = sb("col", [128, CN])
    xt = sb("xt", [128, 4, D])
    RS = 12288
    ringbuf = sb("ring", [128, RS])
    ring = Ring(K, ringbuf, RS)
    t_cst = K.dma("sp", lambda e: e.dma_start(csb[:, :], A["cst"]))
    t_col = K.dma("sp", lambda e: e.dma_start(col[:, :], A["cols"]))
    t_x = K.dma("sp", lambda e: e.dma_start(xt[:, :, :], A["x"].rearrange("(b p) d -> p b d", p=128)))

    def C(name):
        a, w = cmap[name]
        return csb[:, a:a + w]

    def cc(name, j=0, n=1):
        a = CO[name][0] + j
        return col[:, a:a + n]

    ident = C("ident")

    def rowload(dst, name, *toks, e="sp", j=0, n=None):
        a, w = RO[name]
        n = n or w
        src = A["rows"][:, a + j:a + j + n].partition_broadcast(128) if False else A["rows"][0:1, a + j:a + j + n].to_broadcast([128, n])
        return K.dma(e, lambda g: g.dma_start(dst, src), *toks)

    for e in ("pe", "dve", "act", "pool"):
        K.wait(e, t_cst, t_col)

    eps5 = sb("eps5", [128, 4])
    t_eps = memset(eps5[:, 0:1], 1e-5)
    memset(eps5[:, 1:2], 64e-5)
    memset(eps5[:, 2:3], 1e-6)
    t_eps = memset(eps5[:, 3:4], 1.0)
    K.wait("act", t_eps)
    EPS5, EPS64, EPS6, ONE = (eps5[:, j:j + 1] for j in range(4))

    stt6 = sb("stt6", [128, 2, 6])
    mv = sb("mv", [128, 2])
    rstd = sb("rstd", [128, 2])

    def ln_stats(src, *toks):
        for j in range(2):
            op("dve", lambda g, j=j: g.bn_stats(stt6[:, j, :], src[:, j * 512:(j + 1) * 512]), *toks)
        t = op("dve", lambda g: g.bn_aggr(mv[:, :], stt6[:, :, :]))
        t = act(rstd[:, 1:2], mv[:, 1:2], ACT.Sqrt, t, bias=EPS5)
        return recip(rstd[:, 0:1], rstd[:, 1:2], t)

    uT = sb("uT", [128, 8, 768])
    ym = uT[:, :, :].rearrange("p k t -> p (k t)")[:, 0:4096].rearrange("p (k t) -> p k t", k=8)
    modc = sb("modc", [128, 4, 8, 2])
    scv = sb("scv", [128, 8, 2])
    sig = sb("sigc", [128, 16])
    act(sig[:, 0:16], cc("c", 0, 16), ACT.Sigmoid)
    t = tt(sig[:, 0:16], sig[:, 0:16], cc("c", 0, 16), ALU.mult, K.last("act"))
    t_sc = copy(scv[:, :, :], sig[:, 0:16].rearrange("p (b k) -> p k b", b=2))

    def ada(sec, mrow, brow, g12=None):
        tb = K.dma("sp", lambda e: e.dma_start(brow[0:1, :], A["ada_b"][0:1, sec * D:(sec + 1) * D]), K.last("pe"))
        for h in range(2):
            w = sec * D + h * 512
            ent, wap, tk = ring.load([(0, 4096, 8, A["ada_w"][:, w:w + 512].rearrange("(k p) n -> p k n", p=128))], 4096)
            wv = wap.rearrange("p (k n) -> p k n", k=8)
            b = bank()
            mm(b[0:2, :], C("ones")[0:1, 0:2], brow[0:1, h * 512:(h + 1) * 512], tb, tk, t_sc, start=True, stop=False)
            for k in range(8):
                t = mm(b[0:2, :], scv[:, k, :], wv[:, k, :], start=False, stop=(k == 7))
            ent[2] = t
            t = act(mrow[0:2, h * 512:(h + 1) * 512], b[0:2, :], ACT.Copy, t, K.last("pe"))
            give(b, t)
            yield
        slot = {0: 0, 1: 1, 3: 2, 4: 3}.get(sec)
        if slot is not None:
            b = bank()
            for k in range(8):
                t = tr(b[:, 2 * k:2 * k + 2], mrow[0:2, k * 128:(k + 1) * 128], ident[0:2, 0:2], t)
            yield
            t = ts(modc[:, slot, :, :].rearrange("p k b -> p (k b)"), b[:, 0:16], 1.0 if slot in (1, 3) else 0.0, None, ALU.add, None, t)
            give(b, t)
        else:
            for h in range(2):
                b = bank()
                t = mm(b[:, :], C("row0")[0:2, :], mrow[0:2, h * 512:(h + 1) * 512], t)
                t2 = act(g12[:, 0 if sec == 2 else 1, h * 512:(h + 1) * 512], b[:, :], ACT.Copy, t)
                give(b, t2)
        yield

    with ExitStack() as s0:
        mrow = sb("mrow", [2, D], c=s0)
        brow = sb("brow", [1, D], c=s0)
        run(ada(0, mrow, brow))
        run(ada(1, mrow, brow))
        K.barrier()

    m1 = ExitStack()
    uctx = ExitStack()
    rwm = sb("rwm", [128, 9, 768], c=m1)
    m1b = ExitStack()
    zx = sb("zx", [128, 4, 512], c=m1b)
    xbc = sb("xbc", [128, 8, 768], c=m1b)
    gqT = sb("gqT", [128, 512], c=m1b)
    gkT = sb("gkT", [128, 768], c=m1b)
    gkv = sb("gkv", [128, 6, 384], c=m1b)
    ogt = sb("ogt", [128, 4, 256], c=m1b)
    gdT = sb("gdT", [32, 768], c=m1b)
    dtt = sb("dtt", [128, 6, 16], c=m1b)
    ctxt = sb("ctxt", [128, 2, D], c=uctx)
    xn = sb("xn", [128, 2, D], c=uctx)
    t_ctx = K.dma("sp", lambda e: e.dma_start(ctxt[:, :, :], A["ctx"].rearrange("(b p) d -> p b d", p=128)), K.all())
    t_mod = K.last("dve")
    xnt = [None, None]
    for b6 in range(6):
        src = ctxt[:, b6, :] if b6 < 2 else xt[:, b6 - 2, :]
        ln_stats(src, t_x, t_ctx)
        ts(xn[:, b6 % 2, :], src, mv[:, 0:1], rstd[:, 0:1], ALU.subtract, ALU.mult, xnt[b6 % 2])
        tn = K.last("dve")
        s = 1 if b6 < 2 else 0
        for hf in range(2):
            b = bank()
            for k in range(4):
                t = tr(b[:, k * 128:(k + 1) * 128], xn[:, b6 % 2, (hf * 4 + k) * 128:(hf * 4 + k + 1) * 128], ident, tn)
            xnt[b6 % 2] = t
            for k in range(4):
                kk = hf * 4 + k
                t2 = act(uT[:, kk, b6 * 128:(b6 + 1) * 128], b[:, k * 128:(k + 1) * 128], ACT.Identity, t, t_mod,
                         bias=modc[:, 0, kk, s:s + 1], scale=modc[:, 1, kk, s:s + 1])
            give(b, t2)
    t_u = K.last("act")
    K.barrier()
    uctx.close()
    raw = sb("raw", [128, 2, 768], c=uctx)
    cv = sb("cv", [128, 2, 768], c=uctx)
    dtb = sb("dtb", [128, 16], c=uctx)
    sg = sb("sg", [128, 96], c=uctx)
    oms = sb("oms", [128, 2, 9], c=uctx)
    t_dtb = rowload(dtb[:, :], "dtb", K.all())
    dump("uT", uT[:, :, :])

    def wload(c0, n):
        ent, wap, tk = ring.load([(0, 8 * n, 8, A["w_in"][:, c0:c0 + n].rearrange("(k p) n -> p k n", p=128))], 8 * n)
        return ent, wap.rearrange("p (k n) -> p k n", k=8), tk

    def proj_tok(wv, lo, n, b6, tk):
        b = bank()
        for k in range(8):
            t = mm(b[:, 0:n], uT[:, k, b6 * 128:(b6 + 1) * 128], wv[:, k, lo:lo + n], t_u, tk, start=(k == 0), stop=(k == 7))
        return b, t

    def proj_ch(wv, lo, n, tk, ctxtoo=True):
        b = bank()
        for k in range(8):
            t = mm(b[0:n, :], wv[:, k, lo:lo + n], uT[:, k, 256:768], t_u, tk, start=(k == 0), stop=(k == 7))
        b2 = None
        if ctxtoo:
            b2 = bank()
            for k in range(8):
                t = mm(b2[0:n, 0:256], wv[:, k, lo:lo + n], uT[:, k, 0:256], start=(k == 0), stop=(k == 7))
        return b, b2, t

    ent, wv, tk = wload(1536, 16)
    for b6 in range(6):
        b, t = proj_tok(wv, 0, 16, b6, tk)
        t = tt(dtt[:, b6, :], b[:, 0:16], dtb[:, :], ALU.add, t, t_dtb)
        give(b, t)
    ent[2] = K.last("pe")
    dtf = dtt[:, :, :].rearrange("p a b -> p (a b)")
    sp1 = sg[:, 0:96]
    t = act(sp1, dtf, ACT.Abs, K.last("dve"))
    act(sp1, sp1, ACT.Exp, scale=-1.0)
    t = act(sp1, sp1, ACT.Ln, bias=ONE)
    t_dt = stt(dtf, dtf, 0.0, sp1, ALU.max, ALU.add, t)
    ent, wv, tk = wload(0, 512)
    for i in range(4):
        b, t = proj_tok(wv, 0, 512, i + 2, tk)
        t = act(zx[:, i, :], b[:, :], ACT.Silu, t)
        give(b, t)
    ent[2] = K.last("pe")
    ent, wv, tk = wload(3248, 256)
    for i in range(4):
        b, t = proj_tok(wv, 0, 256, i + 2, tk)
        t = act(ogt[:, i, :], b[:, 0:256], ACT.Silu, t)
        give(b, t)
    ent[2] = K.last("pe")
    ent, wv, tk = wload(2832, 384)
    for b6 in range(6):
        b, t = proj_tok(wv, 0, 384, b6, tk)
        t = copy(gkv[:, b6, :], b[:, 0:384], t)
        give(b, t)
    b, b2, t = proj_ch(wv, 0, 128, tk)
    t1 = copy(gkT[:, 256:768], b[:, :], t, e="act")
    t2 = copy(gkT[:, 0:256], b2[:, 0:256], t, e="act")
    give(b, t1)
    give(b2, t2)
    ent[2] = K.last("pe")
    ent, wv, tk = wload(2704, 128)
    b, _, t = proj_ch(wv, 0, 128, tk, False)
    t1 = act(gqT[:, :], b[:, :], ACT.Copy, t, scale=32 ** -0.5)
    give(b, t1)
    ent[2] = t
    ent, wv, tk = wload(3216, 32)
    b, b2, t = proj_ch(wv, 0, 32, tk)
    t1 = copy(gdT[:, 256:768], b[0:32, :], t, e="act")
    t2 = copy(gdT[:, 0:256], b2[0:32, 0:256], t, e="act")
    give(b, t1)
    give(b2, t2)
    ent[2] = t
    rawr = [None, None]
    cvr = [None, None]
    ts(oms[:, 0, :], cc("mu", 0, 9), -1.0, 1.0, ALU.mult, ALU.add)
    tt(oms[:, 0, :], oms[:, 0, :], cc("mu", 9, 9), ALU.subtract)
    tt(oms[:, 1, :], oms[:, 0, :], cc("mu", 18, 9), ALU.subtract)
    tt(oms[:, 1, :], oms[:, 1, :], cc("mu", 27, 9), ALU.subtract)
    n = 0
    for g in range(5):
        c0, w = [(512, 512), (1024, 512), (1552, 512), (2064, 512), (2576, 128)][g]
        ent, wv, tk = wload(c0, w)
        for j in range(w // 128):
            b, b2, t = proj_ch(wv, j * 128, 128, tk)
            r = raw[:, n % 2, :]
            t1 = act(r[:, 256:768], b[:, :], ACT.Copy, t, rawr[n % 2])
            t2 = act(r[:, 0:256], b2[:, 0:256], ACT.Copy)
            give(b, t1)
            give(b2, t2)
            if n < 8:
                o = cv[:, n % 2, :]
                ts(o, r, cc("conv_w", 8 + n), cc("conv_b", n), ALU.mult, ALU.add, t2, cvr[n % 2])
                for a, z in ((0, 256), (256, 768)):
                    stt(o[:, a + 1:z], r[:, a:z - 1], cc("conv_w", n), o[:, a + 1:z], ALU.mult, ALU.add)
                    t = stt(o[:, a:z - 1], r[:, a + 1:z], cc("conv_w", 16 + n), o[:, a:z - 1], ALU.mult, ALU.add)
                rawr[n % 2] = t
                t = act(xbc[:, n, :], o, ACT.Silu, t)
                cvr[n % 2] = t
            else:
                m = n - 8
                o = rwm[:, m, :]
                mu = [cc("mu", 9 * q + m) for q in range(4)]
                ts(o[:, 0:256], r[:, 0:256], oms[:, 0, m:m + 1], None, ALU.mult, None, t2)
                stt(o[:, 1:256], r[:, 0:255], mu[0], o[:, 1:256], ALU.mult, ALU.add)
                stt(o[:, 0:255], r[:, 1:256], mu[1], o[:, 0:255], ALU.mult, ALU.add)
                ts(o[:, 256:768], r[:, 256:768], oms[:, 1, m:m + 1], None, ALU.mult, None)
                og = o[:, 256:768].rearrange("p (r c) -> p r c", c=64)
                rg = r[:, 256:768].rearrange("p (r c) -> p r c", c=64)
                stt(og[:, :, 1:64], rg[:, :, 0:63], mu[0], og[:, :, 1:64], ALU.mult, ALU.add)
                stt(og[:, :, 0:63], rg[:, :, 1:64], mu[1], og[:, :, 0:63], ALU.mult, ALU.add)
                stt(o[:, 320:768], r[:, 256:704], mu[2], o[:, 320:768], ALU.mult, ALU.add)
                t = stt(o[:, 256:704], r[:, 320:768], mu[3], o[:, 256:704], ALU.mult, ALU.add)
                rawr[n % 2] = t
            n += 1
        ent[2] = K.last("pe")
    K.barrier()
    uctx.close()
    dump("xbc", xbc[:, :, :])
    dump("rwm", rwm[:, :, :])
    dump("dtt", dtt[:, :, :])

    FW = [0, 1, 2, 3, 4, 5]
    BW = [1, 0, 5, 4, 3, 2]
    ORD = (FW, BW)

    s1 = ExitStack()
    btk = sb("btk", [128, 2, 256], c=s1)
    las = sb("las", [128, 6, 16], c=s1)
    na = sb("na", [128, 16], c=s1)
    ysd = sb("ysd", [128, 4, 512], c=s1)
    gtm = sb("gtm", [128, 2, 256], c=s1)
    big, scr, over = ring.take(8704)
    K.wait("dve", over)
    K.wait("act", over)
    K.wait("pool", over)
    xst = scr[:, 6144:7168].rearrange("p (a b) -> p a b", a=2)
    Hs = scr[:, 7168:8192].rearrange("p (a b) -> p a b", a=2)
    yo = scr[:, 8192:8704]
    lax = scr[:, 0:2048].rearrange("p (a b) -> p a b", a=2)
    sct = scr[:, 2048:4096].rearrange("p (a b) -> p a b", a=2)
    xdt = scr[:, 4096:5120].rearrange("p (a b) -> p a b", a=2)
    xde = scr[:, 5120:6144].rearrange("p (a b) -> p a b", a=2)
    ex3 = sb("ex3", [128, 2, 24], c=s1)
    sdd = sb("sdd", [128, 8], c=s1)
    t_na = rowload(na[:, :], "alog", K.all())
    t_sdd = rowload(sdd[:, :], "ssd_d", K.all())
    t = act(na[:, :], na[:, :], ACT.Exp, t_na)
    t = ts(na[:, :], na[:, :], -1.0, None, ALU.mult, None, t)
    tt(las[:, :, :], dtt[:, :, :], bcm(na[:, :], 6), ALU.mult, t_dt)
    memset(Hs[:, :, :], 0.0, e="dve")
    t_las = K.last("dve")

    def ssd_unit(d, b6, first):
        u = d
        tok = slice(b6 * 128, (b6 + 1) * 128)
        b = bank()
        for j in range(4):
            t = tr(b[:, j * 128:(j + 1) * 128], xbc[:, j, tok], ident, K.last("act"))
        t1 = act(xst[:, u, :], b[:, :], ACT.Copy, t, K.last("dve"))
        give(b, t1)
        b = bank()
        for j in range(2):
            t = tr(b[:, j * 128:(j + 1) * 128], xbc[:, 4 + j, tok], ident)
        t2 = act(btk[:, u, :], b[:, 0:256], ACT.Copy, t)
        give(b, t2)
        yield
        la = las[:, b6, 8 * d:8 * d + 8]
        b = bank()
        mm(b[:, 0:8], C(f"i128_{d}"), la, t_las)
        mm(b[:, 8:16], C(f"g128_{d}"), la)
        t = mm(b[:, 16:24], C("ones"), la)
        t = act(ex3[:, u, :], b[:, 0:24], ACT.Exp, t, K.last("dve"))
        give(b, t)
        t_ex = t
        t_xdt = tt(xdt[:, u, :].rearrange("p (h q) -> p h q", q=64), xst[:, u, :].rearrange("p (h q) -> p h q", q=64),
                   bc(dtt[:, b6, 8 * d:8 * d + 8], 64), ALU.mult, t1, K.last("pe"))
        t_xde = tt(xde[:, u, :].rearrange("p (h q) -> p h q", q=64), xdt[:, u, :].rearrange("p (h q) -> p h q", q=64),
                   bc(ex3[:, u, 8:16], 64), ALU.mult, t_ex, K.last("pe"))
        yield
        if b6 >= 2:
            b = bank()
            for g in range(2):
                t = mm(b[:, g * 128:(g + 1) * 128], xbc[:, 4 + g, tok], xbc[:, 6 + g, tok])
            t_g = tt(gtm[:, u, :].rearrange("p (g t) -> p g t", g=2), b[:, 0:256].rearrange("p (g t) -> p g t", g=2),
                     bcm(C(f"i128_{d}"), 2), ALU.mult, t)
            give(b, t_g)
            t_lx = tt(lax[:, u, :].rearrange("p (h s) -> p h s", h=8), bcm(C(f"g128_{d}"), 8), bc(la, 128), ALU.mult)
            yield
            for hf in range(2):
                b = bank()
                for h in range(4):
                    hh = hf * 4 + h
                    t = mm(b[:, h * 128:(h + 1) * 128], lax[:, u, hh * 128:(hh + 1) * 128], C(f"i128_{d}"), t_lx)
                o = sct[:, u, hf * 512:(hf + 1) * 512]
                t = act(o, b[:, :], ACT.Exp, t)
                give(b, t)
                t_sc_ = tt(o.rearrange("p (h t) -> p h t", h=4), o.rearrange("p (h t) -> p h t", h=4),
                          bcm(gtm[:, u, hf * 128:(hf + 1) * 128], 4), ALU.mult, t)
                yield
            by = bank()
            for h in range(8):
                t_y = mm(by[:, h * 64:(h + 1) * 64], sct[:, u, h * 128:(h + 1) * 128], xdt[:, u, h * 64:(h + 1) * 64], t_sc_, t_xdt)
            bo = bank()
            for g in range(2):
                t_o = mm(bo[:, g * 256:(g + 1) * 256], xbc[:, 6 + g, tok], Hs[:, d, g * 256:(g + 1) * 256], K.last("dve"))
            yield
            ydst = ysd[:, b6 - 2, :]
            t = tt(yo[:, :].rearrange("p (h q) -> p h q", q=64), bo[:, :].rearrange("p (h q) -> p h q", q=64),
                   bc(ex3[:, u, 0:8], 64), ALU.mult, t_o)
            give(bo, t)
            if first:
                t = tt(ydst, by[:, :], yo[:, :], ALU.add, t_y)
                give(by, t)
                tt(yo[:, :].rearrange("p (h q) -> p h q", q=64), xst[:, u, :].rearrange("p (h q) -> p h q", q=64),
                   bc(sdd[:, :], 64), ALU.mult, t_sdd)
            else:
                t = tt(yo[:, :], by[:, :], yo[:, :], ALU.add, t_y)
                give(by, t)
            tt(ydst, ydst, yo[:, :], ALU.add)
        b = bank()
        for g in range(2):
            t = mm(b[:, g * 256:(g + 1) * 256], btk[:, u, g * 128:(g + 1) * 128], xde[:, u, g * 256:(g + 1) * 256], t2, t_xde)
        yield
        tt(Hs[:, d, :].rearrange("p (h q) -> p h q", q=64), Hs[:, d, :].rearrange("p (h q) -> p h q", q=64),
           bc(ex3[:, u, 16:24], 64), ALU.mult, t)
        t = tt(Hs[:, d, :], Hs[:, d, :], b[:, :], ALU.add)
        give(b, t)
        yield

    seen = set()
    for i in range(6):
        gens = []
        for d in range(2):
            b6 = ORD[d][i]
            gens.append(ssd_unit(d, b6, b6 not in seen))
            seen.add(b6)
        for g in gens:
            run(g)
    dump("ysd", ysd[:, :, :])
    for i in range(4):
        tt(ysd[:, i, :], ysd[:, i, :], zx[:, i, :], ALU.mult)
        for g in range(2):
            src = ysd[:, i, g * 256:(g + 1) * 256]
            t = act(yo[:, g * 256:(g + 1) * 256], src, ACT.Square, K.last("dve"), K.last("pe"), accum=mv[:, g:g + 1])
        t = act(rstd[:, 0:2], mv[:, 0:2], ACT.Sqrt, t, bias=EPS5, scale=1.0 / 256)
        recip(mv[:, 0:2], rstd[:, 0:2], t)
        for g in range(2):
            t = ts(yo[:, g * 256:(g + 1) * 256], ysd[:, i, g * 256:(g + 1) * 256], mv[:, g:g + 1], None, ALU.mult, None)
        b = bank()
        for j in range(4):
            t = tr(b[:, j * 128:(j + 1) * 128], yo[:, j * 128:(j + 1) * 128], ident, K.last("dve"))
        for j in range(4):
            t2 = ts(ym[:, j, i * 128:(i + 1) * 128], b[:, j * 128:(j + 1) * 128], cc("ssd_w", j), None, ALU.mult, None, t)
        give(b, t2)
    K.barrier()
    big[2] = K.all()
    s1.close()

    s2 = ExitStack()
    lag = sb("lag", [128, 6, 256], c=s2)
    gux = sb("gux", [32, 256], c=s2)
    gbr = sb("gbr", [1, 256], c=s2)
    big, scr, over = ring.take(8704)
    for e in ("dve", "act", "pool"):
        K.wait(e, over)
    gt1 = scr[:, 0:1536].rearrange("p (a b) -> p a b", a=6)
    kde = scr[:, 6144:7168]
    stm = scr[:, 7168:7680]
    og2 = scr[:, 7680:8704].rearrange("p (i n) -> p i n", i=4)
    Sg = scr[:, 1536:6144].rearrange("p (d c n) -> p d c n", d=2, c=9)
    cq = sb("cq", [128, 128], c=s2)
    eq = sb("eq", [128, 4, 128], c=s2)
    etot = sb("etot", [128, 8], c=s2)
    qp = sb("qp", [128, 2, 128], c=s2)
    qx = sb("qx", [128, 1152], c=s2)
    sTg = sb("sTg", [128, 512], c=s2)
    t1 = K.dma("sp", lambda e: e.dma_start(gux[:, :], A["gux"]), K.all())
    t2 = K.dma("sp", lambda e: e.dma_start(gbr[:, :], A["rows"][0:1, RO["gb"][0]:RO["gb"][0] + 256]), K.all())
    memset(qx[:, :], 0.0)
    memset(Sg[:, :, :, :], 0.0)
    for b6 in range(6):
        b = bank()
        mm(b[:, 0:256], C("ones")[0:1, :], gbr[0:1, :], t1, t2, start=True, stop=False)
        t = mm(b[:, 0:256], gdT[0:32, b6 * 128:(b6 + 1) * 128], gux[:, :], start=False, stop=True)
        t = copy(lag[:, b6, :], b[:, 0:256], t)
        give(b, t)
    lf = lag[:, :, :].rearrange("p a b -> p (a b)")
    gf = gt1[:, :, :].rearrange("p a b -> p (a b)")
    act(gf, lf, ACT.Abs, K.last("dve"))
    act(gf, gf, ACT.Exp, scale=-1.0)
    t = act(gf, gf, ACT.Ln, bias=ONE)
    t_lag = stt(lf, lf, 0.0, gf, ALU.min, ALU.subtract, t)
    dump("lag", lag[:, :, :])

    def gla_unit(d, b6, first, s_in):
        tok = slice(b6 * 128, (b6 + 1) * 128)
        la = lag[:, b6, 128 * d:128 * d + 128]
        b = bank()
        mm(b[:, 0:128], la, C(f"q16_{d}"), t_lag)
        mm(b[:, 128:256], la, C(f"i16_{d}"))
        mm(b[:, 256:264], la, C(f"c16_{d}"))
        t = mm(b[:, 384:512], C(f"x16_{d}"), la)
        t3 = ts(cq[:, :], b[:, 0:128], 640.0, -640.0, ALU.min, ALU.max, t, K.last("act"))
        pe0 = K.last("pe")
        t2 = act(eq[:, 3, :], b[:, 384:512], ACT.Exp, t, pe0, K.last("dve"), scale=1.0 / 16)
        act(etot[:, :], b[:, 256:264], ACT.Exp, K.last("dve"), scale=1.0 / 16)
        if b6 >= 2:
            act(eq[:, 2, :], b[:, 128:256], ACT.Exp, scale=1.0 / 16)
            act(eq[:, 0, :], cq[:, :], ACT.Exp, t3, scale=1.0 / 16)
            act(eq[:, 1, :], cq[:, :], ACT.Exp, scale=-1.0 / 16)
        t_e = K.last("act")
        give(b, t_e, t3)
        kd = eq[:, 3, :]
        tt(kd, kd, gkv[:, b6, 0:128], ALU.mult, t_e)
        t_k = tt(kde[:, :].rearrange("p (c k) -> p c k", c=8), bcm(kd, 8), bc(C(f"c16_{d}"), 128), ALU.mult, pe0)
        order = range(8) if d == 0 else range(7, -1, -1)
        S = Sg[:, d, :, :]
        chunks = list(order)
        for jj in range(4):
            b = bank()
            for q in range(2):
                c = chunks[2 * jj + q]
                t = mm(b[:, q * 256:(q + 1) * 256], kde[:, c * 128:(c + 1) * 128], gkv[:, b6, 128:384], t_k)
            t = tt(stm[:, :].rearrange("p (a b) -> p a b", a=2), b[:, :].rearrange("p (a b) -> p a b", a=2),
                   bcm(C("bd"), 2), ALU.mult, t)
            give(b, t)
            for q in range(2):
                n_ = 2 * jj + q
                t = stt(S[:, n_ + 1, :], S[:, n_, :], etot[:, chunks[n_]:chunks[n_] + 1], stm[:, q * 256:(q + 1) * 256],
                        ALU.mult, ALU.add)
        if b6 >= 2:
            xt_ = slice((b6 - 2) * 128, (b6 - 1) * 128)
            tt(qp[:, 0, :], gqT[:, xt_], eq[:, 0, :], ALU.mult)
            t_qp = tt(qp[:, 1, :], gkT[:, tok], eq[:, 1, :], ALU.mult)
            t_qx = tt(qx[:, :].rearrange("p (c w) -> p c w", w=144)[:, :, 0:16],
                      gqT[:, xt_].rearrange("p (c w) -> p c w", w=16),
                      eq[:, 2, :].rearrange("p (c w) -> p c w", w=16), ALU.mult)
            b = bank()
            for h in range(4):
                hs = slice(32 * h, 32 * h + 32)
                t = mm(b[:, h * 128:(h + 1) * 128], qp[hs, 1, :], qp[hs, 0, :], t_qp, after=h > 0)
            t_s = tt(sTg[:, :].rearrange("p (h t) -> p h t", h=4), b[:, :].rearrange("p (h t) -> p h t", h=4),
                     bcm(C(f"i16_{d}"), 4), ALU.mult, t)
            give(b, t_s)
            b = bank()
            for n_ in range(8):
                c = chunks[n_]
                mm(b[:, 0:256], qx[:, c * 128:(c + 1) * 128], S[:, n_, :], t_qx, start=(n_ == 0), stop=False)
            for h in range(4):
                t = mm(b[:, 64 * h:64 * h + 64], sTg[:, h * 128:(h + 1) * 128], gkv[:, b6, 128 + 64 * h:192 + 64 * h],
                       t_s, start=False, stop=(h == 3))
            o = og2[:, b6 - 2, :]
            if first:
                t = copy(o, b[:, 0:256], t)
            else:
                t = tt(o, o, b[:, 0:256], ALU.add, t)
            give(b, t)
        copy(S[:, 0, :], S[:, 8, :], K.last("pe"))
        yield

    K.barrier(("pe", "act", "dve"))
    seen = set()
    for i in range(6):
        for d in range(2):
            b6 = ORD[d][i]
            run(gla_unit(d, b6, b6 not in seen, None))
            seen.add(b6)
    dump("og2", og2[:, :, :])
    sq = gt1[:, 0:2, :].rearrange("p a b -> p (a b)")
    for i in range(4):
        o = og2[:, i, :]
        act(sq[:, 0:256], o, ACT.Square, K.last("dve"), K.last("pe"))
        red(etot[:, 0:4], sq[:, 0:256].rearrange("p (h v) -> p h v", h=4), ALU.add, K.last("act"))
        act(etot[:, 4:8], etot[:, 0:4], ACT.Sqrt, K.last("dve"), bias=EPS5, scale=1.0 / 64)
        recip(etot[:, 0:4], etot[:, 4:8], K.last("act"))
        tt(sq[:, 256:512].rearrange("p (h v) -> p h v", h=4), o.rearrange("p (h v) -> p h v", h=4),
           bc(etot[:, 0:4], 64), ALU.mult, K.last("pe"))
        t = tt(sq[:, 256:512], sq[:, 256:512], ogt[:, i, :], ALU.mult)
        b = bank()
        for j in range(2):
            t2 = tr(b[:, j * 128:(j + 1) * 128], sq[:, 256 + j * 128:384 + j * 128], ident, t)
        for j in range(2):
            t = ts(ym[:, 6 + j, i * 128:(i + 1) * 128], b[:, j * 128:(j + 1) * 128], cc("gla_w", j), None, ALU.mult, None, t2)
        give(b, t)
    K.barrier()
    big[2] = K.all()
    s2.close()
    m1b.close()

    s3 = ExitStack()
    w2x = sb("w2x", [128, 512], c=s3)
    a2x = sb("a2x", [128, 512], c=s3)
    g2s = sb("g2s", [128, 256], c=s3)
    w0r = sb("w0r", [1, 512], c=s3)
    lw = sb("lw", [128, 6, 512], c=s3)
    aT = sb("aT", [128, 4, 768], c=s3)
    kkT = sb("kkT", [128, 2, 768], c=s3)
    kd_ = sb("kd_", [128, 4, 768], c=s3)
    tmp = sb("tmp", [128, 768], c=s3)
    tmp2 = sb("tmp2", [128, 768], c=s3)
    yR = sb("yR", [128, 2, 512], c=s3)
    K.wait("sp", K.all())
    tw = [K.dma("sp", lambda e: e.dma_start(w2x[:, :], A["w2x"])), K.dma("sp", lambda e: e.dma_start(a2x[:, :], A["a2x"])),
          K.dma("sp", lambda e: e.dma_start(g2s[:, :], A["g2"])),
          K.dma("sp", lambda e: e.dma_start(w0r[:, :], A["rows"][0:1, RO["w0"][0]:RO["w0"][0] + 512]))]
    act(tmp[:, :], rwm[:, 6, :], ACT.Tanh)
    t_th = K.last("act")
    for b6 in range(6):
        b = bank()
        mm(b[:, :], C("ones")[0:1, :], w0r[0:1, :], *tw, start=True, stop=False)
        t = mm(b[:, :], tmp[:, b6 * 128:(b6 + 1) * 128], w2x[:, :], t_th, start=False, stop=True)
        t = act(lw[:, b6, :], b[:, :], ACT.Sigmoid, t)
        give(b, t)
    for q in range(4):
        for lo, n_ in ((0, 512), (512, 256)):
            b = bank()
            t = mm(b[:, 0:n_], a2x[:, q * 128:(q + 1) * 128], rwm[:, 7, lo:lo + n_], *tw)
            t = act(aT[:, q, lo:lo + n_], b[:, 0:n_], ACT.Sigmoid, t, bias=cc("a0", q))
            give(b, t)
    for p in range(2):
        ts(kkT[:, p, :], rwm[:, 2 + p, :], cc("kk", p), None, ALU.mult, None)
        t = act(tmp[:, :], kkT[:, p, :], ACT.Square, K.last("dve"), K.last("pe"))
        for lo, n_ in ((0, 512), (512, 256)):
            b = bank()
            t = mm(b[:, 0:n_], C("h64"), tmp[:, lo:lo + n_], K.last("act"))
            t = act(tmp2[:, lo:lo + n_], b[:, 0:n_], ACT.Sqrt, t, K.last("dve"))
            give(b, t)
        ts(tmp2[:, :], tmp2[:, :], 1e-12, None, ALU.max, None, t)
        recip(tmp2[:, :], tmp2[:, :])
        tt(kkT[:, p, :], kkT[:, p, :], tmp2[:, :], ALU.mult)
    for q in range(4):
        p = q % 2
        ts(kd_[:, q, :], aT[:, q, :], -1.0, cc("ka", p), ALU.add, ALU.mult, K.last("act"))
        stt(kd_[:, q, :], kd_[:, q, :], 1.0, rwm[:, 2 + p, :], ALU.add, ALU.mult)
        tt(aT[:, q, :], aT[:, q, :], kkT[:, p, :], ALU.mult)
    dump("kd_", kd_[:, :, :])
    dump("lw", lw[:, :, :])
    K.barrier()
    s4 = ExitStack()
    E3 = sb("E3", [128, 2, 3, 128], c=s4)
    Dt = sb("Dt", [128, 2, 2], c=s4)
    big, scr, over = ring.take(8192)
    for e in ("dve", "act", "pool"):
        K.wait(e, over)
    ATm, Aof, Tm, TT, Xm, BTm, Abt, Akt = (
        scr[:, 512 * j:512 * j + 512].rearrange("p (h t) -> p h t", h=4) for j in range(8))
    OPC = scr[:, 4096:5120].rearrange("p (a q t) -> p a q t", a=4, q=2)
    OPT = scr[:, 5120:6144].rearrange("p (a c) -> p a c", a=4)
    BV = sb("BV", [128, 256], c=s4)
    U0 = sb("U0", [128, 256], c=s4)
    TK = sb("TK", [128, 2, 128], c=s4)
    SA = sb("SA", [128, 256], c=s4)
    Hr = sb("Hr", [128, 2, 2, 64], c=s4)
    memset(Hr[:, :, :, :], 0.0, e="dve")

    def v4(x):
        return x.rearrange("p (h t) -> p h t", h=4)

    def hp(h):
        return slice(64 * (h % 2), 64 * (h % 2) + 64), h // 2

    def rw_unit(d, b6, first):
        tok = slice(b6 * 128, (b6 + 1) * 128)
        isx = b6 >= 2
        K.wait("dve", K.last("pe"), K.last("act"))
        K.wait("act", K.last("pe"), K.last("dve"))
        bd_ = bank()
        for p in range(2):
            l = lw[:, b6, 256 * d + 128 * p:256 * d + 128 * p + 128]
            b = bank()
            mm(b[:, 0:128], l, C(f"i64_{d}"))
            t = mm(b[:, 128:256], l, C(f"e64_{d}"))
            t2 = mm(bd_[:, 2 * p:2 * p + 2], l, C("ch64"))
            act(E3[:, p, 0:2, :].rearrange("p a b -> p (a b)"), b[:, 0:256], ACT.Exp, t, scale=-E05)
            t = act(E3[:, p, 2, :], b[:, 0:128], ACT.Exp, scale=E05)
            give(b, t)
        t_e = act(Dt[:, :, :].rearrange("p c q -> p q c"), bd_[:, 0:4].rearrange("p (q c) -> p q c", q=2), ACT.Exp, t2, scale=-E05)
        give(bd_, t_e)
        if isx:
            tt(OPC[:, 0, :, :], rwm[:, 0:2, tok], E3[:, :, 0, :], ALU.mult, t_e)
        tt(OPC[:, 1, :, :], kkT[:, :, tok], E3[:, :, 1, :], ALU.mult, t_e)
        tt(OPC[:, 2, :, :], aT[:, 2 * d:2 * d + 2, tok], E3[:, :, 2, :], ALU.mult)
        t_c = tt(OPC[:, 3, :, :], kd_[:, 2 * d:2 * d + 2, tok], E3[:, :, 2, :], ALU.mult)
        for a in range(2):
            b = bank()
            for q in range(2):
                for p in range(2):
                    k = 2 * a + q
                    src = rwm[:, 4 + p, tok] if k == 0 else OPC[:, k, p, :]
                    t = tr(b[:, q * 256 + p * 128:q * 256 + (p + 1) * 128], src, ident, t_c)
            if a == 0:
                act(OPT[:, 0, :], b[:, 0:256], ACT.Copy, t)
                t = act(OPT[:, 1, :], b[:, 256:512], ACT.Copy, scale=-1.0)
            else:
                t = act(OPT[:, 2:4, :].rearrange("p a b -> p (a b)"), b[:, :], ACT.Copy, t)
            give(b, t)
        t_t = t
        def prod(i, j, msk, dst):
            b = bank()
            for h in (0, 2, 1, 3):
                ps_, q = hp(h)
                t = mm(b[:, h * 128:(h + 1) * 128], OPC[ps_, i, q, :], OPC[ps_, j, q, :], t_c, after=h == 1)
            t = tt(dst[:, :, :], v4(b[:, :]), bcm(C(msk), 4), ALU.mult, t)
            give(b, t)
            return t
        prod(1, 2, f"l0_{1 - d}", Tm)
        t = stt(Tm[:, :, :], Tm[:, :, :], -1.0, bcm(ident, 4), ALU.mult, ALU.add)
        prod(2, 1, f"e64_{d}", ATm)
        tt(TT[:, :, :], ATm[:, :, :], bcm(C(f"l0_{d}"), 4), ALU.mult)
        t_T = stt(TT[:, :, :], TT[:, :, :], -1.0, bcm(ident, 4), ALU.mult, ALU.add)
        t_B = prod(3, 1, f"e64_{d}", BTm)
        if isx:
            prod(2, 0, f"i64_{d}", Abt)
            t_A = prod(3, 0, f"i64_{d}", Akt)
        b = bank()
        for h in range(4):
            t = mm(b[:, 64 * h:64 * h + 64], BTm[:, h, :], OPT[:, 0, 64 * h:64 * h + 64], t_B, t_t)
        t_bv = act(BV[:, :], b[:, 0:256], ACT.Copy, t, scale=-1.0)
        give(b, t_bv)
        for k in range(1, 6):
            t_a = tt(Aof[:, :, :], ATm[:, :, :], bcm(C(f"l{k}_{d}"), 4), ALU.mult, K.last("pe"))
            b = bank()
            for h in range(4):
                t = mm(b[:, h * 128:(h + 1) * 128], Aof[:, h, :], Tm[:, h, :], t_a, t_T)
            t_X = act(Xm[:, :, :], v4(b[:, :]), ACT.Copy, t)
            give(b, t_X)
            if k < 5:
                b = bank()
                for h in range(4):
                    t1 = mm(b[:, h * 128:(h + 1) * 128], TT[:, h, :], Xm[:, h, :], t_X)
            b2 = bank()
            for h in range(4):
                t2 = mm(b2[:, h * 128:(h + 1) * 128], Xm[:, h, :], TT[:, h, :], t_X)
            if k < 5:
                t = tt(Tm[:, :, :], Tm[:, :, :], v4(b[:, :]), ALU.subtract, t1)
                give(b, t)
            t_T = tt(TT[:, :, :], TT[:, :, :], v4(b2[:, :]), ALU.subtract, t2)
            give(b2, t_T)
        b = bank()
        for h in range(4):
            t = mm(b[:, 64 * h:64 * h + 64], TT[:, h, :], BV[:, 64 * h:64 * h + 64], t_T, t_bv)
        for h in range(4):
            ps_, q = hp(h)
            t = mm(b[ps_, 256 + q * 128:384 + q * 128], OPT[:, 1, 64 * h:64 * h + 64], TT[:, h, :], t_t)
        act(U0[:, :], b[:, 0:256], ACT.Copy, t)
        t_u0 = act(TK[:, :, :].rearrange("p a b -> p (a b)"), b[:, 256:512], ACT.Copy)
        give(b, t_u0)
        by = bank() if isx else None
        for ch in ((0, 1) if d == 0 else (1, 0)):
            cs = slice(64 * ch, 64 * ch + 64)
            t_H = K.last("dve")
            b = bank()
            for h in (0, 2, 1, 3):
                ps_, q = hp(h)
                t = mm(b[cs, 64 * h:64 * h + 64], TK[ps_, q, cs], Hr[ps_, d, q, :], t_H, t_u0, after=h == 1)
            t_sa = tt(SA[cs, :], b[cs, 0:256], U0[cs, :], ALU.add, t)
            give(b, t_sa)
            if isx:
                for h in range(4):
                    ps_, q = hp(h)
                    o = by[ps_, q * 128 + 64 * ch:q * 128 + 64 * ch + 64]
                    mm(o, Hr[ps_, d, q, :], OPC[ps_, 0, q, cs], start=True, stop=False, after=True)
                    mm(o, SA[cs, 64 * h:64 * h + 64], Abt[cs, h, cs], t_sa, t_A, start=False, stop=False, after=True)
                    t_y = mm(o, OPT[cs, 0, 64 * h:64 * h + 64], Akt[cs, h, cs], start=False, stop=True)
            b = bank()
            for h in range(4):
                ps_, q = hp(h)
                o = b[ps_, q * 64:q * 64 + 64]
                mm(o, OPT[cs, 3, 64 * h:64 * h + 64], OPT[cs, 0, 64 * h:64 * h + 64], start=True, stop=False)
                t = mm(o, OPT[cs, 2, 64 * h:64 * h + 64], SA[cs, 64 * h:64 * h + 64], t_sa, start=False, stop=True)
            t = tt(Hr[:, d, :, :], Hr[:, d, :, :], b[:, 0:128].rearrange("p (q v) -> p q v", q=2), ALU.add, t)
            give(b, t)
            tt(Hr[:, d, :, :], Hr[:, d, :, :], bc(Dt[:, ch, :], 64), ALU.mult)
        if isx:
            o = yR[:, :, (b6 - 2) * 128:(b6 - 1) * 128]
            src = by[:, 0:256].rearrange("p (q t) -> p q t", q=2)
            t = copy(o, src, t_y) if first else tt(o, o, src, ALU.add, t_y)
            give(by, t)
        yield

    seen = set()
    for i in range(6):
        for d in range(2):
            b6 = ORD[d][i]
            run(rw_unit(d, b6, b6 not in seen))
            seen.add(b6)
    K.barrier()
    big[2] = K.all()
    s4.close()
    dump("yR", yR[:, :, :])
    t5 = tmp[:, 0:512]
    t6 = tmp2[:, 0:512]
    X = slice(256, 768)
    for p in range(2):
        y = yR[:, p, :]
        b = bank()
        t = mm(b[:, :], C("h64"), y, K.last("dve"))
        t = stt(y, b[:, :], -1.0 / 64, y, ALU.mult, ALU.add, t)
        give(b, t)
        t = act(t5, y, ACT.Square, t, K.last("pe"))
        b = bank()
        t = mm(b[:, :], C("h64"), t5, t)
        t = act(t6, b[:, :], ACT.Sqrt, t, bias=EPS64, scale=1.0 / 64)
        give(b, t)
        recip(t6, t6, t)
        tt(y, y, t6, ALU.mult)
        ts(y, y, cc("lnw", p), cc("lnb", p), ALU.mult, ALU.add)
        tt(t6, kd_[:, p, X], kd_[:, 2 + p, X], ALU.add)
        stt(t5, rwm[:, p, X], cc("rk", p), t6, ALU.mult, ALU.mult, K.last("pe"))
        b = bank()
        t = mm(b[:, :], C("h64"), t5, K.last("dve"))
        t = tt(t6, b[:, :], rwm[:, 4 + p, X], ALU.mult, t)
        give(b, t)
        tt(y, y, t6, ALU.add)
        if p == 0:
            t_s = act(aT[:, 0, 0:512], rwm[:, 8, X], ACT.Sigmoid, K.last("dve"))
        b = bank()
        t = mm(b[:, :], g2s[:, p * 128:(p + 1) * 128], aT[:, 0, 0:512], t_s)
        t = tt(ym[:, 4 + p, :], y, b[:, :], ALU.mult, t)
        give(b, t)
    dump("ym", ym[:, :, :])
    K.barrier()
    s3.close()
    m1.close()
    g12 = sb("g12", [128, 2, D])
    with ExitStack() as s0:
        mrow = sb("mrow2", [2, D], c=s0)
        brow = sb("brow2", [1, D], c=s0)
        for s in (2, 3, 4, 5):
            run(ada(s, mrow, brow, g12))
        K.barrier()

    m2 = ExitStack()
    hT = sb("hT", [128, 8, 512], c=m2)
    fac = sb("fac", [128, 4, D], c=m2)
    wtok = sb("wtok", [128, 4, 64], c=m2)
    m3 = ExitStack()
    lnr = sb("lnr", [128, 4, D], c=m3)
    xn = sb("xn2", [128, 2, D], c=m3)
    rwt = sb("rwt", [128, 8, 64], c=m3)
    rb = sb("rb", [128, 64], c=m3)
    sel = sb("sel", [128, 64], c=m3)
    sco = sb("sco", [128, 64], c=m3)
    m8 = sb("m8", [128, 8, 8], c=m3)
    gs = sb("gs", [128, 32], c=m3)
    K.wait("sp", K.all())
    tl = [rowload(lnr[:, 0, :], "ln1w"), rowload(lnr[:, 1, :], "ln1b"),
          K.dma("sp", lambda e: e.dma_start(rwt[:, :, :], A["router_w"].rearrange("(k p) n -> p k n", p=128))),
          rowload(rb[:, :], "rb")]

    def out_proj(W, i, src, dst_fn):
        pass

    ents = []
    for hf in range(2):
        ent, wap, tk = ring.load([(0, 4096, 8, A["w_out"][:, hf * 512:(hf + 1) * 512].rearrange("(k p) n -> p k n", p=128))], 4096)
        wv = wap.rearrange("p (k n) -> p k n", k=8)
        for i in range(4):
            b = bank()
            for k in range(8):
                t = mm(b[:, :], ym[:, k, i * 128:(i + 1) * 128], wv[:, k, :], tk, start=(k == 0), stop=(k == 7))
            hs = slice(hf * 512, (hf + 1) * 512)
            tmpv = xn[:, 0, hs]
            t = tt(tmpv, b[:, :], g12[:, 0, hs], ALU.mult, t)
            give(b, t)
            stt(xt[:, i, hs], xt[:, i, hs], ALPHA, tmpv, ALU.mult, ALU.add)
        ent[2] = K.last("pe")

    def layer_norm(x, w, bb, *toks):
        ln_stats(x, *toks)
        ts(x, x, mv[:, 0:1], rstd[:, 0:1], ALU.subtract, ALU.mult)
        tt(x, x, w, ALU.mult, *toks)
        return tt(x, x, bb, ALU.add)

    xnt = [None, None]
    for i in range(4):
        layer_norm(xt[:, i, :], lnr[:, 0, :], lnr[:, 1, :], *tl)
        ln_stats(xt[:, i, :])
        tn = ts(xn[:, i % 2, :], xt[:, i, :], mv[:, 0:1], rstd[:, 0:1], ALU.subtract, ALU.mult, xnt[i % 2])
        for hf in range(2):
            b = bank()
            for k in range(4):
                t = tr(b[:, k * 128:(k + 1) * 128], xn[:, i % 2, (hf * 4 + k) * 128:(hf * 4 + k + 1) * 128], ident, tn)
            xnt[i % 2] = t
            for k in range(4):
                kk = hf * 4 + k
                t2 = act(hT[:, kk, i * 128:(i + 1) * 128], b[:, k * 128:(k + 1) * 128], ACT.Identity, t,
                         bias=modc[:, 2, kk, 0:1], scale=modc[:, 3, kk, 0:1])
            give(b, t2)
    t_h = K.last("act")
    dump("x1", xt[:, :, :])
    dump("hT", hT[:, :, :])
    for i in range(4):
        b = bank()
        for k in range(8):
            t = mm(b[:, 0:64], hT[:, k, i * 128:(i + 1) * 128], rwt[:, k, :], t_h, *tl, start=(k == 0), stop=(k == 7))
        t = act(sco[:, :], b[:, 0:64], ACT.Sigmoid, t, K.last("dve"))
        give(b, t)
        tt(sel[:, :], sco[:, :], rb[:, :], ALU.add, t, *tl)
        for g in range(8):
            max8(m8[:, g, :], sel[:, 8 * g:8 * g + 8])
        tt(gs[:, 0:8], m8[:, :, 0], m8[:, :, 1], ALU.add)
        max8(gs[:, 8:16], gs[:, 0:8])
        ts(gs[:, 16:24], gs[:, 0:8], gs[:, 11:12], None, ALU.is_ge, None)
        ts(gs[:, 24:32], gs[:, 16:24], -1.0, 1e30, ALU.add, ALU.mult)
        s3_ = sel[:, :].rearrange("p (g e) -> p g e", g=8)
        tt(s3_, s3_, bc(gs[:, 16:24], 8), ALU.mult)
        tt(s3_, s3_, bc(gs[:, 24:32], 8), ALU.add)
        max8(gs[:, 8:16], sel[:, :])
        strike(sel[:, :], gs[:, 8:16], sel[:, :])
        ts(sel[:, :], sel[:, :], -2e38, None, ALU.is_lt, None)
        tt(sel[:, :], sel[:, :], sco[:, :], ALU.mult)
        red(gs[:, 0:1], sel[:, :], ALU.add)
        recip(gs[:, 1:2], gs[:, 0:1])
        ts(wtok[:, i, :], sel[:, :], gs[:, 1:2], 2.5, ALU.mult, ALU.mult)
    dump("wtok", wtok[:, :, :])
    K.barrier()
    m3.close()

    m4 = ExitStack()
    hid = sb("hid", [128, 2, 2, 512], c=m4)
    gsl = sb("gsl", [128, 2, 512], c=m4)
    hrel = [None, None]
    gi = 0
    for e in range(65):
        src = A["ew"][e] if e < 64 else A["sw"]
        ent, wap, tk = ring.load([(0, 6144, 0, src)], 6144)
        w1 = wap[:, 0:2048].rearrange("p (k n) -> p k n", k=8)
        w3 = wap[:, 2048:4096].rearrange("p (k n) -> p k n", k=8)
        w2 = wap[:, 4096:6144].rearrange("p (k n) -> p k n", k=2)
        H = hid[:, e % 2, :, :]
        for f in range(2):
            b = bank()
            for k in range(8):
                t = mm(b[:, :], w1[:, k, f * 128:(f + 1) * 128], hT[:, k, :], tk, t_h, start=(k == 0), stop=(k == 7))
            b2 = bank()
            for k in range(8):
                t2 = mm(b2[:, :], w3[:, k, f * 128:(f + 1) * 128], hT[:, k, :], start=(k == 0), stop=(k == 7))
            g = gsl[:, gi % 2, :]
            t = act(g, b[:, :], ACT.Silu, t, hrel[gi % 2])
            give(b, t)
            t = tt(H[:, f, :], g, b2[:, :], ALU.mult, t, t2)
            hrel[gi % 2] = t
            give(b2, t)
            gi += 1
        t_h2 = t
        for i in range(4):
            for n_ in range(2):
                b = bank()
                for f in range(2):
                    t = mm(b[:, :], H[:, f, i * 128:(i + 1) * 128], w2[:, f, n_ * 512:(n_ + 1) * 512], t_h2, start=(f == 0), stop=(f == 1))
                o = fac[:, i, n_ * 512:(n_ + 1) * 512]
                if e == 0:
                    t = ts(o, b[:, :], wtok[:, i, 0:1], None, ALU.mult, None, t)
                elif e < 64:
                    t = stt(o, b[:, :], wtok[:, i, e:e + 1], o, ALU.mult, ALU.add, t)
                else:
                    t = tt(o, b[:, :], o, ALU.add, t)
                give(b, t)
        ent[2] = K.last("pe")
    dump("fac", fac[:, :, :])
    K.barrier()
    m4.close()
    m5 = ExitStack()
    lnr = sb("lnr2", [128, 2, D], c=m5)
    tl = [rowload(lnr[:, 0, :], "ln2w", K.all()), rowload(lnr[:, 1, :], "ln2b", K.all())]
    for i in range(4):
        tt(fac[:, i, :], fac[:, i, :], g12[:, 1, :], ALU.mult)
        stt(xt[:, i, :], xt[:, i, :], ALPHA, fac[:, i, :], ALU.mult, ALU.add)
        layer_norm(xt[:, i, :], lnr[:, 0, :], lnr[:, 1, :], *tl)
    dump("x2", xt[:, :, :])
    K.barrier()
    m5.close()
    m2.close()

    m6 = ExitStack()
    hT = sb("hT2", [128, 8, 512], c=m6)
    xn = sb("xn3", [128, D], c=m6)
    rope = sb("rope", [128, 4, 512], c=m6)
    t_rope = K.dma("sp", lambda e: e.dma_start(rope[:, :, :], A["rope"]), K.all())
    lamr = sb("lamr", [128, 512], c=m6)
    lms = sb("lms", [128, 8], c=m6)
    t_lam = rowload(lamr[:, :], "lam", K.all())
    gfr = g12[:, 0, :]
    t_gf = rowload(gfr, "gfin", K.all())
    for l in range(2):
        for q in range(2):
            a = lamr[:, l * 256 + q * 128:l * 256 + q * 128 + 64]
            b_ = lamr[:, l * 256 + q * 128 + 64:l * 256 + q * 128 + 128]
            tt(a, a, b_, ALU.mult, t_lam)
            red(lms[:, 2 * q:2 * q + 1], a, ALU.add)
        act(lms[:, 4:5], lms[:, 0:1], ACT.Exp, K.last("dve"))
        act(lms[:, 5:6], lms[:, 2:3], ACT.Exp)
        li = 0.8 - 0.6 * float(np.exp(-0.3 * l))
        tt(lms[:, 6 + l:7 + l], lms[:, 5:6], lms[:, 4:5], ALU.subtract, K.last("act"))
        ts(lms[:, 6 + l:7 + l], lms[:, 6 + l:7 + l], -li, None, ALU.add, None)

    def rms_rows(x, *toks):
        act(xn[:, :], x, ACT.Square, K.last("dve"), K.last("pe"), *toks, accum=mv[:, 0:1])
        act(rstd[:, 1:2], mv[:, 0:1], ACT.Sqrt, bias=EPS6, scale=1.0 / D)
        return recip(rstd[:, 0:1], rstd[:, 1:2], K.last("act"))

    def rms_T(gname, l):
        for i in range(4):
            rms_rows(xt[:, i, :])
            tn = ts(xn[:, :], xt[:, i, :], rstd[:, 0:1], None, ALU.mult, None, K.last("pe"))
            for hf in range(2):
                b = bank()
                for k in range(4):
                    t = tr(b[:, k * 128:(k + 1) * 128], xn[:, (hf * 4 + k) * 128:(hf * 4 + k + 1) * 128], ident, tn)
                for k in range(4):
                    kk = hf * 4 + k
                    t2 = act(hT[:, kk, i * 128:(i + 1) * 128], b[:, k * 128:(k + 1) * 128], ACT.Copy, t,
                             scale=cc(gname, l * 8 + kk))
                give(b, t2)
        return K.last("act")

    for l in range(2):
        t_h = rms_T("g_mix", l)
        at = ExitStack()
        qT = sb(f"qT{l}", [128, 16, 512], c=at)
        iT = sb(f"iT{l}", [128, 3, 512], c=at)
        vt = sb(f"vt{l}", [128, 4, 1024], c=at)
        iw = sb(f"iw{l}", [128, 4, 8], c=at)
        r1 = sb(f"r1{l}", [128, 2, 512], c=at)
        r2 = sb(f"r2{l}", [128, 2, 512], c=at)
        W2 = A["w_in_2"][l]

        def wl2(c0, n_):
            ent, wap, tk = ring.load([(0, 8 * n_, 8, W2[:, c0:c0 + n_].rearrange("(k p) n -> p k n", p=128))], 8 * n_)
            return ent, wap.rearrange("p (k n) -> p k n", k=8), tk

        rr = [None, None]
        n_ = 0
        for c0, w in ((0, 512), (512, 512), (1024, 512), (1536, 512), (2048, 384)):
            ent, wv, tk = wl2(c0, w)
            for j in range(w // 128):
                dst = qT[:, n_, :] if n_ < 16 else iT[:, n_ - 16, :]
                ct, sn, swp = (rope[:, 0, :], rope[:, 1, :], "sw64") if n_ < 16 else (rope[:, 2, :], rope[:, 3, :], "sw32")
                b = bank()
                for k in range(8):
                    t = mm(b[:, :], wv[:, k, j * 128:(j + 1) * 128], hT[:, k, :], t_h, tk, start=(k == 0), stop=(k == 7))
                r = r1[:, n_ % 2, :]
                t = act(r, b[:, :], ACT.Copy, t, rr[n_ % 2])
                give(b, t)
                b = bank()
                t2 = mm(b[:, :], C(swp), r, t)
                tt(dst, r, ct, ALU.mult, t, t_rope)
                rr2 = r2[:, n_ % 2, :]
                t3 = tt(rr2, b[:, :], sn, ALU.mult, t2)
                give(b, t3)
                rr[n_ % 2] = [t2, t3]
                tt(dst, dst, rr2, ALU.add)
                n_ += 1
            ent[2] = K.last("pe")
        for q in range(2):
            ent, wv, tk = wl2(2432 + 512 * q, 512)
            for i in range(4):
                b = bank()
                for k in range(8):
                    t = mm(b[:, :], hT[:, k, i * 128:(i + 1) * 128], wv[:, k, :], tk, start=(k == 0), stop=(k == 7))
                t = act(vt[:, i, q * 512:(q + 1) * 512], b[:, :], ACT.Copy, t)
                give(b, t)
            ent[2] = K.last("pe")
        ent, wv, tk = wl2(3456, 8)
        b = bank()
        for i in range(4):
            for k in range(8):
                t = mm(b[:, 8 * i:8 * i + 8], hT[:, k, i * 128:(i + 1) * 128], wv[:, k, :], tk, start=(k == 0), stop=(k == 7))
        t = ts(iw[:, :, :].rearrange("p a b -> p (a b)"), b[:, 0:32], float(32 ** -0.5 * 8 ** -0.5), None, ALU.mult, None, t)
        give(b, t)
        ent[2] = K.last("pe")
        dump(f"qT{l}", qT[:, :, :])

        spare = uT[:, :, :].rearrange("p k t -> p (k t)")[:, 4096:6144]
        sc, wk, bi, ob = (spare[:, 512 * j:512 * j + 512] for j in range(4))
        big, scr, over = ring.take(2048)
        for e in ("dve", "act", "pool"):
            K.wait(e, over)
        P = scr[:, 0:1024].rearrange("p (a b) -> p a b", a=2)
        PT = scr[:, 1024:2048].rearrange("p (a b c) -> p a b c", a=2, b=4)
        m8b = sb(f"m8b{l}", [128, 8], c=at)
        st = sb(f"st{l}", [128, 16], c=at)
        K.barrier()
        pn = 0

        def softmax(b, ns, bias, slot, k, *toks):
            p_ = P[:, slot, 0:ns]
            t = stt(p_, b[:, 0:ns], 0.125, bias, ALU.mult, ALU.add, *toks)
            give(b, t)
            red(st[:, k:k + 1], p_, ALU.max)
            t = ts(st[:, k:k + 1], st[:, k:k + 1], -1.0, None, ALU.mult, None)
            t = act(p_, p_, ACT.Exp, t, bias=st[:, k:k + 1], accum=st[:, k + 1:k + 2])
            return recip(st[:, k + 2:k + 3], st[:, k + 1:k + 2], t)

        for i in range(4):
            qs = slice(i * 128, (i + 1) * 128)
            ns = 128 * (i + 1)
            S_, W_, B_ = sc[:, 0:ns], wk[:, 0:ns], bi[:, 0:ns]
            if i > 0:
                for h in range(8):
                    hs = slice(32 * (h % 4), 32 * (h % 4) + 32)
                    b = bank()
                    t = mm(b[:, 0:ns], iT[hs, h // 4, qs], iT[hs, 2, 0:ns])
                    t2 = act(r1[:, h % 2, 0:ns], b[:, 0:ns], ACT.Relu, t, K.last("dve"))
                    give(b, t2)
                    if h == 0:
                        ts(S_, r1[:, 0, 0:ns], iw[:, i, 0:1], None, ALU.mult, None, t2)
                    else:
                        stt(S_, r1[:, h % 2, 0:ns], iw[:, i, h:h + 1], S_, ALU.mult, ALU.add, t2)
                memset(sc[0:64, ns - 64:ns], -1e30, e="dve")
                src = S_
                for r in range(16):
                    max8(m8b[:, :], src)
                    strike(W_, m8b[:, :], src)
                    src = W_
                ts(B_, W_, -2e38, -1.0, ALU.is_lt, ALU.add)
                ts(B_, B_, 1e30, None, ALU.mult, None)
            else:
                memset(B_, 0.0, e="dve")
            memset(bi[0:64, ns - 64:ns], -1e30, e="dve")
            for h in range(8):
                ps_ = slice(64 * (h % 2), 64 * (h % 2) + 64)
                b = bank()
                t = mm(b[:, 0:ns], qT[ps_, h // 2, qs], qT[ps_, 4 + h // 2, 0:ns])
                softmax(b, ns, B_, 0, 0, t, K.last("pe"))
                t_p = ts(P[:, 0, 0:ns], P[:, 0, 0:ns], st[:, 2:3], None, ALU.mult, None)
                b = bank()
                for j in range(i + 1):
                    t = tr(b[:, j * 128:(j + 1) * 128], P[:, 0, j * 128:(j + 1) * 128], ident, t_p)
                u = pn % 2
                pn += 1
                t = act(PT[:, u, 0:i + 1, :].rearrange("p a b -> p (a b)"), b[:, 0:ns], ACT.Copy, t, K.last("pe"))
                give(b, t)
                if h % 2 == 0:
                    bo = bank()
                for j in range(i + 1):
                    t2 = mm(bo[ps_, 0:128], vt[:, j, 64 * h:64 * h + 64], PT[:, u, j, :], t, start=(j == 0), stop=(j == i))
                if h % 2 == 1:
                    t = act(ym[:, h // 2, qs], bo[:, 0:128], ACT.Copy, t2)
                    give(bo, t)
            memset(B_, 0.0, e="dve")
            memset(bi[0:64, ns - 64:ns], -1e30, e="dve")
            bo = bank()
            for h in range(4):
                for c in range(2):
                    ps_ = slice(64 * c, 64 * c + 64)
                    b = bank()
                    t = mm(b[:, 0:ns], qT[ps_, 8 + h, qs], qT[ps_, 12 + h, 0:ns])
                    softmax(b, ns, B_, c, 4 * c, t, K.last("pe"))
                ts(P[:, 0, 0:ns], P[:, 0, 0:ns], st[:, 2:3], None, ALU.mult, None)
                tt(st[:, 8:9], st[:, 6:7], lms[:, 6 + l:7 + l], ALU.mult)
                t_p = stt(P[:, 0, 0:ns], P[:, 1, 0:ns], st[:, 8:9], P[:, 0, 0:ns], ALU.mult, ALU.add)
                b = bank()
                for j in range(i + 1):
                    t = tr(b[:, j * 128:(j + 1) * 128], P[:, 0, j * 128:(j + 1) * 128], ident, t_p)
                u = pn % 2
                pn += 1
                t = act(PT[:, u, 0:i + 1, :].rearrange("p a b -> p (a b)"), b[:, 0:ns], ACT.Copy, t, K.last("pe"))
                give(b, t)
                for j in range(i + 1):
                    t2 = mm(bo[:, 128 * h:128 * h + 128], PT[:, u, j, :], vt[:, j, 512 + 128 * h:640 + 128 * h], t, start=(j == 0), stop=(j == i))
            t = act(r1[:, 0, :], bo[:, :], ACT.Square, t2, K.last("dve"))
            red(st[:, 8:12], v4(r1[:, 0, :]), ALU.add, t)
            act(st[:, 12:16], st[:, 8:12], ACT.Sqrt, K.last("dve"), bias=EPS6, scale=1.0 / 128)
            recip(st[:, 8:12], st[:, 12:16], K.last("act"))
            t = tt(v4(ob[:, :]), v4(bo[:, :]), bc(st[:, 8:12], 128), ALU.mult)
            give(bo, t)
            b = bank()
            for h in range(4):
                t2 = tr(b[:, h * 128:(h + 1) * 128], ob[:, h * 128:(h + 1) * 128], ident, t)
            li = 0.8 - 0.6 * float(np.exp(-0.3 * l))
            t = ts(ym[:, 4:8, qs], v4(b[:, :]), cc("g_sub", l), 1.0 - li, ALU.mult, ALU.mult, t2)
            give(b, t)
        dump(f"ymb{l}", ym[:, :, :])
        big[2] = K.all()
        for hf in range(2):
            ent, wap, tk = ring.load([(0, 4096, 8, A["w_out_2"][l][:, hf * 512:(hf + 1) * 512].rearrange("(k p) n -> p k n", p=128))], 4096)
            wv = wap.rearrange("p (k n) -> p k n", k=8)
            for i in range(4):
                b = bank()
                for k in range(8):
                    t = mm(b[:, :], ym[:, k, i * 128:(i + 1) * 128], wv[:, k, :], tk, K.last("act"), K.last("dve") if i == 0 else None,
                           start=(k == 0), stop=(k == 7))
                hs = slice(hf * 512, (hf + 1) * 512)
                t = tt(xt[:, i, hs], xt[:, i, hs], b[:, :], ALU.add, t)
                give(b, t)
            ent[2] = K.last("pe")
        K.barrier()
        at.close()
        dump(f"xa{l}", xt[:, :, :])
        ff = ExitStack()
        hf_ = sb(f"hf{l}", [128, 22, 512], c=ff)
        gsl = sb(f"gsl{l}", [128, 2, 512], c=ff)
        t_h = rms_T("g_ffn", l)
        gr = [None, None]
        for fp in range(11):
            ws = [A["w_gate"][l][:, fp * 256:(fp + 1) * 256].rearrange("(k p) n -> p k n", p=128),
                  A["w_up"][l][:, fp * 256:(fp + 1) * 256].rearrange("(k p) n -> p k n", p=128)]
            ent, wap, tk = ring.load([(0, 2048, 8, ws[0]), (2048, 2048, 8, ws[1])], 4096)
            w1 = wap[:, 0:2048].rearrange("p (k n) -> p k n", k=8)
            w3 = wap[:, 2048:4096].rearrange("p (k n) -> p k n", k=8)
            for f in range(2):
                b = bank()
                for k in range(8):
                    t = mm(b[:, :], w1[:, k, f * 128:(f + 1) * 128], hT[:, k, :], tk, t_h, start=(k == 0), stop=(k == 7))
                b2 = bank()
                for k in range(8):
                    t2 = mm(b2[:, :], w3[:, k, f * 128:(f + 1) * 128], hT[:, k, :], start=(k == 0), stop=(k == 7))
                t = act(gsl[:, f, :], b[:, :], ACT.Silu, t, gr[f])
                give(b, t)
                t = tt(hf_[:, 2 * fp + f, :], gsl[:, f, :], b2[:, :], ALU.mult, t, t2)
                gr[f] = t
                give(b2, t)
            ent[2] = K.last("pe")
        t_hf = K.last("dve")
        for hf in range(2):
            bs = [bank() for _ in range(4)]
            for g in range(4):
                fs = list(range(g * 6, min(22, g * 6 + 6)))
                nf = len(fs)
                src = A["w_down"][l][fs[0] * 128:(fs[-1] + 1) * 128, hf * 512:(hf + 1) * 512].rearrange("(k p) n -> p k n", p=128)
                ent, wap, tk = ring.load([(0, nf * 512, nf, src)], nf * 512)
                wv = wap.rearrange("p (k n) -> p k n", k=nf)
                for i in range(4):
                    for q, f in enumerate(fs):
                        t = mm(bs[i][:, :], hf_[:, f, i * 128:(i + 1) * 128], wv[:, q, :], tk, t_hf, start=(f == 0), stop=(f == 21))
                ent[2] = t
            for i in range(4):
                hs = slice(hf * 512, (hf + 1) * 512)
                t = tt(xt[:, i, hs], xt[:, i, hs], bs[i][:, :], ALU.add, K.last("pe"))
                give(bs[i], t)
        K.barrier()
        ff.close()
        dump(f"xf{l}", xt[:, :, :])
    od = out.rearrange("(b p) d -> p b d", p=128)
    for i in range(4):
        rms_rows(xt[:, i, :])
        t = stt(xt[:, i, :], xt[:, i, :], rstd[:, 0:1], gfr, ALU.mult, ALU.mult, t_gf)
        t_o = K.dma("sp", lambda e, i=i: e.dma_start(od[:, i, :], xt[:, i, :]), t)
        K.wait("sp", t_o)
    for i in range(48):
        if K.dn[i]:
            K.wait("sp", (f"d{i}", K.dsem[i], K.dn[i]))
    m6.close()
    K.emit()


def _layout(I):
    a = {k: np.asarray(v) for k, v in I.items()}

    def colp(v):
        return v.reshape(-1, 128).T

    cols = {
        "conv_w": colp(a["ssd_conv_w"][0]), "conv_b": colp(a["ssd_conv_b"][0]), "mu": colp(a["rwkv_mu"][0]),
        "a0": colp(a["rwkv_a0"][0]), "kk": colp(a["rwkv_kk"][0]), "ka": colp(a["rwkv_ka"][0]),
        "rk": colp(a["rwkv_rk"][0]), "lnw": colp(a["rwkv_lnx_w"][0]), "lnb": colp(a["rwkv_lnx_b"][0]),
        "c": colp(a["c"][0]), "cc": colp(a["c_ctx"]), "g_mix": colp(a["g_mix_2"]), "g_ffn": colp(a["g_ffn_2"]),
        "g_sub": colp(a["g_subln_2"]), "gla_w": colp(a["gla_norm_w"][0]), "ssd_w": colp(a["ssd_norm_w"][0]),
    }
    rows = {
        "dtb": a["ssd_dt_bias"], "alog": a["ssd_a_log"], "ssd_d": a["ssd_d"], "w0": a["rwkv_w0"], "gb": a["gla_gb"],
        "ln1w": a["ln1_w"], "ln1b": a["ln1_b"], "ln2w": a["ln2_w"], "ln2b": a["ln2_b"], "rb": a["router_b"],
        "gfin": a["g_final_2"],
        "lam": np.stack([a["lam_q1_2"], a["lam_k1_2"], a["lam_q2_2"], a["lam_k2_2"]], 1),
    }

    def bdiag(x, n):
        k, m = x.shape[1:]
        o = np.zeros((n, 2 * m), x.dtype)
        for i in range(2):
            o[i * k:(i + 1) * k, i * m:(i + 1) * m] = x[i]
        return o

    def expert(w1, w3, w2):
        n = w1.shape[0]
        f = lambda w, k: w.reshape(n, k, 128, -1).transpose(0, 2, 1, 3).reshape(n, 128, -1)
        return np.concatenate([f(w1, 8), f(w3, 8), f(w2, 2)], 2)

    W = a["w_in_2"]
    ik = W[:, :, 1792:1824]
    w_in_2 = np.concatenate([W[:, :, 0:1024], W[:, :, 1832:2856], W[:, :, 1536:1792], ik, ik, ik, ik,
                             W[:, :, 1024:1536], W[:, :, 2856:3368], W[:, :, 1824:1832]], 2)
    out = {
        "x": a["x"][0], "ctx": a["ctx"][0], "ada_w": a["ada_w"][0], "ada_b": a["ada_b"], "w_in": a["w_in"][0],
        "cst": _const_mats()[1], "rope": _rope_tables(),
        "cols": np.concatenate([cols[n] for n, _ in COLS], 1),
        "rows": np.concatenate([rows[n].reshape(1, -1) for n, _ in ROWS], 1),
        "gux": bdiag(a["gla_gu"][0], 32), "w2x": bdiag(a["rwkv_w2"][0], 128), "a2x": bdiag(a["rwkv_a2"][0], 128),
        "g2": a["rwkv_g2"][0], "w_out": a["w_out"][0], "router_w": a["router_w"][0],
        "ew": expert(a["exp_w1"][0], a["exp_w3"][0], a["exp_w2"][0]),
        "sw": expert(a["sh_w1"], a["sh_w3"], a["sh_w2"])[0],
        "w_in_2": w_in_2, "w_out_2": a["w_out_2"], "w_gate": a["w_gate_2"], "w_up": a["w_up_2"], "w_down": a["w_down_2"],
    }
    return {k: np.ascontiguousarray(v) for k, v in out.items()}


def _declare(nc, arrays):
    return {k: nc.dram_tensor("in_" + k, v.shape, mybir.dt.from_np(v.dtype), kind="ExternalInput").ap()
            for k, v in arrays.items()}


def kernel(**inputs):
    import concourse.bacc as _bacc
    from concourse.bass_utils import run_bass_kernel_spmd as _run

    nc = _bacc.Bacc("TRN2", target_bir_lowering=False, num_devices=1)
    arrays = _layout(inputs)
    A = _declare(nc, arrays)
    out = nc.dram_tensor("out", (512, 1024), F32, kind="ExternalOutput").ap()
    build(nc, A, out)
    r = _run(nc, [{"in_" + k: v for k, v in arrays.items()}], core_ids=[0])
    return r.results[0]["out"].reshape(1, 512, 1024)
```

```python
import numpy as np
import concourse.bass as bass
from concourse import mybir
from contextlib import ExitStack

F32 = mybir.dt.float32
I32 = mybir.dt.int32
ALU = mybir.AluOpType
ACT = mybir.ActivationFunctionType
AX = mybir.AxisListType

D = 1024
NIN = 3504
E05 = float(np.exp(-0.5))
ALPHA = float(2 ** 0.25)

def _const_mats():
    i = np.arange(128)
    s, t = i[:, None], i[None, :]
    m = {}
    for d in range(2):
        le = (s <= t) if d == 0 else (s >= t)
        lt = (s < t) if d == 0 else (s > t)
        gt = (s > t) if d == 0 else (s < t)
        b64 = s // 64 == t // 64
        b16 = s // 16 == t // 16
        m[f"i128_{d}"] = le
        m[f"g128_{d}"] = gt
        m[f"i64_{d}"] = le & b64
        m[f"e64_{d}"] = lt & b64
        half = (s % 16 < 8) if d == 0 else (s % 16 >= 8)
        m[f"q16_{d}"] = (le & b16).astype(np.float32) - (half & b16)
        m[f"i16_{d}"] = le & b16
        m[f"c16_{d}"] = s // 16 == np.arange(8)[None, :]
        m[f"x16_{d}"] = gt & b16
        for k in range(6):
            w = 1 << k
            blk = s // (2 * w) == t // (2 * w)
            sh, th = (s // w) % 2, (t // w) % 2
            m[f"l{k}_{d}"] = blk & ((sh == 0) & (th == 1) if d == 0 else (sh == 1) & (th == 0))
    m["ones"] = np.ones((128, 128))
    m["ident"] = np.eye(128)
    m["h64"] = s // 64 == t // 64
    m["ch64"] = s // 64 == np.arange(2)[None, :]
    m["bd"] = s // 32 == np.arange(256)[None, :] // 64
    m["sw64"] = (s // 64 == t // 64) & ((s % 64 + 32) % 64 == t % 64)
    m["sw32"] = (s // 32 == t // 32) & ((s % 32 + 16) % 32 == t % 32)
    m["iota"] = t + 0 * s
    m["one8"] = np.ones((128, 64))
    ii = np.arange(128)[:, None]
    m["ii"] = ii
    m["tri64"] = (s < t)[:, 0:64]
    r0 = np.zeros((128, 128))
    r0[0] = 1
    m["row0"] = r0
    out, at, parts = {}, 0, []
    for k, v in m.items():
        v = np.asarray(v, np.float32)
        out[k] = (at, v.shape[1])
        parts.append(v)
        at += v.shape[1]
    return out, np.ascontiguousarray(np.concatenate(parts, 1))


def _rope_tables():
    out = []
    for dim in (64, 32):
        half = dim // 2
        inv = 10000.0 ** (-np.arange(0, dim, 2, dtype=np.float32) / np.float32(dim))
        ang = np.arange(512, dtype=np.float32)[:, None] * inv.astype(np.float32)[None, :]
        c, s = np.cos(ang).T, np.sin(ang).T
        p = np.arange(128) % dim
        out.append(c[p % half])
        out.append(np.where((p < half)[:, None], -s[p % half], s[p % half]))
    return np.ascontiguousarray(np.stack(out, 1).astype(np.float32))


COLS = [("conv_w", 24), ("conv_b", 8), ("mu", 36), ("a0", 4), ("kk", 2), ("ka", 2), ("rk", 2),
        ("lnw", 2), ("lnb", 2), ("c", 8), ("cc", 8), ("g_mix", 16), ("g_ffn", 16), ("g_sub", 2),
        ("gla_w", 2), ("ssd_w", 4)]
ROWS = [("dtb", 16), ("alog", 16), ("ssd_d", 8), ("w0", 512), ("gb", 256), ("ln1w", 1024), ("ln1b", 1024),
        ("ln2w", 1024), ("ln2b", 1024), ("rb", 64), ("gfin", 1024), ("lam", 512)]


def _offsets(items):
    o, at = {}, 0
    for n, w in items:
        o[n] = (at, w)
        at += w
    return o, at


CO, CN = _offsets(COLS)
RO, RN = _offsets(ROWS)


class Queues:

    def __init__(self, nc, ctx):
        self.nc, self.ctx = nc, ctx
        self.q = {e: [] for e in ("pe", "act", "dve", "pool", "sp")}
        self.sem = {e: ctx.enter_context(nc.semaphore("s_" + e)) for e in ("pe", "act", "dve", "pool")}
        self.n = {e: 0 for e in self.sem}
        self.seen = {e: {} for e in self.q}
        self.dsem = [ctx.enter_context(nc.semaphore(f"s_dma{i}")) for i in range(56)]
        self.dn = [0] * 56
        self.dnext = [0, 0]
        self.parts, self.tag = {}, ""

    def wait(self, e, *toks):
        for t in toks:
            if t is None:
                continue
            if isinstance(t, list):
                self.wait(e, *t)
                continue
            name, s, v = t
            if self.seen[e].get(name, 0) >= v:
                continue
            self.seen[e][name] = v
            self.q[e].append(lambda eng, s=s, v=v: eng.wait_ge(s, v))

    def op(self, e, fn, *toks, chain=None):
        self.wait(e, *toks)
        if (e != "pe" if chain is None else chain) and self.n[e]:
            self.wait(e, (self.tag + e, self.sem[e], self.n[e]))
        self.n[e] += 1
        s = self.sem[e]
        self.q[e].append(lambda eng: fn(eng).then_inc(s, 1))
        return (self.tag + e, s, self.n[e])

    def last(self, e):
        return (self.tag + e, self.sem[e], self.n[e]) if self.n[e] else None

    def all(self):
        return [self.last(e) for e in self.sem]

    def dma(self, e, fn, *toks):
        sw, hw = e == "pool", len(self.dsem) - len(self.dsem) // 7
        i = self.dnext[sw]
        self.dnext[sw] = (i + 1) % (len(self.dsem) - hw if sw else hw)
        i += hw * sw
        s = self.dsem[i]
        if self.dn[i]:
            self.wait(e, (f"{self.tag}d{i}", s, self.dn[i]))
        self.wait(e, *toks)
        self.dn[i] += 16
        self.q[e].append(lambda eng: fn(eng).then_inc(s, 16))
        return (f"{self.tag}d{i}", s, self.dn[i])

    def barrier(self, engines=("pe", "act", "dve", "pool")):
        toks = self.all()
        for e in engines:
            self.wait(e, *toks)

    def part(self, name):
        self.saved = (self.q, self.sem, self.n, self.seen, self.dsem, self.dn, self.dnext)
        new = lambda n: self.ctx.enter_context(self.nc.semaphore(n))
        if name not in self.parts:
            self.parts[name] = ({e: new(f"{name}_{e}") for e in self.sem}, {e: 0 for e in self.sem},
                                [new(f"{name}_d{i}") for i in range(14)], [0] * 14)
        self.sem, self.n, self.dsem, self.dn = self.parts[name]
        self.tag = name
        self.q = {e: [] for e in self.q}
        self.seen = {e: {} for e in self.q}
        self.dnext = [0, 0]

    def part_end(self, guard):
        sub = self.q
        self.q, self.sem, self.n, self.seen, self.dsem, self.dn, self.dnext = self.saved
        self.tag = ""
        for e in self.q:
            def body(eng, e=e):
                with guard(e, eng):
                    for f in sub[e]:
                        f(eng)
            self.q[e].append(body)

    def emit(self):
        block = self.ctx.enter_context(self.nc.Block())
        for e, deco in (("sp", block.sync), ("act", block.scalar), ("dve", block.vector),
                        ("pool", block.gpsimd), ("pe", block.tensor)):
            lst = self.q[e]

            def body(eng, lst=lst):
                for f in lst:
                    f(eng)
            deco(body)


def run(*gens):
    gens = list(gens)
    while gens:
        for g in list(gens):
            try:
                next(g)
            except StopIteration:
                gens.remove(g)


class Ring:

    def __init__(self, K, buf, size):
        self.K, self.buf, self.size, self.pos, self.live = K, buf, size, 0, []

    def take(self, n):
        if self.pos + n > self.size:
            self.pos = 0
        a, b = self.pos, self.pos + n
        self.pos = b
        over = [x for x in self.live if x[0] < b and a < x[1]]
        self.live = [x for x in self.live if not (x[0] < b and a < x[1])]
        ent = [a, b, None]
        self.live.append(ent)
        for x in over:
            assert x[2] is not None, "ring slot still in use"
        return ent, self.buf[:, a:b], [x[2] for x in over]

    def load(self, srcs, n):
        ent, ap, over = self.take(n)
        toks = []
        for o, w, a, src in srcs:
            dst = ap[:, o:o + w]
            if a:
                dst = dst.rearrange("p (a b) -> p a b", a=a)
            toks.append(self.K.dma("sp", lambda e, dst=dst, src=src: e.dma_start(dst, src), over))
        return ent, ap, toks


def build(nc, A, out, DBG=None):
    ctx = ExitStack()
    with ctx:
        _program(nc, ctx, A, out, DBG)


def _program(nc, ctx, A, out, DBG):
    K = Queues(nc, ctx)
    op = K.op
    cmap, _ = _const_mats()

    def sb(name, shape, dt=F32, c=ctx):
        return c.enter_context(nc.sbuf_tensor(name, shape, dt))

    banks = [ctx.enter_context(nc.psum_tensor(f"ps{i}", [128, 512], F32)) for i in range(8)]
    free = [(b, None) for b in banks]

    def bank():
        b, tok = free.pop(0)
        K.wait("pe", tok)
        return b

    def give(b, *toks):
        free.append((b, list(toks)))

    def mm(o, l, r, *toks, start=True, stop=True, after=False):
        return op("pe", lambda e: e.matmul(o, l, r, start=start, stop=stop), *toks, chain=after)

    def tr(o, i, idn, *toks):
        return op("pe", lambda e: e.transpose(o, i, idn), *toks)

    def tt(o, a, b, alu, *toks, e="dve"):
        return op(e, lambda g: g.tensor_tensor(o, a, b, alu), *toks)

    def ts(o, a, s1, s2, o1, o2, *toks, e="dve"):
        if s2 is None:
            return op(e, lambda g: g.tensor_scalar(o, a, s1, None, o1), *toks)
        return op(e, lambda g: g.tensor_scalar(o, a, s1, s2, o1, o2), *toks)

    def stt(o, a, s, b, o1, o2, *toks):
        return op("dve", lambda g: g.scalar_tensor_tensor(out=o, in0=a, scalar=s, in1=b, op0=o1, op1=o2), *toks)

    def act(o, i, f, *toks, bias=None, scale=1.0, accum=None):
        kw = {"scale": scale}
        if bias is not None:
            kw["bias"] = bias
        if accum is not None:
            kw["accum_out"] = accum
        return op("act", lambda g: g.activation(o, i, f, **kw), *toks)

    def copy(o, i, *toks, e="dve"):
        if e == "act":
            return act(o, i, ACT.Copy, *toks)
        return op(e, lambda g: g.tensor_copy(o, i), *toks)

    def memset(o, v, *toks, e="pool"):
        return op(e, lambda g: g.memset(o, v), *toks)

    def ttr(o, a, b, sc_, init, o0, o1, acc, *toks):
        return op("dve", lambda g: g.tensor_tensor_reduce(out=o, in0=a, in1=b, scale=sc_, scalar=init, op0=o0, op1=o1,
                                                          accum_out=acc), *toks)

    def recip(o, i, *toks):
        return op("dve", lambda g: g.reciprocal(o, i), *toks)

    def max8(o, i, *toks):
        return op("dve", lambda g: g.max(o, i), *toks)

    def strike(o, m, i, *toks):
        return op("dve", lambda g: g.match_replace(out=o, in_to_replace=m, in_values=i, imm_value=-3e38), *toks)

    def red(o, i, alu, *toks):
        return op("dve", lambda g: g.tensor_reduce(o, i, AX.X, alu), *toks)

    def dump(name, ap, *toks):
        if DBG is None or name not in DBG:
            return
        K.wait("sp", K.all())
        t = K.dma("sp", lambda e: e.dma_start(DBG[name], ap))
        for e in ("pe", "act", "dve", "pool"):
            K.wait(e, t)

    def bc(ap, n):
        return ap.unsqueeze(2).to_broadcast([ap.shape[0], ap.shape[1], n])

    def bcm(ap, n):
        return ap.unsqueeze(1).to_broadcast([ap.shape[0], n, ap.shape[1]])

    csb = sb("csb", [128, A["cst"].shape[1]])
    col = sb("col", [128, CN])
    xt = sb("xt", [128, 4, D])
    RS = 12288
    ringbuf = sb("ring", [128, RS])
    ring = Ring(K, ringbuf, RS)
    t_cst = K.dma("sp", lambda e: e.dma_start(csb[:, :], A["cst"]))
    t_col = K.dma("sp", lambda e: e.dma_start(col[:, :], A["cols"]))
    t_x = K.dma("sp", lambda e: e.dma_start(xt[:, :, :], A["x"].rearrange("(b p) d -> p b d", p=128)))

    def C(name):
        a, w = cmap[name]
        return csb[:, a:a + w]

    def cc(name, j=0, n=1):
        a = CO[name][0] + j
        return col[:, a:a + n]

    ident = C("ident")

    def rowload(dst, name, *toks, e="sp", j=0, n=None):
        a, w = RO[name]
        n = n or w
        src = A["rows"][:, a + j:a + j + n].partition_broadcast(128) if False else A["rows"][0:1, a + j:a + j + n].to_broadcast([128, n])
        return K.dma(e, lambda g: g.dma_start(dst, src), *toks)

    for e in ("pe", "dve", "act", "pool"):
        K.wait(e, t_cst, t_col)

    eps5 = sb("eps5", [128, 4])
    t_eps = memset(eps5[:, 0:1], 1e-5)
    memset(eps5[:, 1:2], 64e-5)
    memset(eps5[:, 2:3], 1e-6)
    t_eps = memset(eps5[:, 3:4], 1.0)
    K.wait("act", t_eps)
    EPS5, EPS64, EPS6, ONE = (eps5[:, j:j + 1] for j in range(4))

    stt6 = sb("stt6", [128, 2, 6])
    mv = sb("mv", [128, 2])
    rstd = sb("rstd", [128, 2])

    def ln_stats(src, *toks):
        for j in range(2):
            op("dve", lambda g, j=j: g.bn_stats(stt6[:, j, :], src[:, j * 512:(j + 1) * 512]), *toks)
        t = op("dve", lambda g: g.bn_aggr(mv[:, :], stt6[:, :, :]))
        t = act(rstd[:, 1:2], mv[:, 1:2], ACT.Sqrt, t, bias=EPS5)
        return recip(rstd[:, 0:1], rstd[:, 1:2], t)

    uT = sb("uT", [128, 8, 768])
    ym = uT[:, :, :].rearrange("p k t -> p (k t)")[:, 0:4096].rearrange("p (k t) -> p k t", k=8)
    modc = sb("modc", [128, 2, 8, 2])
    scv = sb("scv", [128, 8, 2])
    sig = sb("sigc", [128, 16])
    act(sig[:, 0:16], cc("c", 0, 16), ACT.Sigmoid)
    t = tt(sig[:, 0:16], sig[:, 0:16], cc("c", 0, 16), ALU.mult, K.last("act"))
    t_sc = copy(scv[:, :, :], sig[:, 0:16].rearrange("p (b k) -> p k b", b=2))

    def ada(sec, mrow, brow, g12=None):
        tb = K.dma("sp", lambda e: e.dma_start(brow[0:1, :], A["ada_b"][0:1, sec * D:(sec + 1) * D]), K.last("pe"))
        for h in range(2):
            w = sec * D + h * 512
            ent, wap, tk = ring.load([(0, 4096, 8, A["ada_w"][:, w:w + 512].rearrange("(k p) n -> p k n", p=128))], 4096)
            wv = wap.rearrange("p (k n) -> p k n", k=8)
            b = bank()
            mm(b[0:2, :], C("ones")[0:1, 0:2], brow[0:1, h * 512:(h + 1) * 512], tb, tk, t_sc, start=True, stop=False)
            for k in range(8):
                t = mm(b[0:2, :], scv[:, k, :], wv[:, k, :], start=False, stop=(k == 7))
            ent[2] = t
            t = act(mrow[0:2, h * 512:(h + 1) * 512], b[0:2, :], ACT.Copy, t, K.last("pe"))
            give(b, t)
            yield
        slot = {0: 0, 1: 1}.get(sec)
        if slot is not None:
            b = bank()
            for k in range(8):
                t = tr(b[:, 2 * k:2 * k + 2], mrow[0:2, k * 128:(k + 1) * 128], ident[0:2, 0:2], t)
            yield
            t = ts(modc[:, slot, :, :].rearrange("p k b -> p (k b)"), b[:, 0:16], 1.0 if slot in (1, 3) else 0.0, None, ALU.add, None, t)
            give(b, t)
        else:
            for h in range(2):
                b = bank()
                t = mm(b[:, :], C("row0")[0:2, :], mrow[0:2, h * 512:(h + 1) * 512], t)
                t2 = act(g12[:, {2: 0, 5: 1, 3: 2, 4: 3}[sec], h * 512:(h + 1) * 512], b[:, :], ACT.Identity, t,
                         bias=1.0 if sec == 4 else 0.0)
                give(b, t2)
        yield

    with ExitStack() as s0:
        mrow = sb("mrow", [2, D], c=s0)
        brow = sb("brow", [1, D], c=s0)
        run(ada(0, mrow, brow))
        run(ada(1, mrow, brow))
        K.barrier()

    m1 = ExitStack()
    uctx = ExitStack()
    rwm = sb("rwm", [128, 9, 768], c=m1)
    m1b = ExitStack()
    zx = sb("zx", [128, 4, 512], c=m1b)
    xbc = sb("xbc", [128, 8, 768], c=m1b)
    gqT = sb("gqT", [128, 512], c=m1b)
    gkT = sb("gkT", [128, 768], c=m1b)
    gkv = sb("gkv", [128, 6, 384], c=m1b)
    ogt = sb("ogt", [128, 4, 256], c=m1b)
    gdT = sb("gdT", [32, 768], c=m1b)
    dtt = sb("dtt", [128, 6, 16], c=m1b)
    ctxt = sb("ctxt", [128, 2, D], c=uctx)
    xn = sb("xn", [128, 2, D], c=uctx)
    t_ctx = K.dma("sp", lambda e: e.dma_start(ctxt[:, :, :], A["ctx"].rearrange("(b p) d -> p b d", p=128)), K.all())
    t_mod = K.last("dve")
    xnt = [None, None]
    for b6 in range(6):
        src = ctxt[:, b6, :] if b6 < 2 else xt[:, b6 - 2, :]
        ln_stats(src, t_x, t_ctx)
        ts(xn[:, b6 % 2, :], src, mv[:, 0:1], rstd[:, 0:1], ALU.subtract, ALU.mult, xnt[b6 % 2])
        tn = K.last("dve")
        s = 1 if b6 < 2 else 0
        for hf in range(2):
            b = bank()
            for k in range(4):
                t = tr(b[:, k * 128:(k + 1) * 128], xn[:, b6 % 2, (hf * 4 + k) * 128:(hf * 4 + k + 1) * 128], ident, tn)
            xnt[b6 % 2] = t
            for k in range(4):
                kk = hf * 4 + k
                t2 = act(uT[:, kk, b6 * 128:(b6 + 1) * 128], b[:, k * 128:(k + 1) * 128], ACT.Identity, t, t_mod,
                         bias=modc[:, 0, kk, s:s + 1], scale=modc[:, 1, kk, s:s + 1])
            give(b, t2)
    t_u = K.last("act")
    K.barrier()
    uctx.close()
    raw = sb("raw", [128, 2, 768], c=uctx)
    cv = sb("cv", [128, 2, 768], c=uctx)
    dtb = sb("dtb", [128, 16], c=uctx)
    sg = sb("sg", [128, 96], c=uctx)
    oms = sb("oms", [128, 2, 9], c=uctx)
    t_dtb = rowload(dtb[:, :], "dtb", K.all())
    dump("uT", uT[:, :, :])

    def wload(c0, n):
        ent, wap, tk = ring.load([(0, 8 * n, 8, A["w_in"][:, c0:c0 + n].rearrange("(k p) n -> p k n", p=128))], 8 * n)
        return ent, wap.rearrange("p (k n) -> p k n", k=8), tk

    def proj_tok(wv, lo, n, b6, tk):
        b = bank()
        for k in range(8):
            t = mm(b[:, 0:n], uT[:, k, b6 * 128:(b6 + 1) * 128], wv[:, k, lo:lo + n], t_u, tk, start=(k == 0), stop=(k == 7))
        return b, t

    def proj_ch(wv, lo, n, tk, ctxtoo=True):
        b = bank()
        for k in range(8):
            t = mm(b[0:n, :], wv[:, k, lo:lo + n], uT[:, k, 256:768], t_u, tk, start=(k == 0), stop=(k == 7))
        b2 = None
        if ctxtoo:
            b2 = bank()
            for k in range(8):
                t = mm(b2[0:n, 0:256], wv[:, k, lo:lo + n], uT[:, k, 0:256], start=(k == 0), stop=(k == 7))
        return b, b2, t

    ent, wv, tk = wload(1536, 16)
    for b6 in range(6):
        b, t = proj_tok(wv, 0, 16, b6, tk)
        t = tt(dtt[:, b6, :], b[:, 0:16], dtb[:, :], ALU.add, t, t_dtb)
        give(b, t)
    ent[2] = K.last("pe")
    dtf = dtt[:, :, :].rearrange("p a b -> p (a b)")
    sp1 = sg[:, 0:96]
    t = act(sp1, dtf, ACT.Abs, K.last("dve"))
    act(sp1, sp1, ACT.Exp, scale=-1.0)
    t = act(sp1, sp1, ACT.Ln, bias=ONE)
    t_dt = stt(dtf, dtf, 0.0, sp1, ALU.max, ALU.add, t)
    ent, wv, tk = wload(0, 512)
    for i in range(4):
        b, t = proj_tok(wv, 0, 512, i + 2, tk)
        t = act(zx[:, i, :], b[:, :], ACT.Silu, t)
        give(b, t)
    ent[2] = K.last("pe")
    ent, wv, tk = wload(3248, 256)
    for i in range(4):
        b, t = proj_tok(wv, 0, 256, i + 2, tk)
        t = act(ogt[:, i, :], b[:, 0:256], ACT.Silu, t)
        give(b, t)
    ent[2] = K.last("pe")
    ent, wv, tk = wload(2832, 384)
    for b6 in range(6):
        b, t = proj_tok(wv, 0, 384, b6, tk)
        t = copy(gkv[:, b6, :], b[:, 0:384], t)
        give(b, t)
    b, b2, t = proj_ch(wv, 0, 128, tk)
    t1 = copy(gkT[:, 256:768], b[:, :], t, e="act")
    t2 = copy(gkT[:, 0:256], b2[:, 0:256], t, e="act")
    give(b, t1)
    give(b2, t2)
    ent[2] = K.last("pe")
    ent, wv, tk = wload(2704, 128)
    b, _, t = proj_ch(wv, 0, 128, tk, False)
    t1 = act(gqT[:, :], b[:, :], ACT.Copy, t, scale=32 ** -0.5)
    give(b, t1)
    ent[2] = t
    ent, wv, tk = wload(3216, 32)
    b, b2, t = proj_ch(wv, 0, 32, tk)
    t1 = copy(gdT[:, 256:768], b[0:32, :], t, e="act")
    t2 = copy(gdT[:, 0:256], b2[0:32, 0:256], t, e="act")
    give(b, t1)
    give(b2, t2)
    ent[2] = t
    rawr = [None, None]
    cvr = [None, None]
    ts(oms[:, 0, :], cc("mu", 0, 9), -1.0, 1.0, ALU.mult, ALU.add)
    tt(oms[:, 0, :], oms[:, 0, :], cc("mu", 9, 9), ALU.subtract)
    tt(oms[:, 1, :], oms[:, 0, :], cc("mu", 18, 9), ALU.subtract)
    tt(oms[:, 1, :], oms[:, 1, :], cc("mu", 27, 9), ALU.subtract)
    n = 0
    for g in range(5):
        c0, w = [(512, 512), (1024, 512), (1552, 512), (2064, 512), (2576, 128)][g]
        ent, wv, tk = wload(c0, w)
        for j in range(w // 128):
            b, b2, t = proj_ch(wv, j * 128, 128, tk)
            r = raw[:, n % 2, :]
            t1 = act(r[:, 256:768], b[:, :], ACT.Copy, t, rawr[n % 2])
            t2 = act(r[:, 0:256], b2[:, 0:256], ACT.Copy)
            give(b, t1)
            give(b2, t2)
            if n < 8:
                o = cv[:, n % 2, :]
                ts(o, r, cc("conv_w", 8 + n), cc("conv_b", n), ALU.mult, ALU.add, t2, cvr[n % 2])
                for a, z in ((0, 256), (256, 768)):
                    stt(o[:, a + 1:z], r[:, a:z - 1], cc("conv_w", n), o[:, a + 1:z], ALU.mult, ALU.add)
                    t = stt(o[:, a:z - 1], r[:, a + 1:z], cc("conv_w", 16 + n), o[:, a:z - 1], ALU.mult, ALU.add)
                rawr[n % 2] = t
                t = act(xbc[:, n, :], o, ACT.Silu, t)
                cvr[n % 2] = t
            else:
                m = n - 8
                o = rwm[:, m, :]
                mu = [cc("mu", 9 * q + m) for q in range(4)]
                ts(o[:, 0:256], r[:, 0:256], oms[:, 0, m:m + 1], None, ALU.mult, None, t2)
                stt(o[:, 1:256], r[:, 0:255], mu[0], o[:, 1:256], ALU.mult, ALU.add)
                stt(o[:, 0:255], r[:, 1:256], mu[1], o[:, 0:255], ALU.mult, ALU.add)
                ts(o[:, 256:768], r[:, 256:768], oms[:, 1, m:m + 1], None, ALU.mult, None)
                og = o[:, 256:768].rearrange("p (r c) -> p r c", c=64)
                rg = r[:, 256:768].rearrange("p (r c) -> p r c", c=64)
                stt(og[:, :, 1:64], rg[:, :, 0:63], mu[0], og[:, :, 1:64], ALU.mult, ALU.add)
                stt(og[:, :, 0:63], rg[:, :, 1:64], mu[1], og[:, :, 0:63], ALU.mult, ALU.add)
                stt(o[:, 320:768], r[:, 256:704], mu[2], o[:, 320:768], ALU.mult, ALU.add)
                t = stt(o[:, 256:704], r[:, 320:768], mu[3], o[:, 256:704], ALU.mult, ALU.add)
                rawr[n % 2] = t
            n += 1
        ent[2] = K.last("pe")
    K.barrier()
    uctx.close()
    dump("xbc", xbc[:, :, :])
    dump("rwm", rwm[:, :, :])
    dump("dtt", dtt[:, :, :])

    FW = [0, 1, 2, 3, 4, 5]
    BW = [1, 0, 5, 4, 3, 2]
    ORD = (FW, BW)

    s1 = ExitStack()
    btk = sb("btk", [128, 2, 256], c=s1)
    las = sb("las", [128, 6, 16], c=s1)
    na = sb("na", [128, 16], c=s1)
    ysd = sb("ysd", [128, 4, 512], c=s1)
    gtm = sb("gtm", [128, 2, 256], c=s1)
    big, scr, over = ring.take(8704)
    K.wait("dve", over)
    K.wait("act", over)
    K.wait("pool", over)
    xst = scr[:, 6144:7168].rearrange("p (a b) -> p a b", a=2)
    Hs = scr[:, 7168:8192].rearrange("p (a b) -> p a b", a=2)
    yo = scr[:, 8192:8704]
    lax = scr[:, 0:2048].rearrange("p (a b) -> p a b", a=2)
    sct = scr[:, 2048:4096].rearrange("p (a b) -> p a b", a=2)
    xdt = scr[:, 4096:5120].rearrange("p (a b) -> p a b", a=2)
    xde = scr[:, 5120:6144].rearrange("p (a b) -> p a b", a=2)
    ex3 = sb("ex3", [128, 2, 24], c=s1)
    sdd = sb("sdd", [128, 8], c=s1)
    t_na = rowload(na[:, :], "alog", K.all())
    t_sdd = rowload(sdd[:, :], "ssd_d", K.all())
    t = act(na[:, :], na[:, :], ACT.Exp, t_na)
    t = ts(na[:, :], na[:, :], -1.0, None, ALU.mult, None, t)
    tt(las[:, :, :], dtt[:, :, :], bcm(na[:, :], 6), ALU.mult, t_dt)
    memset(Hs[:, :, :], 0.0, e="dve")
    t_las = K.last("dve")

    def ssd_unit(d, b6, first):
        u = d
        tok = slice(b6 * 128, (b6 + 1) * 128)
        b = bank()
        for j in range(4):
            t = tr(b[:, j * 128:(j + 1) * 128], xbc[:, j, tok], ident, K.last("act"))
        t1 = act(xst[:, u, :], b[:, :], ACT.Copy, t, K.last("dve"))
        give(b, t1)
        b = bank()
        for j in range(2):
            t = tr(b[:, j * 128:(j + 1) * 128], xbc[:, 4 + j, tok], ident)
        t2 = act(btk[:, u, :], b[:, 0:256], ACT.Copy, t)
        give(b, t2)
        yield
        la = las[:, b6, 8 * d:8 * d + 8]
        b = bank()
        mm(b[:, 0:8], C(f"i128_{d}"), la, t_las)
        mm(b[:, 8:16], C(f"g128_{d}"), la)
        t = mm(b[:, 16:24], C("ones"), la)
        t = act(ex3[:, u, :], b[:, 0:24], ACT.Exp, t, K.last("dve"))
        give(b, t)
        t_ex = t
        t_xdt = tt(xdt[:, u, :].rearrange("p (h q) -> p h q", q=64), xst[:, u, :].rearrange("p (h q) -> p h q", q=64),
                   bc(dtt[:, b6, 8 * d:8 * d + 8], 64), ALU.mult, t1, K.last("pe"))
        t_xde = tt(xde[:, u, :].rearrange("p (h q) -> p h q", q=64), xdt[:, u, :].rearrange("p (h q) -> p h q", q=64),
                   bc(ex3[:, u, 8:16], 64), ALU.mult, t_ex, K.last("pe"))
        yield
        if b6 >= 2:
            b = bank()
            for g in range(2):
                t = mm(b[:, g * 128:(g + 1) * 128], xbc[:, 4 + g, tok], xbc[:, 6 + g, tok])
            t_g = tt(gtm[:, u, :].rearrange("p (g t) -> p g t", g=2), b[:, 0:256].rearrange("p (g t) -> p g t", g=2),
                     bcm(C(f"i128_{d}"), 2), ALU.mult, t)
            give(b, t_g)
            t_lx = tt(lax[:, u, :].rearrange("p (h s) -> p h s", h=8), bcm(C(f"g128_{d}"), 8), bc(la, 128), ALU.mult)
            yield
            for hf in range(2):
                b = bank()
                for h in range(4):
                    hh = hf * 4 + h
                    t = mm(b[:, h * 128:(h + 1) * 128], lax[:, u, hh * 128:(hh + 1) * 128], C(f"i128_{d}"), t_lx)
                o = sct[:, u, hf * 512:(hf + 1) * 512]
                t = act(o, b[:, :], ACT.Exp, t)
                give(b, t)
                t_sc_ = tt(o.rearrange("p (h t) -> p h t", h=4), o.rearrange("p (h t) -> p h t", h=4),
                          bcm(gtm[:, u, hf * 128:(hf + 1) * 128], 4), ALU.mult, t)
                yield
            by = bank()
            for h in range(8):
                t_y = mm(by[:, h * 64:(h + 1) * 64], sct[:, u, h * 128:(h + 1) * 128], xdt[:, u, h * 64:(h + 1) * 64], t_sc_, t_xdt)
            bo = bank()
            for g in range(2):
                t_o = mm(bo[:, g * 256:(g + 1) * 256], xbc[:, 6 + g, tok], Hs[:, d, g * 256:(g + 1) * 256], K.last("dve"))
            yield
            ydst = ysd[:, b6 - 2, :]
            t = tt(yo[:, :].rearrange("p (h q) -> p h q", q=64), bo[:, :].rearrange("p (h q) -> p h q", q=64),
                   bc(ex3[:, u, 0:8], 64), ALU.mult, t_o)
            give(bo, t)
            if first:
                t = tt(ydst, by[:, :], yo[:, :], ALU.add, t_y)
                give(by, t)
                tt(yo[:, :].rearrange("p (h q) -> p h q", q=64), xst[:, u, :].rearrange("p (h q) -> p h q", q=64),
                   bc(sdd[:, :], 64), ALU.mult, t_sdd)
            else:
                t = tt(yo[:, :], by[:, :], yo[:, :], ALU.add, t_y)
                give(by, t)
            tt(ydst, ydst, yo[:, :], ALU.add)
        b = bank()
        for g in range(2):
            t = mm(b[:, g * 256:(g + 1) * 256], btk[:, u, g * 128:(g + 1) * 128], xde[:, u, g * 256:(g + 1) * 256], t2, t_xde)
        yield
        tt(Hs[:, d, :].rearrange("p (h q) -> p h q", q=64), Hs[:, d, :].rearrange("p (h q) -> p h q", q=64),
           bc(ex3[:, u, 16:24], 64), ALU.mult, t)
        t = tt(Hs[:, d, :], Hs[:, d, :], b[:, :], ALU.add)
        give(b, t)
        yield

    seen = set()
    for i in range(6):
        gens = []
        for d in range(2):
            b6 = ORD[d][i]
            gens.append(ssd_unit(d, b6, b6 not in seen))
            seen.add(b6)
        for g in gens:
            run(g)
    dump("ysd", ysd[:, :, :])
    for i in range(4):
        tt(ysd[:, i, :], ysd[:, i, :], zx[:, i, :], ALU.mult)
        for g in range(2):
            src = ysd[:, i, g * 256:(g + 1) * 256]
            t = act(yo[:, g * 256:(g + 1) * 256], src, ACT.Square, K.last("dve"), K.last("pe"), accum=mv[:, g:g + 1])
        t = act(rstd[:, 0:2], mv[:, 0:2], ACT.Sqrt, t, bias=EPS5, scale=1.0 / 256)
        recip(mv[:, 0:2], rstd[:, 0:2], t)
        for g in range(2):
            t = ts(yo[:, g * 256:(g + 1) * 256], ysd[:, i, g * 256:(g + 1) * 256], mv[:, g:g + 1], None, ALU.mult, None)
        b = bank()
        for j in range(4):
            t = tr(b[:, j * 128:(j + 1) * 128], yo[:, j * 128:(j + 1) * 128], ident, K.last("dve"))
        for j in range(4):
            t2 = ts(ym[:, j, i * 128:(i + 1) * 128], b[:, j * 128:(j + 1) * 128], cc("ssd_w", j), None, ALU.mult, None, t)
        give(b, t2)
    K.barrier()
    big[2] = K.all()
    s1.close()

    s2 = ExitStack()
    lag = sb("lag", [128, 6, 256], c=s2)
    gux = sb("gux", [32, 256], c=s2)
    gbr = sb("gbr", [1, 256], c=s2)
    big, scr, over = ring.take(8704)
    for e in ("dve", "act", "pool"):
        K.wait(e, over)
    gt1 = scr[:, 0:1536].rearrange("p (a b) -> p a b", a=6)
    kde = scr[:, 6144:7168]
    stm = scr[:, 7168:7680]
    og2 = scr[:, 7680:8704].rearrange("p (i n) -> p i n", i=4)
    Sg = scr[:, 1536:6144].rearrange("p (d c n) -> p d c n", d=2, c=9)
    cq = sb("cq", [128, 128], c=s2)
    eq = sb("eq", [128, 4, 128], c=s2)
    etot = sb("etot", [128, 8], c=s2)
    qp = sb("qp", [128, 2, 128], c=s2)
    qx = sb("qx", [128, 1152], c=s2)
    sTg = sb("sTg", [128, 512], c=s2)
    t1 = K.dma("sp", lambda e: e.dma_start(gux[:, :], A["gux"]), K.all())
    t2 = K.dma("sp", lambda e: e.dma_start(gbr[:, :], A["rows"][0:1, RO["gb"][0]:RO["gb"][0] + 256]), K.all())
    memset(qx[:, :], 0.0)
    memset(Sg[:, :, :, :], 0.0)
    for b6 in range(6):
        b = bank()
        mm(b[:, 0:256], C("ones")[0:1, :], gbr[0:1, :], t1, t2, start=True, stop=False)
        t = mm(b[:, 0:256], gdT[0:32, b6 * 128:(b6 + 1) * 128], gux[:, :], start=False, stop=True)
        t = copy(lag[:, b6, :], b[:, 0:256], t)
        give(b, t)
    lf = lag[:, :, :].rearrange("p a b -> p (a b)")
    gf = gt1[:, :, :].rearrange("p a b -> p (a b)")
    act(gf, lf, ACT.Abs, K.last("dve"))
    act(gf, gf, ACT.Exp, scale=-1.0)
    t = act(gf, gf, ACT.Ln, bias=ONE)
    t_lag = stt(lf, lf, 0.0, gf, ALU.min, ALU.subtract, t)
    dump("lag", lag[:, :, :])

    def gla_unit(d, b6, first, s_in):
        tok = slice(b6 * 128, (b6 + 1) * 128)
        la = lag[:, b6, 128 * d:128 * d + 128]
        b = bank()
        mm(b[:, 0:128], la, C(f"q16_{d}"), t_lag)
        mm(b[:, 128:256], la, C(f"i16_{d}"))
        mm(b[:, 256:264], la, C(f"c16_{d}"))
        t = mm(b[:, 384:512], C(f"x16_{d}"), la)
        t3 = ts(cq[:, :], b[:, 0:128], 640.0, -640.0, ALU.min, ALU.max, t, K.last("act"))
        pe0 = K.last("pe")
        t2 = act(eq[:, 3, :], b[:, 384:512], ACT.Exp, t, pe0, K.last("dve"), scale=1.0 / 16)
        act(etot[:, :], b[:, 256:264], ACT.Exp, K.last("dve"), scale=1.0 / 16)
        if b6 >= 2:
            act(eq[:, 2, :], b[:, 128:256], ACT.Exp, scale=1.0 / 16)
            act(eq[:, 0, :], cq[:, :], ACT.Exp, t3, scale=1.0 / 16)
            act(eq[:, 1, :], cq[:, :], ACT.Exp, scale=-1.0 / 16)
        t_e = K.last("act")
        give(b, t_e, t3)
        kd = eq[:, 3, :]
        tt(kd, kd, gkv[:, b6, 0:128], ALU.mult, t_e)
        t_k = tt(kde[:, :].rearrange("p (c k) -> p c k", c=8), bcm(kd, 8), bc(C(f"c16_{d}"), 128), ALU.mult, pe0)
        order = range(8) if d == 0 else range(7, -1, -1)
        S = Sg[:, d, :, :]
        chunks = list(order)
        for jj in range(4):
            b = bank()
            for q in range(2):
                c = chunks[2 * jj + q]
                t = mm(b[:, q * 256:(q + 1) * 256], kde[:, c * 128:(c + 1) * 128], gkv[:, b6, 128:384], t_k)
            t = tt(stm[:, :].rearrange("p (a b) -> p a b", a=2), b[:, :].rearrange("p (a b) -> p a b", a=2),
                   bcm(C("bd"), 2), ALU.mult, t)
            give(b, t)
            for q in range(2):
                n_ = 2 * jj + q
                t = stt(S[:, n_ + 1, :], S[:, n_, :], etot[:, chunks[n_]:chunks[n_] + 1], stm[:, q * 256:(q + 1) * 256],
                        ALU.mult, ALU.add)
        if b6 >= 2:
            xt_ = slice((b6 - 2) * 128, (b6 - 1) * 128)
            tt(qp[:, 0, :], gqT[:, xt_], eq[:, 0, :], ALU.mult)
            t_qp = tt(qp[:, 1, :], gkT[:, tok], eq[:, 1, :], ALU.mult)
            t_qx = tt(qx[:, :].rearrange("p (c w) -> p c w", w=144)[:, :, 0:16],
                      gqT[:, xt_].rearrange("p (c w) -> p c w", w=16),
                      eq[:, 2, :].rearrange("p (c w) -> p c w", w=16), ALU.mult)
            b = bank()
            for h in range(4):
                hs = slice(32 * h, 32 * h + 32)
                t = mm(b[:, h * 128:(h + 1) * 128], qp[hs, 1, :], qp[hs, 0, :], t_qp, after=h > 0)
            t_s = tt(sTg[:, :].rearrange("p (h t) -> p h t", h=4), b[:, :].rearrange("p (h t) -> p h t", h=4),
                     bcm(C(f"i16_{d}"), 4), ALU.mult, t)
            give(b, t_s)
            b = bank()
            for n_ in range(8):
                c = chunks[n_]
                mm(b[:, 0:256], qx[:, c * 128:(c + 1) * 128], S[:, n_, :], t_qx, start=(n_ == 0), stop=False)
            for h in range(4):
                t = mm(b[:, 64 * h:64 * h + 64], sTg[:, h * 128:(h + 1) * 128], gkv[:, b6, 128 + 64 * h:192 + 64 * h],
                       t_s, start=False, stop=(h == 3))
            o = og2[:, b6 - 2, :]
            if first:
                t = copy(o, b[:, 0:256], t)
            else:
                t = tt(o, o, b[:, 0:256], ALU.add, t)
            give(b, t)
        copy(S[:, 0, :], S[:, 8, :], K.last("pe"))
        yield

    K.barrier(("pe", "act", "dve"))
    seen = set()
    for i in range(6):
        for d in range(2):
            b6 = ORD[d][i]
            run(gla_unit(d, b6, b6 not in seen, None))
            seen.add(b6)
    dump("og2", og2[:, :, :])
    sq = gt1[:, 0:2, :].rearrange("p a b -> p (a b)")
    for i in range(4):
        o = og2[:, i, :]
        act(sq[:, 0:256], o, ACT.Square, K.last("dve"), K.last("pe"))
        red(etot[:, 0:4], sq[:, 0:256].rearrange("p (h v) -> p h v", h=4), ALU.add, K.last("act"))
        act(etot[:, 4:8], etot[:, 0:4], ACT.Sqrt, K.last("dve"), bias=EPS5, scale=1.0 / 64)
        recip(etot[:, 0:4], etot[:, 4:8], K.last("act"))
        tt(sq[:, 256:512].rearrange("p (h v) -> p h v", h=4), o.rearrange("p (h v) -> p h v", h=4),
           bc(etot[:, 0:4], 64), ALU.mult, K.last("pe"))
        t = tt(sq[:, 256:512], sq[:, 256:512], ogt[:, i, :], ALU.mult)
        b = bank()
        for j in range(2):
            t2 = tr(b[:, j * 128:(j + 1) * 128], sq[:, 256 + j * 128:384 + j * 128], ident, t)
        for j in range(2):
            t = ts(ym[:, 6 + j, i * 128:(i + 1) * 128], b[:, j * 128:(j + 1) * 128], cc("gla_w", j), None, ALU.mult, None, t2)
        give(b, t)
    K.barrier()
    big[2] = K.all()
    s2.close()
    m1b.close()

    s3 = ExitStack()
    w2x = sb("w2x", [128, 512], c=s3)
    a2x = sb("a2x", [128, 512], c=s3)
    g2s = sb("g2s", [128, 256], c=s3)
    w0r = sb("w0r", [1, 512], c=s3)
    lw = sb("lw", [128, 6, 512], c=s3)
    aT = sb("aT", [128, 4, 768], c=s3)
    kkT = sb("kkT", [128, 2, 768], c=s3)
    kd_ = sb("kd_", [128, 4, 768], c=s3)
    tmp = sb("tmp", [128, 768], c=s3)
    tmp2 = sb("tmp2", [128, 768], c=s3)
    yR = sb("yR", [128, 2, 512], c=s3)
    K.wait("sp", K.all())
    tw = [K.dma("sp", lambda e: e.dma_start(w2x[:, :], A["w2x"])), K.dma("sp", lambda e: e.dma_start(a2x[:, :], A["a2x"])),
          K.dma("sp", lambda e: e.dma_start(g2s[:, :], A["g2"])),
          K.dma("sp", lambda e: e.dma_start(w0r[:, :], A["rows"][0:1, RO["w0"][0]:RO["w0"][0] + 512]))]
    act(tmp[:, :], rwm[:, 6, :], ACT.Tanh)
    t_th = K.last("act")
    for b6 in range(6):
        b = bank()
        mm(b[:, :], C("ones")[0:1, :], w0r[0:1, :], *tw, start=True, stop=False)
        t = mm(b[:, :], tmp[:, b6 * 128:(b6 + 1) * 128], w2x[:, :], t_th, start=False, stop=True)
        t = act(lw[:, b6, :], b[:, :], ACT.Sigmoid, t)
        give(b, t)
    for q in range(4):
        for lo, n_ in ((0, 512), (512, 256)):
            b = bank()
            t = mm(b[:, 0:n_], a2x[:, q * 128:(q + 1) * 128], rwm[:, 7, lo:lo + n_], *tw)
            t = act(aT[:, q, lo:lo + n_], b[:, 0:n_], ACT.Sigmoid, t, bias=cc("a0", q))
            give(b, t)
    for p in range(2):
        ts(kkT[:, p, :], rwm[:, 2 + p, :], cc("kk", p), None, ALU.mult, None)
        t = act(tmp[:, :], kkT[:, p, :], ACT.Square, K.last("dve"), K.last("pe"))
        for lo, n_ in ((0, 512), (512, 256)):
            b = bank()
            t = mm(b[:, 0:n_], C("h64"), tmp[:, lo:lo + n_], K.last("act"))
            t = act(tmp2[:, lo:lo + n_], b[:, 0:n_], ACT.Sqrt, t, K.last("dve"))
            give(b, t)
        ts(tmp2[:, :], tmp2[:, :], 1e-12, None, ALU.max, None, t)
        recip(tmp2[:, :], tmp2[:, :])
        tt(kkT[:, p, :], kkT[:, p, :], tmp2[:, :], ALU.mult)
    for q in range(4):
        p = q % 2
        ts(kd_[:, q, :], aT[:, q, :], -1.0, cc("ka", p), ALU.add, ALU.mult, K.last("act"))
        stt(kd_[:, q, :], kd_[:, q, :], 1.0, rwm[:, 2 + p, :], ALU.add, ALU.mult)
        tt(aT[:, q, :], aT[:, q, :], kkT[:, p, :], ALU.mult)
    dump("kd_", kd_[:, :, :])
    dump("lw", lw[:, :, :])
    K.barrier()
    s4 = ExitStack()
    big, scr, over = ring.take(12288)
    for e in ("dve", "act", "pool"):
        K.wait(e, over)
    spare = uT[:, :, :].rearrange("p k t -> p (k t)")[:, 4096:6144]
    Hr = sb("Hr", [128, 2, 2, 64], c=s4)
    t_H0 = memset(Hr[:, :, :, :], 0.0, e="dve")

    def rw_buffers(d):
        s_ = scr[:, 6144 * d:6144 * d + 6144]
        B = {n: s_[:, 512 * j:512 * j + 512].rearrange("p (h t) -> p h t", h=4)
             for j, n in enumerate(("ATm", "Aof", "Tm", "TT", "Xm", "BTm", "Abt", "Akt"))}
        B["OPC"] = s_[:, 4096:5120].rearrange("p (a q t) -> p a q t", a=4, q=2)
        B["OPT"] = s_[:, 5120:6144].rearrange("p (a c) -> p a c", a=4)
        B["E3"] = spare[:, 768 * d:768 * d + 768].rearrange("p (q a t) -> p q a t", q=2, a=3)
        B["BV"] = spare[:, 1536 + 256 * d:1792 + 256 * d]
        for n, w in (("U0", 256), ("SA", 256), ("TK", 256), ("Dt", 4)):
            B[n] = sb(f"{n}{d}", [128, w], c=s4)
        return B

    def v4(x):
        return x.rearrange("p (h t) -> p h t", h=4)

    def hp(h):
        return slice(64 * (h % 2), 64 * (h % 2) + 64), h // 2

    RB = [rw_buffers(d) for d in range(2)]
    r_end = [[t_H0], [t_H0]]
    yseen = set()

    def rw_unit(d, b6):
        B = RB[d]
        ATm, Aof, Tm, TT, Xm, BTm, Abt, Akt, OPC, OPT, E3, BV = (
            B[n] for n in ("ATm", "Aof", "Tm", "TT", "Xm", "BTm", "Abt", "Akt", "OPC", "OPT", "E3", "BV"))
        U0, SA = B["U0"], B["SA"]
        TK = B["TK"][:, :].rearrange("p (q t) -> p q t", q=2)
        Dt = B["Dt"][:, :].rearrange("p (c q) -> p c q", c=2)
        tok = slice(b6 * 128, (b6 + 1) * 128)
        isx = b6 >= 2
        K.wait("dve", r_end[d])
        K.wait("act", r_end[d])
        bd_ = bank()
        for p in range(2):
            l = lw[:, b6, 256 * d + 128 * p:256 * d + 128 * p + 128]
            b = bank()
            mm(b[:, 0:128], l, C(f"i64_{d}"))
            t = mm(b[:, 128:256], l, C(f"e64_{d}"))
            t2 = mm(bd_[:, 2 * p:2 * p + 2], l, C("ch64"))
            act(E3[:, p, 0:2, :].rearrange("p a b -> p (a b)"), b[:, 0:256], ACT.Exp, t, scale=-E05)
            t = act(E3[:, p, 2, :], b[:, 0:128], ACT.Exp, scale=E05)
            give(b, t)
            t_e = t
        t_D = act(Dt.rearrange("p c q -> p q c"), bd_[:, 0:4].rearrange("p (q c) -> p q c", q=2), ACT.Exp, t2, scale=-E05)
        give(bd_, t_D)
        yield
        tt(OPC[:, 1, :, :], kkT[:, :, tok], E3[:, :, 1, :], ALU.mult, t_e)
        t_c = tt(OPC[:, 2, :, :], aT[:, 2 * d:2 * d + 2, tok], E3[:, :, 2, :], ALU.mult)
        t_k = tt(OPC[:, 3, :, :], kd_[:, 2 * d:2 * d + 2, tok], E3[:, :, 2, :], ALU.mult)
        if isx:
            t_r = tt(OPC[:, 0, :, :], rwm[:, 0:2, tok], E3[:, :, 0, :], ALU.mult)
        yield

        def prod(i, j, *toks):
            b = bank()
            for h in (0, 2, 1, 3):
                ps_, q = hp(h)
                t = mm(b[:, h * 128:(h + 1) * 128], OPC[ps_, i, q, :], OPC[ps_, j, q, :], *toks, after=h == 1)
            return b, t

        def masked(bt, msk, dst):
            t = tt(dst[:, :, :], v4(bt[0][:, :]), bcm(C(msk), 4), ALU.mult, bt[1])
            give(bt[0], t)
            return t
        p1, p2 = prod(1, 2, t_c), prod(2, 1)
        masked(p1, f"l0_{1 - d}", Tm)
        stt(Tm[:, :, :], Tm[:, :, :], -1.0, bcm(ident, 4), ALU.mult, ALU.add)
        masked(p2, f"e64_{d}", ATm)
        tt(TT[:, :, :], ATm[:, :, :], bcm(C(f"l0_{d}"), 4), ALU.mult)
        t_T = stt(TT[:, :, :], TT[:, :, :], -1.0, bcm(ident, 4), ALU.mult, ALU.add)
        yield

        def side():
            nonlocal t_t, t_bv, t_A
            for a in range(2):
                b = bank()
                for q in range(2):
                    for p in range(2):
                        k = 2 * a + q
                        src = rwm[:, 4 + p, tok] if k == 0 else OPC[:, k, p, :]
                        t = tr(b[:, q * 256 + p * 128:q * 256 + (p + 1) * 128], src, ident, t_k)
                if a == 0:
                    act(OPT[:, 0, :], b[:, 0:256], ACT.Copy, t)
                    t_t = act(OPT[:, 1, :], b[:, 256:512], ACT.Copy, scale=-1.0)
                else:
                    t_t = act(OPT[:, 2:4, :].rearrange("p a b -> p (a b)"), b[:, :], ACT.Copy, t)
                give(b, t_t)
                yield
            t_B = masked(prod(3, 1, t_k), f"e64_{d}", BTm)
            yield
            b = bank()
            for h in range(4):
                t = mm(b[:, 64 * h:64 * h + 64], BTm[:, h, :], OPT[:, 0, 64 * h:64 * h + 64], t_B, t_t)
            t_bv = act(BV[:, :], b[:, 0:256], ACT.Copy, t, scale=-1.0)
            give(b, t_bv)
            yield
            if isx:
                masked(prod(2, 0, t_r), f"i64_{d}", Abt)
                t_A = masked(prod(3, 0), f"i64_{d}", Akt)
            yield
        t_t = t_bv = t_A = None
        beside = side()
        t_m = None
        for k in range(1, 6):
            t_a = tt(Aof[:, :, :], ATm[:, :, :], bcm(C(f"l{k}_{d}"), 4), ALU.mult, t_m)
            b = bank()
            for h in range(4):
                t_m = mm(b[:, h * 128:(h + 1) * 128], Aof[:, h, :], Tm[:, h, :], t_a, t_T)
            t_X = act(Xm[:, :, :], v4(b[:, :]), ACT.Copy, t_m)
            give(b, t_X)
            next(beside)
            yield
            b2 = bank()
            for h in range(4):
                t2 = mm(b2[:, h * 128:(h + 1) * 128], Xm[:, h, :], TT[:, h, :], t_X)
            if k < 5:
                b = bank()
                for h in range(4):
                    t1 = mm(b[:, h * 128:(h + 1) * 128], TT[:, h, :], Xm[:, h, :])
                t = tt(Tm[:, :, :], Tm[:, :, :], v4(b[:, :]), ALU.subtract, t1)
                give(b, t)
            t_T = tt(TT[:, :, :], TT[:, :, :], v4(b2[:, :]), ALU.subtract, t2)
            give(b2, t_T)
            t_m = [t_m, t2]
            yield
        b = bank()
        for h in range(4):
            t = mm(b[:, 64 * h:64 * h + 64], TT[:, h, :], BV[:, 64 * h:64 * h + 64], t_T, t_bv)
        for h in range(4):
            ps_, q = hp(h)
            t = mm(b[ps_, 256 + q * 128:384 + q * 128], OPT[:, 1, 64 * h:64 * h + 64], TT[:, h, :], t_t)
        act(U0[:, :], b[:, 0:256], ACT.Copy, t)
        t_u0 = act(TK.rearrange("p a b -> p (a b)"), b[:, 256:512], ACT.Copy)
        give(b, t_u0)
        yield
        by = bank() if isx else None
        t_H, t_y = r_end[d][0], None
        for ch in ((0, 1) if d == 0 else (1, 0)):
            cs = slice(64 * ch, 64 * ch + 64)
            b = bank()
            for h in (0, 2, 1, 3):
                ps_, q = hp(h)
                t = mm(b[cs, 64 * h:64 * h + 64], TK[ps_, q, cs], Hr[ps_, d, q, :], t_H, t_u0, after=h == 1)
            t_sa = tt(SA[cs, :], b[cs, 0:256], U0[cs, :], ALU.add, t)
            give(b, t_sa)
            b = bank()
            for h in range(4):
                ps_, q = hp(h)
                o = b[ps_, q * 64:q * 64 + 64]
                mm(o, OPT[cs, 3, 64 * h:64 * h + 64], OPT[cs, 0, 64 * h:64 * h + 64], start=True, stop=False)
                t = mm(o, OPT[cs, 2, 64 * h:64 * h + 64], SA[cs, 64 * h:64 * h + 64], t_sa, start=False, stop=True)
            if isx:
                for h in range(4):
                    ps_, q = hp(h)
                    o = by[ps_, q * 128 + 64 * ch:q * 128 + 64 * ch + 64]
                    mm(o, Hr[ps_, d, q, :], OPC[ps_, 0, q, cs], start=True, stop=False, after=True)
                    mm(o, SA[cs, 64 * h:64 * h + 64], Abt[cs, h, cs], t_sa, t_A, start=False, stop=False, after=True)
                    t_y = mm(o, OPT[cs, 0, 64 * h:64 * h + 64], Akt[cs, h, cs], start=False, stop=True)
            t = tt(Hr[:, d, :, :], Hr[:, d, :, :], b[:, 0:128].rearrange("p (q v) -> p q v", q=2), ALU.add, t, t_y, t_D)
            give(b, t)
            t_H = tt(Hr[:, d, :, :], Hr[:, d, :, :], bc(Dt[:, ch, :], 64), ALU.mult)
            yield
        r_end[d] = [t_H, t, t_y]
        if isx:
            o = yR[:, :, (b6 - 2) * 128:(b6 - 1) * 128]
            src = by[:, 0:256].rearrange("p (q t) -> p q t", q=2)
            t = tt(o, o, src, ALU.add, t_y) if b6 in yseen else copy(o, src, t_y)
            yseen.add(b6)
            give(by, t)

    def rw_strand(d):
        for b6 in ORD[d]:
            yield from rw_unit(d, b6)

    run(rw_strand(0), rw_strand(1))
    K.barrier()
    big[2] = K.all()
    s4.close()
    dump("yR", yR[:, :, :])
    t5 = tmp[:, 0:512]
    t6 = tmp2[:, 0:512]
    X = slice(256, 768)
    for p in range(2):
        y = yR[:, p, :]
        b = bank()
        t = mm(b[:, :], C("h64"), y, K.last("dve"))
        t = stt(y, b[:, :], -1.0 / 64, y, ALU.mult, ALU.add, t)
        give(b, t)
        t = act(t5, y, ACT.Square, t, K.last("pe"))
        b = bank()
        t = mm(b[:, :], C("h64"), t5, t)
        t = act(t6, b[:, :], ACT.Sqrt, t, bias=EPS64, scale=1.0 / 64)
        give(b, t)
        recip(t6, t6, t)
        tt(y, y, t6, ALU.mult)
        ts(y, y, cc("lnw", p), cc("lnb", p), ALU.mult, ALU.add)
        tt(t6, kd_[:, p, X], kd_[:, 2 + p, X], ALU.add)
        stt(t5, rwm[:, p, X], cc("rk", p), t6, ALU.mult, ALU.mult, K.last("pe"))
        b = bank()
        t = mm(b[:, :], C("h64"), t5, K.last("dve"))
        t = tt(t6, b[:, :], rwm[:, 4 + p, X], ALU.mult, t)
        give(b, t)
        tt(y, y, t6, ALU.add)
        if p == 0:
            t_s = act(aT[:, 0, 0:512], rwm[:, 8, X], ACT.Sigmoid, K.last("dve"))
        b = bank()
        t = mm(b[:, :], g2s[:, p * 128:(p + 1) * 128], aT[:, 0, 0:512], t_s)
        t = tt(ym[:, 4 + p, :], y, b[:, :], ALU.mult, t)
        give(b, t)
    dump("ym", ym[:, :, :])
    K.barrier()
    s3.close()
    m1.close()
    g12 = sb("g12", [128, 4, D])
    with ExitStack() as s0:
        mrow = sb("mrow2", [2, D], c=s0)
        brow = sb("brow2", [1, D], c=s0)
        for s in (2, 3, 4, 5):
            run(ada(s, mrow, brow, g12))
        K.barrier()

    m2 = ExitStack()
    hD = nc.dram_tensor("h_rows", (512, D), F32, kind="Internal").ap()
    yD = nc.dram_tensor("y_rows", (4096, D), F32, kind="Internal").ap()
    t_hds = []
    hT = sb("hT", [128, 8, 512], c=m2)
    w8 = sb("w8", [128, 4, 8], c=m2)
    msk = sb("msk", [128, 4, 64], c=m2)
    idx = sb("idx", [128, 96, 2], I32, c=m2)
    ovi = sb("ovi", [1, 33], I32, c=m2)
    fac = sb("fac", [128, 4, D], c=m2)
    wtok = sb("wtok", [128, 4, 64], c=m2)
    m3 = ExitStack()
    lnr = sb("lnr", [128, 4, D], c=m3)
    xn = sb("xn2", [128, 2, D], c=m3)
    rwt = sb("rwt", [128, 8, 64], c=m3)
    rb = sb("rb", [128, 64], c=m3)
    sel = sb("sel", [128, 64], c=m3)
    sco = sb("sco", [128, 64], c=m3)
    m8 = sb("m8", [128, 8, 8], c=m3)
    gs = sb("gs", [128, 32], c=m3)
    K.wait("sp", K.all())
    tl = [rowload(lnr[:, 0, :], "ln1w"), rowload(lnr[:, 1, :], "ln1b"),
          K.dma("sp", lambda e: e.dma_start(rwt[:, :, :], A["router_w"].rearrange("(k p) n -> p k n", p=128))),
          rowload(rb[:, :], "rb")]

    def out_proj(W, i, src, dst_fn):
        pass

    ents = []
    for hf in range(2):
        ent, wap, tk = ring.load([(0, 4096, 8, A["w_out"][:, hf * 512:(hf + 1) * 512].rearrange("(k p) n -> p k n", p=128))], 4096)
        wv = wap.rearrange("p (k n) -> p k n", k=8)
        for i in range(4):
            b = bank()
            for k in range(8):
                t = mm(b[:, :], ym[:, k, i * 128:(i + 1) * 128], wv[:, k, :], tk, start=(k == 0), stop=(k == 7))
            hs = slice(hf * 512, (hf + 1) * 512)
            tmpv = xn[:, 0, hs]
            t = tt(tmpv, b[:, :], g12[:, 0, hs], ALU.mult, t)
            give(b, t)
            stt(xt[:, i, hs], xt[:, i, hs], ALPHA, tmpv, ALU.mult, ALU.add)
        ent[2] = K.last("pe")

    def layer_norm(x, w, bb, *toks):
        ln_stats(x, *toks)
        ts(x, x, mv[:, 0:1], rstd[:, 0:1], ALU.subtract, ALU.mult)
        tt(x, x, w, ALU.mult, *toks)
        return tt(x, x, bb, ALU.add)

    xnt = [None, None]
    for i in range(4):
        layer_norm(xt[:, i, :], lnr[:, 0, :], lnr[:, 1, :], *tl)
        ln_stats(xt[:, i, :])
        ts(xn[:, i % 2, :], xt[:, i, :], mv[:, 0:1], rstd[:, 0:1], ALU.subtract, ALU.mult, xnt[i % 2])
        tt(xn[:, i % 2, :], xn[:, i % 2, :], g12[:, 3, :], ALU.mult)
        tn = tt(xn[:, i % 2, :], xn[:, i % 2, :], g12[:, 2, :], ALU.add)
        t_hd = K.dma("sp", lambda e, i=i, xn=xn: e.dma_start(hD[i * 128:(i + 1) * 128, :], xn[:, i % 2, :]), tn)
        t_hds.append(t_hd)
        for hf in range(2):
            b = bank()
            for k in range(4):
                t = tr(b[:, k * 128:(k + 1) * 128], xn[:, i % 2, (hf * 4 + k) * 128:(hf * 4 + k + 1) * 128], ident, tn)
            xnt[i % 2] = [t, t_hd]
            t2 = act(hT[:, hf * 4:hf * 4 + 4, i * 128:(i + 1) * 128], v4(b[:, :]), ACT.Copy, t)
            give(b, t2)
    t_h = K.last("act")
    dump("x1", xt[:, :, :])
    dump("hT", hT[:, :, :])
    for i in range(4):
        b = bank()
        for k in range(8):
            t = mm(b[:, 0:64], hT[:, k, i * 128:(i + 1) * 128], rwt[:, k, :], t_h, *tl, start=(k == 0), stop=(k == 7))
        t = act(sco[:, :], b[:, 0:64], ACT.Sigmoid, t, K.last("dve"))
        give(b, t)
        tt(sel[:, :], sco[:, :], rb[:, :], ALU.add, t, *tl)
        for g in range(8):
            max8(m8[:, g, :], sel[:, 8 * g:8 * g + 8])
        tt(gs[:, 0:8], m8[:, :, 0], m8[:, :, 1], ALU.add)
        max8(gs[:, 8:16], gs[:, 0:8])
        ts(gs[:, 16:24], gs[:, 0:8], gs[:, 11:12], None, ALU.is_ge, None)
        ts(gs[:, 24:32], gs[:, 16:24], -1.0, 1e30, ALU.add, ALU.mult)
        s3_ = sel[:, :].rearrange("p (g e) -> p g e", g=8)
        tt(s3_, s3_, bc(gs[:, 16:24], 8), ALU.mult)
        tt(s3_, s3_, bc(gs[:, 24:32], 8), ALU.add)
        max8(gs[:, 8:16], sel[:, :])
        strike(sel[:, :], gs[:, 8:16], sel[:, :])
        ts(msk[:, i, :], sel[:, :], -2e38, None, ALU.is_lt, None)
        tt(sel[:, :], msk[:, i, :], sco[:, :], ALU.mult)
        red(gs[:, 0:1], sel[:, :], ALU.add)
        recip(gs[:, 1:2], gs[:, 0:1])
        ts(wtok[:, i, :], sel[:, :], gs[:, 1:2], 2.5, ALU.mult, ALU.mult)
    dump("wtok", wtok[:, :, :])
    K.barrier()
    for e in K.sem:
        K.wait(e, t_hds)
    m3.close()

    BIG = 1048576.0
    m4 = ExitStack()
    BF = mybir.dt.bfloat16
    rk = sb("rk", [128, 4, 96], c=m4)
    jr = sb("jr", [128, 4, 64], c=m4)
    val = sb("val", [128, 4, 96, 4], BF, c=m4)
    eT = sb("eT", [64, 2, 512], c=m4)
    ot = sb("ot", [64, 3, 32], c=m4)
    nb = sb("nb", [64, 8], c=m4)
    Pm = sb("Pm", [128, 3, 4, 128], BF, c=m4)
    ixf = sb("ixf", [128, 96, 2], c=m4)
    j8 = sb("j8", [128, 8, 64], c=m4)
    iota = C("iota")
    b = bank()
    for i in range(4):
        for i2 in range(i):
            mm(b[:, 64 * i:64 * i + 64], C("ones"), msk[:, i2, :], K.last("dve"), start=(i2 == 0), stop=False)
        t = mm(b[:, 64 * i:64 * i + 64], C("g128_1"), msk[:, i, :], K.last("dve"), start=(i == 0), stop=True)
    mf = msk[:, :, :]
    ts(rk[:, :, 0:64], mf, -BIG, BIG, ALU.mult, ALU.add)
    t = tt(rk[:, :, 0:64], rk[:, :, 0:64], b[:, 0:256].rearrange("p (i e) -> p i e", i=4), ALU.add, t)
    give(b, t)
    for i in range(4):
        op("dve", lambda g, i=i: g.tensor_tensor_scan(jr[:, i, :], C("one8"), msk[:, i, :], 0.0, ALU.mult, ALU.add))
    tt(jr[:, :, :], jr[:, :, :], mf, ALU.subtract)
    for i in range(4):
        tt(j8[:, :, :], bcm(jr[:, i, :], 8), bc(iota[:, 0:8], 64), ALU.is_equal)
        tt(j8[:, :, :], j8[:, :, :], bcm(wtok[:, i, :], 8), ALU.mult)
        red(w8[:, i, :], j8[:, :, :], ALU.add)
    b = bank()
    for i in range(4):
        t = mm(b[0:64, 0:1], msk[:, i, :], C("ones")[:, 0:1], start=(i == 0), stop=(i == 3))
    ts(nb[:, 0:1], b[0:64, 0:1], 128.5, None, ALU.is_gt, None, t)
    ts(nb[:, 1:2], b[0:64, 0:1], 256.5, None, ALU.is_gt, None)
    t = ts(nb[:, 2:3], b[0:64, 0:1], 384.5, None, ALU.is_gt, None)
    give(b, t)
    tt(nb[:, 3:4], nb[:, 0:1], nb[:, 1:2], ALU.add)
    t = tt(nb[:, 3:4], nb[:, 3:4], nb[:, 2:3], ALU.add)
    b = bank()
    t = mm(b[0:64, 0:1], C("tri64")[0:64, :], nb[:, 3:4], t)
    t = copy(nb[:, 4:5], b[0:64, 0:1], t)
    give(b, t)
    tt(nb[:, 5:6], nb[:, 4:5], nb[:, 3:4], ALU.add)
    O = ot[:, 0, :]
    i32_ = iota[0:64, 0:32]
    ts(O, i32_, nb[:, 4:5], None, ALU.is_ge, None)
    ts(ot[:, 1, :], i32_, nb[:, 5:6], None, ALU.is_lt, None)
    tt(O, O, ot[:, 1, :], ALU.mult)
    ts(ot[:, 1, :], i32_, nb[:, 4:5], 1.0, ALU.subtract, ALU.add)
    stt(ot[:, 1, :], ot[:, 1, :], -128.0, O, ALU.mult, ALU.mult)
    t_O = K.last("dve")
    b = bank()
    mm(b[0:1, 0:32], C("ii")[0:64, :], O, t_O)
    t = mm(b[0:1, 32:33], nb[:, 3:4], C("ones")[0:64, 0:1])
    t_ov = copy(ovi[0:1, :], b[0:1, 0:33], t)
    give(b, t_ov)
    for q, src in enumerate((rk[:, :, 0:64], jr[:, :, :])):
        b = bank()
        for i in range(4):
            t = tr(b[0:64, i * 128:(i + 1) * 128], src[:, i, :], ident, t_O)
        t = copy(eT[:, q, :], b[0:64, :], t, e="act")
        give(b, t)
    b = bank()
    for i in range(4):
        mm(b[:, 32 * i:32 * i + 32], eT[:, 0, i * 128:(i + 1) * 128], O, t, start=True, stop=False)
        t1 = mm(b[:, 32 * i:32 * i + 32], C("ones")[0:64, :], ot[:, 1, :], start=False, stop=True)
    for i in range(4):
        t2 = mm(b[:, 128 + 32 * i:160 + 32 * i], eT[:, 1, i * 128:(i + 1) * 128], O)
    copy(rk[:, :, 64:96], b[:, 0:128].rearrange("p (i e) -> p i e", i=4), t2)
    copy(val[:, :, 64:96, 2], b[:, 128:256].rearrange("p (i e) -> p i e", i=4))
    copy(val[:, :, 0:64, 2], jr[:, :, :])
    t = K.last("dve")
    give(b, t)
    memset(val[:, :, :, 3], 1.0, e="dve")
    for i in range(4):
        memset(val[:, i, :, 0], float(i), e="dve")
        ts(val[:, i, :, 1], iota[:, 0:96], 0.0, C("ii"), ALU.mult, ALU.add)
    t_val = K.last("dve")
    bi_ = bank()
    pmr = [None] * 3
    pmt = [None] * 96
    for n_ in range(96):
        t = tt(Pm[:, n_ % 3, :, :], bcm(iota, 4), bc(rk[:, :, n_], 128), ALU.is_equal, pmr[n_ % 3])
        for i in range(4):
            t = mm(bi_[:, 4 * n_:4 * n_ + 4], Pm[:, n_ % 3, i, :], val[:, i, n_, :], t, t_val, start=(i == 0), stop=(i == 3))
        pmr[n_ % 3] = t
    R4 = bi_[:, 0:384].rearrange("p (b c) -> p b c", c=4)
    off = sb("off", [128, 96], c=m4)
    cvi = sb("cvi", [128, 96, 4], c=m4)
    t = copy(cvi[:, :, :], R4, t)
    give(bi_, t)
    ts(off[:, :], cvi[:, :, 3], -BIG, BIG, ALU.mult, ALU.add)
    stt(ixf[:, :, 0], cvi[:, :, 0], 128.0, cvi[:, :, 1], ALU.mult, ALU.add)
    stt(ixf[:, :, 1], ixf[:, :, 0], 8.0, cvi[:, :, 2], ALU.mult, ALU.add)
    tt(ixf[:, :, :], ixf[:, :, :], bc(off[:, :], 2), ALU.add)
    t_ix = copy(idx[:, :, :], ixf[:, :, :])
    dump("idx", ixf[:, :, :])
    K.barrier()
    m4.close()

    m4 = ExitStack()
    hid = sb("hid", [128, 2, 512], c=m4)
    gsl = sb("gsl", [128, 2, 512], c=m4)
    hg = sb("hg", [128, 3, D], c=m4)
    hgT = sb("hgT", [128, 2, 8, 128], c=m4)
    hd2 = sb("hd2", [128, 2, 256], c=m4)
    hdT = sb("hdT", [128, 2, 2, 128], c=m4)
    sl = sb("sl", [128, 2, 256], c=m4)
    yb = sb("yb", [128, 3, D], c=m4)
    t_hg = memset(hg[:, :, :], 0.0)
    K.wait("pool", t_hds, t_ix, t_hg)

    def block(n_, load_w, st):
        g3, g2 = n_ % 3, n_ % 2
        t_g = K.dma("pool", lambda e: e.indirect_dma_start(
            out=hg[:, g3, :], out_offset=None, in_=hD, in_offset=bass.IndirectOffsetOnAxis(ap=idx[:, n_, 0:1], axis=0),
            bounds_check=511, oob_is_err=False), st["hg"][g3])
        yield
        for q in range(2):
            b = bank()
            for k in range(4):
                t = tr(b[:, k * 128:(k + 1) * 128], hg[:, g3, (q * 4 + k) * 128:(q * 4 + k + 1) * 128], ident, t_g, t_hg)
            t2 = copy(hgT[:, g2, 4 * q:4 * q + 4, :], v4(b[:, :]), t, st["hgT"][g2], e="act" if q else "dve")
            if q == 0:
                ta = t2
            give(b, t2)
        st["hg"][g3] = t
        yield
        e1, wa, tk1 = load_w(0, 4096)
        wv = wa.rearrange("p (k n) -> p k n", k=8)
        b = bank()
        for k in range(8):
            t = mm(b[:, :], hgT[:, g2, k, :], wv[:, k, :], ta, t2, tk1, start=(k == 0), stop=(k == 7))
        e1[2] = t
        st["hgT"][g2] = t
        t3 = act(sl[:, g2, :], b[:, 0:256], ACT.Silu, t, st["sl"][g2])
        t4 = tt(hd2[:, g2, :], sl[:, g2, :], b[:, 256:512], ALU.mult, t3, st["hd2"][g2])
        st["sl"][g2] = t4
        give(b, t4)
        yield
        b = bank()
        for q in range(2):
            t = tr(b[:, q * 128:(q + 1) * 128], hd2[:, g2, q * 128:(q + 1) * 128], ident, t4)
        st["hd2"][g2] = t
        t = act(hdT[:, g2, :, :], b[:, 0:256].rearrange("p (q s) -> p q s", q=2), ACT.Copy, t, st["hdT"][g2])
        give(b, t)
        yield
        e2, wb, tk2 = load_w(4096, 2048)
        w2 = wb.rearrange("p (k n) -> p k n", k=2)
        te = []
        for q in range(2):
            b = bank()
            for k in range(2):
                t5 = mm(b[:, :], hdT[:, g2, k, :], w2[:, k, q * 512:(q + 1) * 512], t, tk2, start=(k == 0), stop=(k == 1))
            t6 = copy(yb[:, g3, q * 512:(q + 1) * 512], b[:, :], t5, st["yb"][g3], e="act" if q else "dve")
            te.append(t6)
            give(b, t6)
        e2[2] = t5
        st["hdT"][g2] = t5
        t_s = K.dma("pool", lambda e: e.indirect_dma_start(
            out=yD, out_offset=bass.IndirectOffsetOnAxis(ap=idx[:, n_, 1:2], axis=0), in_=yb[:, g3, :], in_offset=None,
            bounds_check=4095, oob_is_err=False), *te)
        st["yb"][g3] = t_s
        st["all"].append(t_s)
        yield

    def fresh():
        return {"hg": [None] * 3, "hgT": [None] * 2, "sl": [None] * 2, "hd2": [None] * 2, "hdT": [None] * 2,
                "yb": [None] * 3, "all": []}

    def static_w(e):
        return lambda lo, n: ring.load([(0, n, 0, A["ew"][e][:, lo:lo + n])], n)

    st = fresh()
    live = []
    for n_ in range(64 + 4):
        for g in list(live):
            if next(g, "end") == "end":
                live.remove(g)
        if n_ < 64:
            g = block(n_, static_w(n_), st)
            next(g)
            live.append(g)
    for g in live:
        for _ in g:
            pass
    ent, wap, tk = ring.load([(0, 6144, 0, A["sw"])], 6144)
    wv = wap[:, 0:4096].rearrange("p (k n) -> p k n", k=8)
    w2 = wap[:, 4096:6144].rearrange("p (k n) -> p k n", k=2)
    for f in range(2):
        b = bank()
        for k in range(8):
            t = mm(b[:, :], wv[:, k, f * 128:(f + 1) * 128], hT[:, k, :], tk, t_h, start=(k == 0), stop=(k == 7))
        b2 = bank()
        for k in range(8):
            t2 = mm(b2[:, :], wv[:, k, 256 + f * 128:384 + f * 128], hT[:, k, :], start=(k == 0), stop=(k == 7))
        t = act(gsl[:, f, :], b[:, :], ACT.Silu, t)
        give(b, t)
        t = tt(hid[:, f, :], gsl[:, f, :], b2[:, :], ALU.mult, t, t2)
        give(b2, t)
    t_h2 = t
    for i in range(4):
        for n_ in range(2):
            b = bank()
            for f in range(2):
                t = mm(b[:, :], hid[:, f, i * 128:(i + 1) * 128], w2[:, f, n_ * 512:(n_ + 1) * 512], t_h2, start=(f == 0), stop=(f == 1))
            t = copy(fac[:, i, n_ * 512:(n_ + 1) * 512], b[:, :], t, e="act")
            give(b, t)
    ent[2] = K.last("pe")
    K.barrier(("pe", "act", "dve", "pool", "sp"))
    for e in K.q:
        K.wait(e, t_ov, st["all"])
    nreg = {}

    def load_n(e):
        def f(eng):
            nreg[e] = eng.alloc_register("over_" + e)
            eng.reg_load(nreg[e], ovi[0:1, 32:33])
        K.q[e].append(f)
    for e in K.q:
        load_n(e)
    ent, scr, over = ring.take(6144)
    K.wait("sp", over)
    mfree = free[:]
    for i in range(32):
        K.part("ov")
        free[:] = [(b, None) for b in banks]

        def dyn_w(lo, n, i=i, scr=scr):
            def f(eng):
                v = eng.value_load(ovi[0:1, i:i + 1], min_val=0, max_val=63)
                return eng.dma_start(scr[:, lo:lo + n], A["ew"][bass.ds(v, 1), :, lo:lo + n].rearrange("o p n -> p (o n)"))
            return [0, 0, None], scr[:, lo:lo + n], [K.dma("sp", f)]
        so = fresh()
        for _ in block(64 + i, dyn_w, so):
            pass
        for e in K.q:
            K.wait(e, K.all(), so["all"])
        K.part_end(lambda e, eng, i=i: eng.If_cmp(nreg[e], i, "IS_GT"))
    free[:] = mfree
    ent[2] = K.all()
    K.barrier()
    m4.close()
    m4 = ExitStack()
    yr = sb("yr", [128, 2, 4, D], c=m4)
    yv = yD.rearrange("(i p j) d -> i p j d", p=128, j=8)
    yt = [None, None]
    for i in range(4):
        for q in range(2):
            t = K.dma("sp", lambda e, i=i, q=q: e.dma_start(yr[:, q, :, :], yv[i, :, 4 * q:4 * q + 4, :]), yt[q])
            for j in range(4):
                t2 = stt(fac[:, i, :], yr[:, q, j, :], w8[:, i, 4 * q + j:4 * q + j + 1], fac[:, i, :], ALU.mult, ALU.add, t)
            yt[q] = t2
    dump("fac", fac[:, :, :])
    K.barrier()
    m4.close()
    m5 = ExitStack()
    lnr = sb("lnr2", [128, 2, D], c=m5)
    tl = [rowload(lnr[:, 0, :], "ln2w", K.all()), rowload(lnr[:, 1, :], "ln2b", K.all())]
    for i in range(4):
        tt(fac[:, i, :], fac[:, i, :], g12[:, 1, :], ALU.mult)
        stt(xt[:, i, :], xt[:, i, :], ALPHA, fac[:, i, :], ALU.mult, ALU.add)
        layer_norm(xt[:, i, :], lnr[:, 0, :], lnr[:, 1, :], *tl)
    dump("x2", xt[:, :, :])
    K.barrier()
    m5.close()
    m2.close()

    m6 = ExitStack()
    hT = sb("hT2", [128, 8, 512], c=m6)
    xn = g12[:, 1, :]
    rope = g12[:, 2:4, :].rearrange("p a (b n) -> p (a b) n", b=2)
    t_rope = K.dma("sp", lambda e: e.dma_start(rope[:, :, :], A["rope"]), K.all())
    lamr = sb("lamr", [128, 512], c=m6)
    lms = sb("lms", [128, 8], c=m6)
    t_lam = rowload(lamr[:, :], "lam", K.all())
    gfr = g12[:, 0, :]
    t_gf = rowload(gfr, "gfin", K.all())
    gsc = sb("gsc", [128, 2], c=m6)
    for l in range(2):
        t = ts(gsc[:, l:l + 1], cc("g_sub", l), 1.0 - (0.8 - 0.6 * float(np.exp(-0.3 * l))), None, ALU.mult, None)
    K.wait("act", t)
    for l in range(2):
        for q in range(2):
            a = lamr[:, l * 256 + q * 128:l * 256 + q * 128 + 64]
            b_ = lamr[:, l * 256 + q * 128 + 64:l * 256 + q * 128 + 128]
            tt(a, a, b_, ALU.mult, t_lam)
            red(lms[:, 2 * q:2 * q + 1], a, ALU.add)
        act(lms[:, 4:5], lms[:, 0:1], ACT.Exp, K.last("dve"))
        act(lms[:, 5:6], lms[:, 2:3], ACT.Exp)
        li = 0.8 - 0.6 * float(np.exp(-0.3 * l))
        tt(lms[:, 6 + l:7 + l], lms[:, 5:6], lms[:, 4:5], ALU.subtract, K.last("act"))
        ts(lms[:, 6 + l:7 + l], lms[:, 6 + l:7 + l], -li, None, ALU.add, None)

    def rms_rows(x, *toks):
        act(xn, x, ACT.Square, K.last("dve"), K.last("pe"), *toks, accum=mv[:, 0:1])
        act(rstd[:, 1:2], mv[:, 0:1], ACT.Sqrt, bias=EPS6, scale=1.0 / D)
        return recip(rstd[:, 0:1], rstd[:, 1:2], K.last("act"))

    def rms_T(gname, l):
        for i in range(4):
            rms_rows(xt[:, i, :])
            tn = ts(xn, xt[:, i, :], rstd[:, 0:1], None, ALU.mult, None, K.last("pe"))
            for hf in range(2):
                b = bank()
                for k in range(4):
                    t = tr(b[:, k * 128:(k + 1) * 128], xn[:, (hf * 4 + k) * 128:(hf * 4 + k + 1) * 128], ident, tn)
                for k in range(4):
                    kk = hf * 4 + k
                    t2 = act(hT[:, kk, i * 128:(i + 1) * 128], b[:, k * 128:(k + 1) * 128], ACT.Copy, t,
                             scale=cc(gname, l * 8 + kk))
                give(b, t2)
        return K.last("act")

    for l in range(2):
        t_h = rms_T("g_mix", l)
        at = ExitStack()
        qT = sb(f"qT{l}", [128, 16, 512], c=at)
        iT = sb(f"iT{l}", [128, 3, 512], c=at)
        vt = sb(f"vt{l}", [128, 4, 1024], c=at)
        iw = sb(f"iw{l}", [128, 4, 8], c=at)
        r1 = sb(f"r1{l}", [128, 2, 512], c=at)
        r2 = sb(f"r2{l}", [128, 2, 512], c=at)
        W2 = A["w_in_2"][l]

        def wl2(c0, n_):
            ent, wap, tk = ring.load([(0, 8 * n_, 8, W2[:, c0:c0 + n_].rearrange("(k p) n -> p k n", p=128))], 8 * n_)
            return ent, wap.rearrange("p (k n) -> p k n", k=8), tk

        rr = [None, None]
        n_ = 0
        for c0, w in ((0, 512), (512, 512), (1024, 512), (1536, 512), (2048, 384)):
            ent, wv, tk = wl2(c0, w)
            for j in range(w // 128):
                dst = qT[:, n_, :] if n_ < 16 else iT[:, n_ - 16, :]
                ct, sn, swp = (rope[:, 0, :], rope[:, 1, :], "sw64") if n_ < 16 else (rope[:, 2, :], rope[:, 3, :], "sw32")
                b = bank()
                for k in range(8):
                    t = mm(b[:, :], wv[:, k, j * 128:(j + 1) * 128], hT[:, k, :], t_h, tk, start=(k == 0), stop=(k == 7))
                r = r1[:, n_ % 2, :]
                t = act(r, b[:, :], ACT.Copy, t, rr[n_ % 2])
                give(b, t)
                b = bank()
                t2 = mm(b[:, :], C(swp), r, t)
                tt(dst, r, ct, ALU.mult, t, t_rope)
                rr2 = r2[:, n_ % 2, :]
                t3 = tt(rr2, b[:, :], sn, ALU.mult, t2)
                give(b, t3)
                rr[n_ % 2] = [t2, t3]
                tt(dst, dst, rr2, ALU.add)
                n_ += 1
            ent[2] = K.last("pe")
        for q in range(2):
            ent, wv, tk = wl2(2432 + 512 * q, 512)
            for i in range(4):
                b = bank()
                for k in range(8):
                    t = mm(b[:, :], hT[:, k, i * 128:(i + 1) * 128], wv[:, k, :], tk, start=(k == 0), stop=(k == 7))
                t = act(vt[:, i, q * 512:(q + 1) * 512], b[:, :], ACT.Copy, t)
                give(b, t)
            ent[2] = K.last("pe")
        ent, wv, tk = wl2(3456, 8)
        b = bank()
        for i in range(4):
            for k in range(8):
                t = mm(b[:, 8 * i:8 * i + 8], hT[:, k, i * 128:(i + 1) * 128], wv[:, k, :], tk, start=(k == 0), stop=(k == 7))
        t = ts(iw[:, :, :].rearrange("p a b -> p (a b)"), b[:, 0:32], float(32 ** -0.5 * 8 ** -0.5), None, ALU.mult, None, t)
        give(b, t)
        ent[2] = K.last("pe")
        dump(f"qT{l}", qT[:, :, :])

        NW = 3
        spare = uT[:, :, :].rearrange("p k t -> p (k t)")[:, 4096:6144]
        sc, wk, zb = (spare[:, 512 * j:512 * j + 512] for j in range(3))
        big, scr, over = ring.take(4096 * NW // 2)
        for e in ("dve", "act", "pool"):
            K.wait(e, over)
        P = scr[:, 0:1024 * NW].rearrange("p (w a b) -> p w a b", w=NW, a=2)
        PT = scr[:, 1024 * NW:2048 * NW].rearrange("p (w a b c) -> p w a b c", w=NW, a=2, b=4)
        bi, ob = hT[:, 0:4, :], hT[:, 4:8, :]
        m8b = sb(f"m8b{l}", [128, 8], c=at)
        st = sb(f"st{l}", [128, NW, 8], c=at)
        nrm = sb(f"nrm{l}", [128, 2, 16], c=at)
        K.barrier()
        memset(zb[:, :], 0.0, e="dve")
        t_zb = memset(zb[0:64, 448:512], -1e30, e="dve")
        btok = [t_zb, None, None, None]

        def indexer():
            for i in range(1, 4):
                qs = slice(i * 128, (i + 1) * 128)
                ns = 128 * (i + 1)
                S_, W_, B_ = sc[:, 0:ns], wk[:, 0:ns], bi[:, i, 0:ns]
                tr1 = [None, None]
                for h in range(8):
                    hs = slice(32 * (h % 4), 32 * (h % 4) + 32)
                    b = bank()
                    t = mm(b[:, 0:ns], iT[hs, h // 4, qs], iT[hs, 2, 0:ns])
                    t2 = act(r1[:, h % 2, 0:ns], b[:, 0:ns], ACT.Relu, t, tr1[h % 2])
                    give(b, t2)
                    yield
                    if h == 0:
                        tr1[0] = ts(S_, r1[:, 0, 0:ns], iw[:, i, 0:1], None, ALU.mult, None, t2)
                    else:
                        tr1[h % 2] = stt(S_, r1[:, h % 2, 0:ns], iw[:, i, h:h + 1], S_, ALU.mult, ALU.add, t2)
                memset(sc[0:64, ns - 64:ns], -1e30, e="dve")
                src = S_
                for r in range(16):
                    max8(m8b[:, :], src)
                    strike(W_, m8b[:, :], src)
                    src = W_
                    if r % 2:
                        yield
                ts(B_, W_, -2e38, -1.0, ALU.is_lt, ALU.add)
                ts(B_, B_, 1e30, None, ALU.mult, None)
                btok[i] = memset(bi[0:64, i, ns - 64:ns], -1e30, e="dve")
                yield

        ptr_ = [[None, None] for _ in range(NW)]

        def unit(w, i, h, diff):
            qs = slice(i * 128, (i + 1) * 128)
            ns = 128 * (i + 1)
            if diff or i == 0:
                bias, t_b = zb[:, 512 - ns:512], t_zb
            else:
                while btok[i] is None:
                    yield
                bias, t_b = bi[:, i, 0:ns], btok[i]
            o = 8 if diff else 0
            tq = []
            for c in range(2):
                ps_ = slice(64 * c, 64 * c + 64)
                b = bank()
                t = mm(b[:, 0:ns], qT[ps_, o + h, qs], qT[ps_, o + 4 + h, 0:ns])
                tq.append((b, t))
            yield
            s_ = st[:, w, :]
            te = []
            for c in range(2):
                b, t = tq[c]
                t = ttr(P[:, w, c, 0:ns], b[:, 0:ns], bias, 0.125, -3e38, ALU.add, ALU.max, s_[:, c:c + 1], t, t_b, ptr_[w][c])
                give(b, t)
            t = ts(s_[:, 2:4], s_[:, 0:2], -1.0, None, ALU.mult, None)
            for c in range(2):
                t2 = act(P[:, w, c, 0:ns], P[:, w, c, 0:ns], ACT.Exp, t, bias=s_[:, 2 + c:3 + c], accum=s_[:, 4 + c:5 + c])
            yield
            recip(s_[:, 6:8], s_[:, 4:6], t2)
            if diff:
                tt(s_[:, 7:8], s_[:, 7:8], lms[:, 6 + l:7 + l], ALU.mult)
                ts(P[:, w, 0, 0:ns], P[:, w, 0, 0:ns], s_[:, 6:7], None, ALU.mult, None)
                t = stt(P[:, w, 0, 0:ns], P[:, w, 1, 0:ns], s_[:, 7:8], P[:, w, 0, 0:ns], ALU.mult, ALU.add)
            else:
                for c in range(2):
                    t = ts(P[:, w, c, 0:ns], P[:, w, c, 0:ns], s_[:, 6 + c:7 + c], None, ALU.mult, None)
            yield
            tq = []
            for c in range(1 if diff else 2):
                b = bank()
                for j in range(i + 1):
                    t2 = tr(b[:, j * 128:(j + 1) * 128], P[:, w, c, j * 128:(j + 1) * 128], ident, t)
                ptr_[w][c] = t2
                tq.append((b, t2))
            yield
            tp = []
            for c, (b, t2) in enumerate(tq):
                t = copy(PT[:, w, c, 0:i + 1, :].rearrange("p a b -> p (a b)"), b[:, 0:ns], t2, ptv[w][c], e="act")
                give(b, t)
                tp.append(t)
            yield
            bo = bank()
            if diff:
                for j in range(i + 1):
                    t = mm(bo[:, 0:128], PT[:, w, 0, j, :], vt[:, j, 512 + 128 * h:640 + 128 * h], tp[0], start=(j == 0), stop=(j == i))
                ptv[w][0] = t
                yield
                t = act(ob[:, i, 128 * h:128 * h + 128], bo[:, 0:128], ACT.Copy, t)
            else:
                for c in range(2):
                    ps_ = slice(64 * c, 64 * c + 64)
                    for j in range(i + 1):
                        t = mm(bo[ps_, 0:128], vt[:, j, 128 * h + 64 * c:128 * h + 64 * c + 64], PT[:, w, c, j, :], tp[c],
                               start=(j == 0), stop=(j == i))
                    ptv[w][c] = t
                yield
                t = act(ym[:, h, qs], bo[:, 0:128], ACT.Copy, t)
            give(bo, t)

        ptv = [[None, None] for _ in range(NW)]
        todo = [(0, h, d) for d in (0, 1) for h in range(4)] + [(1, h, 1) for h in range(4)] + \
               [(2, h, 1) for h in range(4)] + [(1, h, 0) for h in range(4)] + [(3, h, 1) for h in range(4)] + \
               [(2, h, 0) for h in range(4)] + [(3, h, 0) for h in range(4)]

        def worker(w):
            while todo:
                i, h, d = todo.pop(0)
                yield from unit(w, i, h, d)
                yield

        run(indexer(), *[worker(w) for w in range(NW)])
        t0 = K.last("act")
        for i in range(4):
            for h in range(4):
                o_ = ob[:, i, 128 * h:128 * h + 128]
                ttr(r1[:, 0, 0:128], o_, o_, 1.0, 0.0, ALU.mult, ALU.add, nrm[:, 0, 4 * i + h:4 * i + h + 1], t0)
        t = act(nrm[:, 1, :], nrm[:, 0, :], ACT.Sqrt, K.last("dve"), bias=EPS6, scale=1.0 / 128)
        recip(nrm[:, 0, :], nrm[:, 1, :], t)
        li = 0.8 - 0.6 * float(np.exp(-0.3 * l))
        for i in range(4):
            t = tt(v4(ob[:, i, :]), v4(ob[:, i, :]), bc(nrm[:, 0, 4 * i:4 * i + 4], 128), ALU.mult)
            b = bank()
            for h in range(4):
                t2 = tr(b[:, h * 128:(h + 1) * 128], ob[:, i, h * 128:(h + 1) * 128], ident, t)
            t = act(ym[:, 4:8, i * 128:(i + 1) * 128], v4(b[:, :]), ACT.Copy, t2, scale=gsc[:, l:l + 1])
            give(b, t)
        dump(f"ymb{l}", ym[:, :, :])
        big[2] = K.all()
        for hf in range(2):
            ent, wap, tk = ring.load([(0, 4096, 8, A["w_out_2"][l][:, hf * 512:(hf + 1) * 512].rearrange("(k p) n -> p k n", p=128))], 4096)
            wv = wap.rearrange("p (k n) -> p k n", k=8)
            for i in range(4):
                b = bank()
                for k in range(8):
                    t = mm(b[:, :], ym[:, k, i * 128:(i + 1) * 128], wv[:, k, :], tk, K.last("act"), K.last("dve") if i == 0 else None,
                           start=(k == 0), stop=(k == 7))
                hs = slice(hf * 512, (hf + 1) * 512)
                t = tt(xt[:, i, hs], xt[:, i, hs], b[:, :], ALU.add, t)
                give(b, t)
            ent[2] = K.last("pe")
        K.barrier()
        at.close()
        dump(f"xa{l}", xt[:, :, :])
        ff = ExitStack()
        hf_ = sb(f"hf{l}", [128, 22, 512], c=ff)
        gsl = sb(f"gsl{l}", [128, 2, 512], c=ff)
        t_h = rms_T("g_ffn", l)
        gr = [None, None]
        for fp in range(11):
            ws = [A["w_gate"][l][:, fp * 256:(fp + 1) * 256].rearrange("(k p) n -> p k n", p=128),
                  A["w_up"][l][:, fp * 256:(fp + 1) * 256].rearrange("(k p) n -> p k n", p=128)]
            ent, wap, tk = ring.load([(0, 2048, 8, ws[0]), (2048, 2048, 8, ws[1])], 4096)
            w1 = wap[:, 0:2048].rearrange("p (k n) -> p k n", k=8)
            w3 = wap[:, 2048:4096].rearrange("p (k n) -> p k n", k=8)
            for f in range(2):
                b = bank()
                for k in range(8):
                    t = mm(b[:, :], w1[:, k, f * 128:(f + 1) * 128], hT[:, k, :], tk, t_h, start=(k == 0), stop=(k == 7))
                b2 = bank()
                for k in range(8):
                    t2 = mm(b2[:, :], w3[:, k, f * 128:(f + 1) * 128], hT[:, k, :], start=(k == 0), stop=(k == 7))
                t = act(gsl[:, f, :], b[:, :], ACT.Silu, t, gr[f])
                give(b, t)
                t = tt(hf_[:, 2 * fp + f, :], gsl[:, f, :], b2[:, :], ALU.mult, t, t2)
                gr[f] = t
                give(b2, t)
            ent[2] = K.last("pe")
        t_hf = K.last("dve")
        for hf in range(2):
            bs = [bank() for _ in range(4)]
            for g in range(4):
                fs = list(range(g * 6, min(22, g * 6 + 6)))
                nf = len(fs)
                src = A["w_down"][l][fs[0] * 128:(fs[-1] + 1) * 128, hf * 512:(hf + 1) * 512].rearrange("(k p) n -> p k n", p=128)
                ent, wap, tk = ring.load([(0, nf * 512, nf, src)], nf * 512)
                wv = wap.rearrange("p (k n) -> p k n", k=nf)
                for i in range(4):
                    for q, f in enumerate(fs):
                        t = mm(bs[i][:, :], hf_[:, f, i * 128:(i + 1) * 128], wv[:, q, :], tk, t_hf, start=(f == 0), stop=(f == 21))
                ent[2] = t
            for i in range(4):
                hs = slice(hf * 512, (hf + 1) * 512)
                t = tt(xt[:, i, hs], xt[:, i, hs], bs[i][:, :], ALU.add, K.last("pe"))
                give(bs[i], t)
        K.barrier()
        ff.close()
        dump(f"xf{l}", xt[:, :, :])
    od = out.rearrange("(b p) d -> p b d", p=128)
    for i in range(4):
        rms_rows(xt[:, i, :])
        t = stt(xt[:, i, :], xt[:, i, :], rstd[:, 0:1], gfr, ALU.mult, ALU.mult, t_gf)
        t_o = K.dma("sp", lambda e, i=i: e.dma_start(od[:, i, :], xt[:, i, :]), t)
        K.wait("sp", t_o)
    for i in range(len(K.dn)):
        if K.dn[i]:
            K.wait("sp", (f"d{i}", K.dsem[i], K.dn[i]))
    m6.close()
    K.emit()


def _layout(I):
    a = {k: np.asarray(v) for k, v in I.items()}

    def colp(v):
        return v.reshape(-1, 128).T

    cols = {
        "conv_w": colp(a["ssd_conv_w"][0]), "conv_b": colp(a["ssd_conv_b"][0]), "mu": colp(a["rwkv_mu"][0]),
        "a0": colp(a["rwkv_a0"][0]), "kk": colp(a["rwkv_kk"][0]), "ka": colp(a["rwkv_ka"][0]),
        "rk": colp(a["rwkv_rk"][0]), "lnw": colp(a["rwkv_lnx_w"][0]), "lnb": colp(a["rwkv_lnx_b"][0]),
        "c": colp(a["c"][0]), "cc": colp(a["c_ctx"]), "g_mix": colp(a["g_mix_2"]), "g_ffn": colp(a["g_ffn_2"]),
        "g_sub": colp(a["g_subln_2"]), "gla_w": colp(a["gla_norm_w"][0]), "ssd_w": colp(a["ssd_norm_w"][0]),
    }
    rows = {
        "dtb": a["ssd_dt_bias"], "alog": a["ssd_a_log"], "ssd_d": a["ssd_d"], "w0": a["rwkv_w0"], "gb": a["gla_gb"],
        "ln1w": a["ln1_w"], "ln1b": a["ln1_b"], "ln2w": a["ln2_w"], "ln2b": a["ln2_b"], "rb": a["router_b"],
        "gfin": a["g_final_2"],
        "lam": np.stack([a["lam_q1_2"], a["lam_k1_2"], a["lam_q2_2"], a["lam_k2_2"]], 1),
    }

    def bdiag(x, n):
        k, m = x.shape[1:]
        o = np.zeros((n, 2 * m), x.dtype)
        for i in range(2):
            o[i * k:(i + 1) * k, i * m:(i + 1) * m] = x[i]
        return o

    def expert(w1, w3, w2):
        n = w1.shape[0]
        f = lambda w, k: w.reshape(n, k, 128, -1).transpose(0, 2, 1, 3).reshape(n, 128, -1)
        w13 = np.concatenate([w1.reshape(n, 8, 128, -1), w3.reshape(n, 8, 128, -1)], 3)
        return np.concatenate([w13.transpose(0, 2, 1, 3).reshape(n, 128, -1), f(w2, 2)], 2)

    W = a["w_in_2"]
    ik = W[:, :, 1792:1824]
    w_in_2 = np.concatenate([W[:, :, 0:1024], W[:, :, 1832:2856], W[:, :, 1536:1792], ik, ik, ik, ik,
                             W[:, :, 1024:1536], W[:, :, 2856:3368], W[:, :, 1824:1832]], 2)
    out = {
        "x": a["x"][0], "ctx": a["ctx"][0], "ada_w": a["ada_w"][0], "ada_b": a["ada_b"], "w_in": a["w_in"][0],
        "cst": _const_mats()[1], "rope": _rope_tables(),
        "cols": np.concatenate([cols[n] for n, _ in COLS], 1),
        "rows": np.concatenate([rows[n].reshape(1, -1) for n, _ in ROWS], 1),
        "gux": bdiag(a["gla_gu"][0], 32), "w2x": bdiag(a["rwkv_w2"][0], 128), "a2x": bdiag(a["rwkv_a2"][0], 128),
        "g2": a["rwkv_g2"][0], "w_out": a["w_out"][0], "router_w": a["router_w"][0],
        "ew": expert(a["exp_w1"][0], a["exp_w3"][0], a["exp_w2"][0]),
        "sw": expert(a["sh_w1"], a["sh_w3"], a["sh_w2"])[0],
        "w_in_2": w_in_2, "w_out_2": a["w_out_2"], "w_gate": a["w_gate_2"], "w_up": a["w_up_2"], "w_down": a["w_down_2"],
    }
    return {k: np.ascontiguousarray(v) for k, v in out.items()}


def _declare(nc, arrays):
    return {k: nc.dram_tensor("in_" + k, v.shape, mybir.dt.from_np(v.dtype), kind="ExternalInput").ap()
            for k, v in arrays.items()}


def kernel(**inputs):
    import concourse.bacc as _bacc
    from concourse.bass_utils import run_bass_kernel_spmd as _run

    nc = _bacc.Bacc("TRN2", target_bir_lowering=False, num_devices=1)
    arrays = _layout(inputs)
    A = _declare(nc, arrays)
    out = nc.dram_tensor("out", (512, 1024), F32, kind="ExternalOutput").ap()
    build(nc, A, out)
    r = _run(nc, [{"in_" + k: v for k, v in arrays.items()}], core_ids=[0])
    return r.results[0]["out"].reshape(1, 512, 1024)
```

```python
import numpy as np
import concourse.bass as bass
from concourse import mybir
from contextlib import ExitStack

F32 = mybir.dt.float32
I32 = mybir.dt.int32
ALU = mybir.AluOpType
ACT = mybir.ActivationFunctionType
AX = mybir.AxisListType

D = 1024
NIN = 3504
E05 = float(np.exp(-0.5))
ALPHA = float(2 ** 0.25)

def _const_mats():
    i = np.arange(128)
    s, t = i[:, None], i[None, :]
    m = {}
    for d in range(2):
        le = (s <= t) if d == 0 else (s >= t)
        lt = (s < t) if d == 0 else (s > t)
        gt = (s > t) if d == 0 else (s < t)
        b64 = s // 64 == t // 64
        b16 = s // 16 == t // 16
        m[f"i128_{d}"] = le
        m[f"g128_{d}"] = gt
        m[f"i64_{d}"] = le & b64
        m[f"e64_{d}"] = lt & b64
        half = (s % 16 < 8) if d == 0 else (s % 16 >= 8)
        m[f"q16_{d}"] = (le & b16).astype(np.float32) - (half & b16)
        m[f"i16_{d}"] = le & b16
        m[f"c16_{d}"] = s // 16 == np.arange(8)[None, :]
        m[f"x16_{d}"] = gt & b16
        for k in range(6):
            w = 1 << k
            blk = s // (2 * w) == t // (2 * w)
            sh, th = (s // w) % 2, (t // w) % 2
            m[f"l{k}_{d}"] = blk & ((sh == 0) & (th == 1) if d == 0 else (sh == 1) & (th == 0))
    m["ones"] = np.ones((128, 128))
    m["ident"] = np.eye(128)
    m["h64"] = s // 64 == t // 64
    m["ch64"] = s // 64 == np.arange(2)[None, :]
    m["bd"] = s // 32 == np.arange(256)[None, :] // 64
    m["sw64"] = (s // 64 == t // 64) & ((s % 64 + 32) % 64 == t % 64)
    m["sw32"] = (s // 32 == t // 32) & ((s % 32 + 16) % 32 == t % 32)
    m["iota"] = t + 0 * s
    m["one8"] = np.ones((128, 64))
    ii = np.arange(128)[:, None]
    m["ii"] = ii
    m["tri64"] = (s < t)[:, 0:64]
    r0 = np.zeros((128, 128))
    r0[0] = 1
    m["row0"] = r0
    out, at, parts = {}, 0, []
    for k, v in m.items():
        v = np.asarray(v, np.float32)
        out[k] = (at, v.shape[1])
        parts.append(v)
        at += v.shape[1]
    return out, np.ascontiguousarray(np.concatenate(parts, 1))


def _rope_tables():
    out = []
    for dim in (64, 32):
        half = dim // 2
        inv = 10000.0 ** (-np.arange(0, dim, 2, dtype=np.float32) / np.float32(dim))
        ang = np.arange(512, dtype=np.float32)[:, None] * inv.astype(np.float32)[None, :]
        c, s = np.cos(ang).T, np.sin(ang).T
        p = np.arange(128) % dim
        out.append(c[p % half])
        out.append(np.where((p < half)[:, None], -s[p % half], s[p % half]))
    return np.ascontiguousarray(np.stack(out, 1).astype(np.float32))


COLS = [("conv_w", 24), ("conv_b", 8), ("mu", 36), ("a0", 4), ("kk", 2), ("ka", 2), ("rk", 2),
        ("lnw", 2), ("lnb", 2), ("c", 8), ("cc", 8), ("g_mix", 16), ("g_ffn", 16), ("g_sub", 2),
        ("gla_w", 2), ("ssd_w", 4)]
ROWS = [("dtb", 16), ("alog", 16), ("ssd_d", 8), ("w0", 512), ("gb", 256), ("ln1w", 1024), ("ln1b", 1024),
        ("ln2w", 1024), ("ln2b", 1024), ("rb", 64), ("gfin", 1024), ("lam", 512)]


def _offsets(items):
    o, at = {}, 0
    for n, w in items:
        o[n] = (at, w)
        at += w
    return o, at


CO, CN = _offsets(COLS)
RO, RN = _offsets(ROWS)


class Queues:

    def __init__(self, nc, ctx):
        self.nc, self.ctx = nc, ctx
        self.q = {e: [] for e in ("pe", "act", "dve", "pool", "sp")}
        self.sem = {e: ctx.enter_context(nc.semaphore("s_" + e)) for e in ("pe", "act", "dve", "pool")}
        self.n = {e: 0 for e in self.sem}
        self.seen = {e: {} for e in self.q}
        self.dsem = [ctx.enter_context(nc.semaphore(f"s_dma{i}")) for i in range(56)]
        self.dn = [0] * 56
        self.dnext = [0, 0]
        self.parts, self.tag = {}, ""

    def wait(self, e, *toks):
        for t in toks:
            if t is None:
                continue
            if isinstance(t, list):
                self.wait(e, *t)
                continue
            name, s, v = t
            if self.seen[e].get(name, 0) >= v:
                continue
            self.seen[e][name] = v
            self.q[e].append(lambda eng, s=s, v=v: eng.wait_ge(s, v))

    def op(self, e, fn, *toks, chain=None):
        self.wait(e, *toks)
        if (e != "pe" if chain is None else chain) and self.n[e]:
            self.wait(e, (self.tag + e, self.sem[e], self.n[e]))
        self.n[e] += 1
        s = self.sem[e]
        self.q[e].append(lambda eng: fn(eng).then_inc(s, 1))
        return (self.tag + e, s, self.n[e])

    def last(self, e):
        return (self.tag + e, self.sem[e], self.n[e]) if self.n[e] else None

    def all(self):
        return [self.last(e) for e in self.sem]

    def dma(self, e, fn, *toks):
        sw, hw = e == "pool", len(self.dsem) - len(self.dsem) // 7
        i = self.dnext[sw]
        self.dnext[sw] = (i + 1) % (len(self.dsem) - hw if sw else hw)
        i += hw * sw
        s = self.dsem[i]
        if self.dn[i]:
            self.wait(e, (f"{self.tag}d{i}", s, self.dn[i]))
        self.wait(e, *toks)
        self.dn[i] += 16
        self.q[e].append(lambda eng: fn(eng).then_inc(s, 16))
        return (f"{self.tag}d{i}", s, self.dn[i])

    def barrier(self, engines=("pe", "act", "dve", "pool")):
        toks = self.all()
        for e in engines:
            self.wait(e, *toks)

    def part(self, name):
        self.saved = (self.q, self.sem, self.n, self.seen, self.dsem, self.dn, self.dnext)
        new = lambda n: self.ctx.enter_context(self.nc.semaphore(n))
        if name not in self.parts:
            self.parts[name] = ({e: new(f"{name}_{e}") for e in self.sem}, {e: 0 for e in self.sem},
                                [new(f"{name}_d{i}") for i in range(14)], [0] * 14)
        self.sem, self.n, self.dsem, self.dn = self.parts[name]
        self.tag = name
        self.q = {e: [] for e in self.q}
        self.seen = {e: {} for e in self.q}
        self.dnext = [0, 0]

    def part_end(self, guard):
        sub = self.q
        self.q, self.sem, self.n, self.seen, self.dsem, self.dn, self.dnext = self.saved
        self.tag = ""
        for e in self.q:
            def body(eng, e=e):
                with guard(e, eng):
                    for f in sub[e]:
                        f(eng)
            self.q[e].append(body)

    def emit(self):
        block = self.ctx.enter_context(self.nc.Block())
        for e, deco in (("sp", block.sync), ("act", block.scalar), ("dve", block.vector),
                        ("pool", block.gpsimd), ("pe", block.tensor)):
            lst = self.q[e]

            def body(eng, lst=lst):
                for f in lst:
                    f(eng)
            deco(body)


def run(*gens):
    gens = list(gens)
    while gens:
        for g in list(gens):
            try:
                next(g)
            except StopIteration:
                gens.remove(g)


class Ring:

    def __init__(self, K, buf, size):
        self.K, self.buf, self.size, self.pos, self.live = K, buf, size, 0, []

    def take(self, n):
        if self.pos + n > self.size:
            self.pos = 0
        a, b = self.pos, self.pos + n
        self.pos = b
        over = [x for x in self.live if x[0] < b and a < x[1]]
        self.live = [x for x in self.live if not (x[0] < b and a < x[1])]
        ent = [a, b, None]
        self.live.append(ent)
        for x in over:
            assert x[2] is not None, "ring slot still in use"
        return ent, self.buf[:, a:b], [x[2] for x in over]

    def load(self, srcs, n):
        ent, ap, over = self.take(n)
        toks = []
        for o, w, a, src in srcs:
            dst = ap[:, o:o + w]
            if a:
                dst = dst.rearrange("p (a b) -> p a b", a=a)
            toks.append(self.K.dma("sp", lambda e, dst=dst, src=src: e.dma_start(dst, src), over))
        return ent, ap, toks


class Ahead:

    def __init__(self, items, n):
        self.items, self.n, self.q = list(items), n, []
        self.fill()

    def fill(self):
        while self.items and len(self.q) < self.n:
            self.q.append(self.items.pop(0)())

    def next(self):
        self.fill()
        return self.q.pop(0)


def build(nc, A, out, DBG=None):
    ctx = ExitStack()
    with ctx:
        _program(nc, ctx, A, out, DBG)


def _program(nc, ctx, A, out, DBG):
    K = Queues(nc, ctx)
    op = K.op
    cmap, _ = _const_mats()

    def sb(name, shape, dt=F32, c=ctx):
        return c.enter_context(nc.sbuf_tensor(name, shape, dt))

    banks = [ctx.enter_context(nc.psum_tensor(f"ps{i}", [128, 512], F32)) for i in range(8)]
    free = [(b, None) for b in banks]

    def bank():
        b, tok = free.pop(0)
        K.wait("pe", tok)
        return b

    def give(b, *toks):
        free.append((b, list(toks)))

    def mm(o, l, r, *toks, start=True, stop=True, after=False):
        return op("pe", lambda e: e.matmul(o, l, r, start=start, stop=stop), *toks, chain=after)

    def tr(o, i, idn, *toks):
        return op("pe", lambda e: e.transpose(o, i, idn), *toks)

    def tt(o, a, b, alu, *toks, e="dve"):
        return op(e, lambda g: g.tensor_tensor(o, a, b, alu), *toks)

    def ts(o, a, s1, s2, o1, o2, *toks, e="dve"):
        if s2 is None:
            return op(e, lambda g: g.tensor_scalar(o, a, s1, None, o1), *toks)
        return op(e, lambda g: g.tensor_scalar(o, a, s1, s2, o1, o2), *toks)

    def stt(o, a, s, b, o1, o2, *toks):
        return op("dve", lambda g: g.scalar_tensor_tensor(out=o, in0=a, scalar=s, in1=b, op0=o1, op1=o2), *toks)

    def act(o, i, f, *toks, bias=None, scale=1.0, accum=None):
        kw = {"scale": scale}
        if bias is not None:
            kw["bias"] = bias
        if accum is not None:
            kw["accum_out"] = accum
        return op("act", lambda g: g.activation(o, i, f, **kw), *toks)

    def copy(o, i, *toks, e="dve"):
        if e == "act":
            return act(o, i, ACT.Copy, *toks)
        return op(e, lambda g: g.tensor_copy(o, i), *toks)

    def memset(o, v, *toks, e="pool"):
        return op(e, lambda g: g.memset(o, v), *toks)

    def ttr(o, a, b, sc_, init, o0, o1, acc, *toks):
        return op("dve", lambda g: g.tensor_tensor_reduce(out=o, in0=a, in1=b, scale=sc_, scalar=init, op0=o0, op1=o1,
                                                          accum_out=acc), *toks)

    def recip(o, i, *toks):
        return op("dve", lambda g: g.reciprocal(o, i), *toks)

    def max8(o, i, *toks):
        return op("dve", lambda g: g.max(o, i), *toks)

    def strike(o, m, i, *toks):
        return op("dve", lambda g: g.match_replace(out=o, in_to_replace=m, in_values=i, imm_value=-3e38), *toks)

    def red(o, i, alu, *toks):
        return op("dve", lambda g: g.tensor_reduce(o, i, AX.X, alu), *toks)

    def dump(name, ap, *toks):
        if DBG is None or name not in DBG:
            return
        K.wait("sp", K.all())
        t = K.dma("sp", lambda e: e.dma_start(DBG[name], ap))
        for e in ("pe", "act", "dve", "pool"):
            K.wait(e, t)

    def bc(ap, n):
        return ap.unsqueeze(2).to_broadcast([ap.shape[0], ap.shape[1], n])

    def bcm(ap, n):
        return ap.unsqueeze(1).to_broadcast([ap.shape[0], n, ap.shape[1]])

    csb = sb("csb", [128, A["cst"].shape[1]])
    col = sb("col", [128, CN])
    xt = sb("xt", [128, 4, D])
    RS = 12288
    ringbuf = sb("ring", [128, RS])
    ring = Ring(K, ringbuf, RS)
    t_cst = K.dma("sp", lambda e: e.dma_start(csb[:, :], A["cst"]))
    t_col = K.dma("sp", lambda e: e.dma_start(col[:, :], A["cols"]))
    t_x = K.dma("sp", lambda e: e.dma_start(xt[:, :, :], A["x"].rearrange("(b p) d -> p b d", p=128)))

    def C(name):
        a, w = cmap[name]
        return csb[:, a:a + w]

    def cc(name, j=0, n=1):
        a = CO[name][0] + j
        return col[:, a:a + n]

    ident = C("ident")

    def rowload(dst, name, *toks, e="sp", j=0, n=None):
        a, w = RO[name]
        n = n or w
        src = A["rows"][0:1, a + j:a + j + n].to_broadcast([128, n])
        return K.dma(e, lambda g: g.dma_start(dst, src), *toks)

    for e in ("pe", "dve", "act", "pool"):
        K.wait(e, t_cst, t_col)

    eps5 = sb("eps5", [128, 4])
    t_eps = memset(eps5[:, 0:1], 1e-5)
    memset(eps5[:, 1:2], 64e-5)
    memset(eps5[:, 2:3], 1e-6)
    t_eps = memset(eps5[:, 3:4], 1.0)
    K.wait("act", t_eps)
    EPS5, EPS64, EPS6, ONE = (eps5[:, j:j + 1] for j in range(4))

    stt6 = sb("stt6", [128, 2, 6])
    mv = sb("mv", [128, 4])
    rstd = sb("rstd", [128, 4])

    def ln_stats(src, *toks):
        for j in range(2):
            op("dve", lambda g, j=j: g.bn_stats(stt6[:, j, :], src[:, j * 512:(j + 1) * 512]), *toks)
        t = op("dve", lambda g: g.bn_aggr(mv[:, 0:2], stt6[:, :, :]))
        t = act(rstd[:, 1:2], mv[:, 1:2], ACT.Sqrt, t, bias=EPS5)
        return recip(rstd[:, 0:1], rstd[:, 1:2], t)

    b1 = ExitStack()
    uT = sb("uT", [128, 8, 768], c=b1)
    ym = uT[:, :, :].rearrange("p k t -> p (k t)")[:, 0:4096].rearrange("p (k t) -> p k t", k=8)
    modc = sb("modc", [128, 2, 8, 2], c=b1)
    scv = sb("scv", [128, 8, 2], c=b1)
    sig = sb("sigc", [128, 16], c=b1)
    act(sig[:, 0:16], cc("c", 0, 16), ACT.Sigmoid)
    t = tt(sig[:, 0:16], sig[:, 0:16], cc("c", 0, 16), ALU.mult, K.last("act"))
    t_sc = copy(scv[:, :, :], sig[:, 0:16].rearrange("p (b k) -> p k b", b=2))

    def ada(sec, mrow, brow):
        tb = K.dma("sp", lambda e: e.dma_start(brow[0:1, :], A["ada_b"][0:1, sec * D:(sec + 1) * D]), K.last("pe"))
        for h in range(2):
            w = sec * D + h * 512
            ent, wap, tk = ring.load([(0, 4096, 8, A["ada_w"][:, w:w + 512].rearrange("(k p) n -> p k n", p=128))], 4096)
            wv = wap.rearrange("p (k n) -> p k n", k=8)
            b = bank()
            mm(b[0:2, :], C("ones")[0:1, 0:2], brow[0:1, h * 512:(h + 1) * 512], tb, tk, t_sc, start=True, stop=False)
            for k in range(8):
                t = mm(b[0:2, :], scv[:, k, :], wv[:, k, :], start=False, stop=(k == 7))
            ent[2] = t
            t = act(mrow[0:2, h * 512:(h + 1) * 512], b[0:2, :], ACT.Copy, t, K.last("pe"))
            give(b, t)
            yield
        b = bank()
        for k in range(8):
            t = tr(b[:, 2 * k:2 * k + 2], mrow[0:2, k * 128:(k + 1) * 128], ident[0:2, 0:2], t)
        yield
        t = ts(modc[:, sec, :, :].rearrange("p k b -> p (k b)"), b[:, 0:16], float(sec), None, ALU.add, None, t)
        give(b, t)
        yield

    with ExitStack() as s0:
        mrow = sb("mrow", [2, D], c=s0)
        brow = sb("brow", [1, D], c=s0)
        run(ada(0, mrow, brow))
        run(ada(1, mrow, brow))
        K.barrier()

    m1 = ExitStack()
    uctx = ExitStack()
    rwm = sb("rwm", [128, 9, 768], c=m1)
    m1b = ExitStack()
    zx = sb("zx", [128, 4, 512], c=m1b)
    xbc = sb("xbc", [128, 8, 768], c=m1b)
    gqT = sb("gqT", [128, 512], c=m1b)
    gkT = sb("gkT", [128, 768], c=m1b)
    gkv = sb("gkv", [128, 6, 384], c=m1b)
    ogt = sb("ogt", [128, 4, 256], c=m1b)
    gdT = sb("gdT", [32, 768], c=m1b)
    dtt = sb("dtt", [128, 6, 16], c=m1b)
    ctxt = sb("ctxt", [128, 2, D], c=uctx)
    xn = sb("xn", [128, 2, D], c=uctx)
    t_ctx = K.dma("sp", lambda e: e.dma_start(ctxt[:, :, :], A["ctx"].rearrange("(b p) d -> p b d", p=128)), K.all())
    t_mod = K.last("dve")
    xnt = [None, None]
    for b6 in range(6):
        src = ctxt[:, b6, :] if b6 < 2 else xt[:, b6 - 2, :]
        ln_stats(src, t_x, t_ctx)
        ts(xn[:, b6 % 2, :], src, mv[:, 0:1], rstd[:, 0:1], ALU.subtract, ALU.mult, xnt[b6 % 2])
        tn = K.last("dve")
        s = 1 if b6 < 2 else 0
        for hf in range(2):
            b = bank()
            for k in range(4):
                t = tr(b[:, k * 128:(k + 1) * 128], xn[:, b6 % 2, (hf * 4 + k) * 128:(hf * 4 + k + 1) * 128], ident, tn)
            xnt[b6 % 2] = t
            for k in range(4):
                kk = hf * 4 + k
                t2 = act(uT[:, kk, b6 * 128:(b6 + 1) * 128], b[:, k * 128:(k + 1) * 128], ACT.Identity, t, t_mod,
                         bias=modc[:, 0, kk, s:s + 1], scale=modc[:, 1, kk, s:s + 1])
            give(b, t2)
    t_u = K.last("act")
    K.barrier()
    uctx.close()
    raw = sb("raw", [128, 2, 768], c=uctx)
    cv = sb("cv", [128, 2, 768], c=uctx)
    dtb = sb("dtb", [128, 16], c=uctx)
    sg = sb("sg", [128, 96], c=uctx)
    oms = sb("oms", [128, 2, 9], c=uctx)
    t_dtb = rowload(dtb[:, :], "dtb", K.all())
    dump("uT", uT[:, :, :])

    def wload(c0, n):
        ent, wap, tk = ring.load([(0, 8 * n, 8, A["w_in"][:, c0:c0 + n].rearrange("(k p) n -> p k n", p=128))], 8 * n)
        return ent, wap.rearrange("p (k n) -> p k n", k=8), tk

    def proj_tok(wv, lo, n, b6, tk):
        b = bank()
        for k in range(8):
            t = mm(b[:, 0:n], uT[:, k, b6 * 128:(b6 + 1) * 128], wv[:, k, lo:lo + n], t_u, tk, start=(k == 0), stop=(k == 7))
        return b, t

    def proj_ch(wv, lo, n, tk, ctxtoo=True):
        b = bank()
        for k in range(8):
            t = mm(b[0:n, :], wv[:, k, lo:lo + n], uT[:, k, 256:768], t_u, tk, start=(k == 0), stop=(k == 7))
        b2 = None
        if ctxtoo:
            b2 = bank()
            for k in range(8):
                t = mm(b2[0:n, 0:256], wv[:, k, lo:lo + n], uT[:, k, 0:256], start=(k == 0), stop=(k == 7))
        return b, b2, t

    ent, wv, tk = wload(1536, 16)
    for b6 in range(6):
        b, t = proj_tok(wv, 0, 16, b6, tk)
        t = tt(dtt[:, b6, :], b[:, 0:16], dtb[:, :], ALU.add, t, t_dtb)
        give(b, t)
    ent[2] = K.last("pe")
    dtf = dtt[:, :, :].rearrange("p a b -> p (a b)")
    sp1 = sg[:, 0:96]
    t = act(sp1, dtf, ACT.Abs, K.last("dve"))
    act(sp1, sp1, ACT.Exp, scale=-1.0)
    t = act(sp1, sp1, ACT.Ln, bias=ONE)
    t_dt = stt(dtf, dtf, 0.0, sp1, ALU.max, ALU.add, t)
    ent, wv, tk = wload(0, 512)
    for i in range(4):
        b, t = proj_tok(wv, 0, 512, i + 2, tk)
        t = act(zx[:, i, :], b[:, :], ACT.Silu, t)
        give(b, t)
    ent[2] = K.last("pe")
    ent, wv, tk = wload(3248, 256)
    for i in range(4):
        b, t = proj_tok(wv, 0, 256, i + 2, tk)
        t = act(ogt[:, i, :], b[:, 0:256], ACT.Silu, t)
        give(b, t)
    ent[2] = K.last("pe")
    ent, wv, tk = wload(2832, 384)
    for b6 in range(6):
        b, t = proj_tok(wv, 0, 384, b6, tk)
        t = copy(gkv[:, b6, :], b[:, 0:384], t)
        give(b, t)
    b, b2, t = proj_ch(wv, 0, 128, tk)
    t1 = copy(gkT[:, 256:768], b[:, :], t, e="act")
    t2 = copy(gkT[:, 0:256], b2[:, 0:256], t, e="act")
    give(b, t1)
    give(b2, t2)
    ent[2] = K.last("pe")
    ent, wv, tk = wload(2704, 128)
    b, _, t = proj_ch(wv, 0, 128, tk, False)
    t1 = act(gqT[:, :], b[:, :], ACT.Copy, t, scale=32 ** -0.5)
    give(b, t1)
    ent[2] = t
    ent, wv, tk = wload(3216, 32)
    b, b2, t = proj_ch(wv, 0, 32, tk)
    t1 = copy(gdT[:, 256:768], b[0:32, :], t, e="act")
    t2 = copy(gdT[:, 0:256], b2[0:32, 0:256], t, e="act")
    give(b, t1)
    give(b2, t2)
    ent[2] = t
    rawr = [None, None]
    cvr = [None, None]
    ts(oms[:, 0, :], cc("mu", 0, 9), -1.0, 1.0, ALU.mult, ALU.add)
    tt(oms[:, 0, :], oms[:, 0, :], cc("mu", 9, 9), ALU.subtract)
    tt(oms[:, 1, :], oms[:, 0, :], cc("mu", 18, 9), ALU.subtract)
    tt(oms[:, 1, :], oms[:, 1, :], cc("mu", 27, 9), ALU.subtract)
    n = 0
    for g in range(5):
        c0, w = [(512, 512), (1024, 512), (1552, 512), (2064, 512), (2576, 128)][g]
        ent, wv, tk = wload(c0, w)
        for j in range(w // 128):
            b, b2, t = proj_ch(wv, j * 128, 128, tk)
            r = raw[:, n % 2, :]
            t1 = act(r[:, 256:768], b[:, :], ACT.Copy, t, rawr[n % 2])
            t2 = act(r[:, 0:256], b2[:, 0:256], ACT.Copy)
            give(b, t1)
            give(b2, t2)
            if n < 8:
                o = cv[:, n % 2, :]
                ts(o, r, cc("conv_w", 8 + n), cc("conv_b", n), ALU.mult, ALU.add, t2, cvr[n % 2])
                for a, z in ((0, 256), (256, 768)):
                    stt(o[:, a + 1:z], r[:, a:z - 1], cc("conv_w", n), o[:, a + 1:z], ALU.mult, ALU.add)
                    t = stt(o[:, a:z - 1], r[:, a + 1:z], cc("conv_w", 16 + n), o[:, a:z - 1], ALU.mult, ALU.add)
                rawr[n % 2] = t
                t = act(xbc[:, n, :], o, ACT.Silu, t)
                cvr[n % 2] = t
            else:
                m = n - 8
                o = rwm[:, m, :]
                mu = [cc("mu", 9 * q + m) for q in range(4)]
                ts(o[:, 0:256], r[:, 0:256], oms[:, 0, m:m + 1], None, ALU.mult, None, t2)
                stt(o[:, 1:256], r[:, 0:255], mu[0], o[:, 1:256], ALU.mult, ALU.add)
                stt(o[:, 0:255], r[:, 1:256], mu[1], o[:, 0:255], ALU.mult, ALU.add)
                ts(o[:, 256:768], r[:, 256:768], oms[:, 1, m:m + 1], None, ALU.mult, None)
                og = o[:, 256:768].rearrange("p (r c) -> p r c", c=64)
                rg = r[:, 256:768].rearrange("p (r c) -> p r c", c=64)
                stt(og[:, :, 1:64], rg[:, :, 0:63], mu[0], og[:, :, 1:64], ALU.mult, ALU.add)
                stt(og[:, :, 0:63], rg[:, :, 1:64], mu[1], og[:, :, 0:63], ALU.mult, ALU.add)
                stt(o[:, 320:768], r[:, 256:704], mu[2], o[:, 320:768], ALU.mult, ALU.add)
                t = stt(o[:, 256:704], r[:, 320:768], mu[3], o[:, 256:704], ALU.mult, ALU.add)
                rawr[n % 2] = t
            n += 1
        ent[2] = K.last("pe")
    K.barrier()
    uctx.close()
    dump("xbc", xbc[:, :, :])
    dump("rwm", rwm[:, :, :])
    dump("dtt", dtt[:, :, :])

    FW = [0, 1, 2, 3, 4, 5]
    BW = [1, 0, 5, 4, 3, 2]
    ORD = (FW, BW)

    s1 = ExitStack()
    big, scr, over = ring.take(12288)
    for e in ("dve", "act", "pool", "sp"):
        K.wait(e, over)
    uf = uT[:, :, :].rearrange("p k t -> p (k t)")
    lax, sct, Hs2, xdt, xst = (uf[:, 0:1024], uf[:, 1024:2048], uf[:, 2048:3072], uf[:, 3072:3584], uf[:, 3584:4096])
    Hs = Hs2.rearrange("p (a b) -> p a b", a=2)
    ysd = uf[:, 4096:6144].rearrange("p (i n) -> p i n", i=4)
    btk, las, na, gtm, ex3, sdd, xde, yo = (
        sb(n, [128, w], c=s1) for n, w in
        (("btk", 256), ("las", 96), ("na", 16), ("gtm", 256), ("ex3", 24), ("sdd", 8), ("xde", 512), ("yo", 512)))
    lag = sb("lag", [128, 6, 256], c=s1)
    las3 = las[:, :].rearrange("p (i h) -> p i h", i=6)
    Sg = scr[:, 0:4608].rearrange("p (d c n) -> p d c n", d=2, c=9)
    og2 = scr[:, 4608:5632].rearrange("p (i n) -> p i n", i=4)
    gt1 = scr[:, 5632:7168].rearrange("p (a b) -> p a b", a=6)
    gux, gbr = scr[0:32, 7680:7936], scr[0:1, 7936:8192]

    def gla_buffers(d):
        B = {"kde": scr[:, 5632 + 1024 * d:6656 + 1024 * d], "stm": scr[:, 7680 + 512 * d:8192 + 512 * d],
             "qx": scr[:, 8704 + 1152 * d:9856 + 1152 * d], "sTg": scr[:, 11008 + 512 * d:11520 + 512 * d],
             "qp": scr[:, 12032:12288] if d == 0 else sb("qp1", [128, 256], c=s1)[:, :]}
        for n, w in (("cq", 128), ("eq", 512), ("etot", 8)):
            B[n] = sb(f"{n}{d}", [128, w], c=s1)[:, :]
        return B

    GB = [gla_buffers(d) for d in range(2)]
    t_na = rowload(na[:, :], "alog", K.all())
    t_sdd = rowload(sdd[:, :], "ssd_d", K.all())
    t1 = K.dma("sp", lambda e: e.dma_start(gux, A["gux"]))
    t2 = K.dma("sp", lambda e: e.dma_start(gbr, A["rows"][0:1, RO["gb"][0]:RO["gb"][0] + 256]))
    t = act(na[:, :], na[:, :], ACT.Exp, t_na)
    t = ts(na[:, :], na[:, :], -1.0, None, ALU.mult, None, t)
    tt(las3, dtt[:, :, :], bcm(na[:, :], 6), ALU.mult, t_dt)
    memset(Hs2, 0.0, e="dve")
    t_las = K.last("dve")
    for b6 in range(6):
        b = bank()
        mm(b[:, 0:256], C("ones")[0:1, :], gbr, t1, t2, start=True, stop=False)
        t = mm(b[:, 0:256], gdT[0:32, b6 * 128:(b6 + 1) * 128], gux, start=False, stop=True)
        t = copy(lag[:, b6, :], b[:, 0:256], t)
        give(b, t)
    lf = lag[:, :, :].rearrange("p a b -> p (a b)")
    gf = gt1[:, :, :].rearrange("p a b -> p (a b)")
    act(gf, lf, ACT.Abs, K.last("dve"))
    act(gf, gf, ACT.Exp, scale=-1.0)
    t = act(gf, gf, ACT.Ln, bias=ONE)
    t_lag = stt(lf, lf, 0.0, gf, ALU.min, ALU.subtract, t)
    for d in range(2):
        memset(GB[d]["qx"], 0.0, e="dve")
        t_gz = memset(Sg[:, d, 0, :], 0.0, e="dve")
    K.wait("act", t_gz)
    dump("lag", lag[:, :, :])

    def h8(x):
        return x.rearrange("p (h q) -> p h q", q=64)

    s_end = [None]

    def ssd_unit(d, b6, first):
        tok = slice(b6 * 128, (b6 + 1) * 128)
        free_ = s_end[0]
        b = bank()
        for j in range(4):
            t = tr(b[:, j * 128:(j + 1) * 128], xbc[:, j, tok], ident)
        t1 = act(xst, b[:, :], ACT.Copy, t, free_)
        give(b, t1)
        b = bank()
        for j in range(2):
            t = tr(b[:, j * 128:(j + 1) * 128], xbc[:, 4 + j, tok], ident)
        t2 = act(btk[:, :], b[:, 0:256], ACT.Copy, t)
        give(b, t2)
        yield
        la = las[:, 16 * b6 + 8 * d:16 * b6 + 8 * d + 8]
        b = bank()
        mm(b[:, 0:8], C(f"i128_{d}"), la, t_las)
        mm(b[:, 8:16], C(f"g128_{d}"), la)
        t = mm(b[:, 16:24], C("ones"), la)
        t_ex = act(ex3[:, :], b[:, 0:24], ACT.Exp, t)
        give(b, t_ex)
        t_xdt = tt(h8(xdt), h8(xst), bc(dtt[:, b6, 8 * d:8 * d + 8], 64), ALU.mult, t1, free_)
        t_xde = tt(h8(xde[:, :]), h8(xdt), bc(ex3[:, 8:16], 64), ALU.mult, t_ex)
        yield
        if b6 >= 2:
            b = bank()
            for g in range(2):
                t = mm(b[:, g * 128:(g + 1) * 128], xbc[:, 4 + g, tok], xbc[:, 6 + g, tok])
            t_lx = tt(lax.rearrange("p (h s) -> p h s", h=8), bcm(C(f"g128_{d}"), 8), bc(la, 128), ALU.mult)
            tt(gtm[:, :].rearrange("p (g t) -> p g t", g=2), b[:, 0:256].rearrange("p (g t) -> p g t", g=2),
               bcm(C(f"i128_{d}"), 2), ALU.mult, t)
            give(b, K.last("dve"))
            yield
            for hf in range(2):
                b = bank()
                for h in range(4):
                    hh = hf * 4 + h
                    t = mm(b[:, h * 128:(h + 1) * 128], lax[:, hh * 128:(hh + 1) * 128], C(f"i128_{d}"), t_lx)
                o = sct[:, hf * 512:(hf + 1) * 512]
                t = act(o, b[:, :], ACT.Exp, t)
                give(b, t)
                yield
                t_sc_ = tt(o.rearrange("p (h t) -> p h t", h=4), o.rearrange("p (h t) -> p h t", h=4),
                           bcm(gtm[:, hf * 128:(hf + 1) * 128], 4), ALU.mult, t)
            by = bank()
            for h in range(8):
                t_y = mm(by[:, h * 64:(h + 1) * 64], sct[:, h * 128:(h + 1) * 128], xdt[:, h * 64:(h + 1) * 64], t_sc_, t_xdt)
            bo = bank()
            for g in range(2):
                t_o = mm(bo[:, g * 256:(g + 1) * 256], xbc[:, 6 + g, tok], Hs[:, d, g * 256:(g + 1) * 256])
            yield
            ydst = ysd[:, b6 - 2, :]
            t = tt(h8(yo[:, :]), h8(bo[:, :]), bc(ex3[:, 0:8], 64), ALU.mult, t_o)
            give(bo, t)
            if first:
                t = tt(ydst, by[:, :], yo[:, :], ALU.add, t_y)
                give(by, t)
                tt(h8(yo[:, :]), h8(xst), bc(sdd[:, :], 64), ALU.mult, t_sdd)
            else:
                t = tt(yo[:, :], by[:, :], yo[:, :], ALU.add, t_y)
                give(by, t)
            tt(ydst, ydst, yo[:, :], ALU.add)
        b = bank()
        for g in range(2):
            t = mm(b[:, g * 256:(g + 1) * 256], btk[:, g * 128:(g + 1) * 128], xde[:, g * 256:(g + 1) * 256], t2, t_xde)
        yield
        tt(h8(Hs[:, d, :]), h8(Hs[:, d, :]), bc(ex3[:, 16:24], 64), ALU.mult, t)
        t = tt(Hs[:, d, :], Hs[:, d, :], b[:, :], ALU.add)
        give(b, t)
        s_end[0] = t

    def ssd_strand():
        seen = set()
        for i in range(6):
            for d in range(2):
                b6 = ORD[d][i]
                K.wait("pe", s_end[0])
                yield from ssd_unit(d, b6, b6 not in seen)
                seen.add(b6)
                yield
        dump("ysd", ysd[:, :, :])
        t_r = None
        for i in range(4):
            t = tt(ysd[:, i, :], ysd[:, i, :], zx[:, i, :], ALU.mult)
            for g in range(2):
                src = ysd[:, i, g * 256:(g + 1) * 256]
                t = act(yo[:, g * 256:(g + 1) * 256], src, ACT.Square, t, t_r, accum=mv[:, g:g + 1])
            t = act(rstd[:, 0:2], mv[:, 0:2], ACT.Sqrt, bias=EPS5, scale=1.0 / 256)
            yield
            recip(mv[:, 0:2], rstd[:, 0:2], t)
            for g in range(2):
                t = ts(yo[:, g * 256:(g + 1) * 256], ysd[:, i, g * 256:(g + 1) * 256], mv[:, g:g + 1], None, ALU.mult, None)
            b = bank()
            for j in range(4):
                t_r = tr(b[:, j * 128:(j + 1) * 128], yo[:, j * 128:(j + 1) * 128], ident, t)
            yield
            for j in range(4):
                t2 = ts(ym[:, j, i * 128:(i + 1) * 128], b[:, j * 128:(j + 1) * 128], cc("ssd_w", j), None, ALU.mult, None, t_r)
            give(b, t2)
            yield

    g_end = [[t_gz], [t_gz]]
    gseen = set()

    def gla_unit(d, b6):
        B = GB[d]
        kde, stm, qx, sTg, cq, etot = (B[n] for n in ("kde", "stm", "qx", "sTg", "cq", "etot"))
        eq = B["eq"].rearrange("p (a t) -> p a t", a=4)
        qp = B["qp"].rearrange("p (a t) -> p a t", a=2)
        tok = slice(b6 * 128, (b6 + 1) * 128)
        la = lag[:, b6, 128 * d:128 * d + 128]
        end = g_end[d]
        b = bank()
        mm(b[:, 0:128], la, C(f"q16_{d}"), t_lag)
        mm(b[:, 128:256], la, C(f"i16_{d}"))
        mm(b[:, 256:264], la, C(f"c16_{d}"))
        t = mm(b[:, 384:512], C(f"x16_{d}"), la)
        act(eq[:, 3, :], b[:, 384:512], ACT.Exp, t, end, scale=1.0 / 16)
        t_e = act(etot, b[:, 256:264], ACT.Exp, scale=1.0 / 16)
        if b6 >= 2:
            t_e = act(eq[:, 2, :], b[:, 128:256], ACT.Exp, scale=1.0 / 16)
            t3 = ts(cq, b[:, 0:128], 640.0, -640.0, ALU.min, ALU.max, t_e)
            act(eq[:, 0, :], cq, ACT.Exp, t3, scale=1.0 / 16)
            t_q = act(eq[:, 1, :], cq, ACT.Exp, scale=-1.0 / 16)
            give(b, t3)
        else:
            give(b, t_e)
        yield
        kd = eq[:, 3, :]
        tt(kd, kd, gkv[:, b6, 0:128], ALU.mult, t_e)
        t_k = tt(kde.rearrange("p (c k) -> p c k", c=8), bcm(kd, 8), bc(C(f"c16_{d}"), 128), ALU.mult, end)
        S = Sg[:, d, :, :]
        chunks = list(range(8) if d == 0 else range(7, -1, -1))
        yield
        if b6 >= 2:
            xt_ = slice((b6 - 2) * 128, (b6 - 1) * 128)
            tt(qp[:, 0, :], gqT[:, xt_], eq[:, 0, :], ALU.mult, t_q)
            t_qp = tt(qp[:, 1, :], gkT[:, tok], eq[:, 1, :], ALU.mult)
            t_qx = tt(qx.rearrange("p (c w) -> p c w", w=144)[:, :, 0:16],
                      gqT[:, xt_].rearrange("p (c w) -> p c w", w=16),
                      eq[:, 2, :].rearrange("p (c w) -> p c w", w=16), ALU.mult)
            b = bank()
            for h in range(4):
                hs = slice(32 * h, 32 * h + 32)
                t = mm(b[:, h * 128:(h + 1) * 128], qp[hs, 1, :], qp[hs, 0, :], t_qp, after=h > 0)
            yield
            t_s = tt(sTg.rearrange("p (h t) -> p h t", h=4), b[:, :].rearrange("p (h t) -> p h t", h=4),
                     bcm(C(f"i16_{d}"), 4), ALU.mult, t)
            give(b, t_s)
            yield
        pend = []

        def kv(jj):
            b = bank()
            for q in range(2):
                c = chunks[2 * jj + q]
                t = mm(b[:, q * 256:(q + 1) * 256], kde[:, c * 128:(c + 1) * 128], gkv[:, b6, 128:384], t_k)
            pend.append((b, t))

        kv(0)
        for jj in range(4):
            if jj < 3:
                kv(jj + 1)
            yield
            b, t = pend.pop(0)
            t_m = t
            t = tt(stm.rearrange("p (a b) -> p a b", a=2), b[:, :].rearrange("p (a b) -> p a b", a=2),
                   bcm(C("bd"), 2), ALU.mult, t)
            give(b, t)
            for q in range(2):
                n_ = 2 * jj + q
                t = stt(S[:, n_ + 1, :], S[:, n_, :], etot[:, chunks[n_]:chunks[n_] + 1], stm[:, q * 256:(q + 1) * 256],
                        ALU.mult, ALU.add)
        if b6 >= 2:
            b = bank()
            for n_ in range(8):
                c = chunks[n_]
                mm(b[:, 0:256], qx[:, c * 128:(c + 1) * 128], S[:, n_, :], t_qx, t, start=(n_ == 0), stop=False)
            for h in range(4):
                t_m = mm(b[:, 64 * h:64 * h + 64], sTg[:, h * 128:(h + 1) * 128], gkv[:, b6, 128 + 64 * h:192 + 64 * h],
                         t_s, start=False, stop=(h == 3))
            yield
            o = og2[:, b6 - 2, :]
            if b6 in gseen:
                t = tt(o, o, b[:, 0:256], ALU.add, t_m)
            else:
                t = copy(o, b[:, 0:256], t_m, e="dve")
            gseen.add(b6)
            give(b, t)
        t = copy(S[:, 0, :], S[:, 8, :], t_m, e="dve")
        g_end[d] = [t]

    def gla_strand(d):
        for b6 in ORD[d]:
            yield from gla_unit(d, b6)
            yield

    run(gla_strand(0), gla_strand(1), ssd_strand())
    dump("og2", og2[:, :, :])
    sq = gt1[:, 0:2, :].rearrange("p a b -> p (a b)")
    etot = GB[0]["etot"]
    t_r = None
    for i in range(4):
        o = og2[:, i, :]
        t = act(sq[:, 0:256], o, ACT.Square, K.last("dve"), K.last("pe"))
        red(etot[:, 0:4], sq[:, 0:256].rearrange("p (h v) -> p h v", h=4), ALU.add, t)
        t = act(etot[:, 4:8], etot[:, 0:4], ACT.Sqrt, K.last("dve"), bias=EPS5, scale=1.0 / 64)
        recip(etot[:, 0:4], etot[:, 4:8], t)
        tt(sq[:, 256:512].rearrange("p (h v) -> p h v", h=4), o.rearrange("p (h v) -> p h v", h=4),
           bc(etot[:, 0:4], 64), ALU.mult, K.last("pe"))
        t = tt(sq[:, 256:512], sq[:, 256:512], ogt[:, i, :], ALU.mult)
        b = bank()
        for j in range(2):
            t2 = tr(b[:, j * 128:(j + 1) * 128], sq[:, 256 + j * 128:384 + j * 128], ident, t)
        for j in range(2):
            t = ts(ym[:, 6 + j, i * 128:(i + 1) * 128], b[:, j * 128:(j + 1) * 128], cc("gla_w", j), None, ALU.mult, None, t2)
        give(b, t)
    K.barrier()
    big[2] = K.all()
    s1.close()
    m1b.close()

    s3 = ExitStack()
    w2x = sb("w2x", [128, 512], c=s3)
    a2x = sb("a2x", [128, 512], c=s3)
    g2s = sb("g2s", [128, 256], c=s3)
    w0r = sb("w0r", [1, 512], c=s3)
    lw = sb("lw", [128, 6, 512], c=s3)
    aT = sb("aT", [128, 4, 768], c=s3)
    kkT = sb("kkT", [128, 2, 768], c=s3)
    kd_ = sb("kd_", [128, 4, 768], c=s3)
    tmp = sb("tmp", [128, 768], c=s3)
    tmp2 = sb("tmp2", [128, 768], c=s3)
    yR = sb("yR", [128, 2, 512], c=s3)
    K.wait("sp", K.all())
    tw = [K.dma("sp", lambda e: e.dma_start(w2x[:, :], A["w2x"])), K.dma("sp", lambda e: e.dma_start(a2x[:, :], A["a2x"])),
          K.dma("sp", lambda e: e.dma_start(g2s[:, :], A["g2"])),
          K.dma("sp", lambda e: e.dma_start(w0r[:, :], A["rows"][0:1, RO["w0"][0]:RO["w0"][0] + 512]))]
    act(tmp[:, :], rwm[:, 6, :], ACT.Tanh)
    t_th = K.last("act")
    for b6 in range(6):
        b = bank()
        mm(b[:, :], C("ones")[0:1, :], w0r[0:1, :], *tw, start=True, stop=False)
        t = mm(b[:, :], tmp[:, b6 * 128:(b6 + 1) * 128], w2x[:, :], t_th, start=False, stop=True)
        t = act(lw[:, b6, :], b[:, :], ACT.Sigmoid, t)
        give(b, t)
    for q in range(4):
        for lo, n_ in ((0, 512), (512, 256)):
            b = bank()
            t = mm(b[:, 0:n_], a2x[:, q * 128:(q + 1) * 128], rwm[:, 7, lo:lo + n_], *tw)
            t = act(aT[:, q, lo:lo + n_], b[:, 0:n_], ACT.Sigmoid, t, bias=cc("a0", q))
            give(b, t)
    for p in range(2):
        ts(kkT[:, p, :], rwm[:, 2 + p, :], cc("kk", p), None, ALU.mult, None)
        t = act(tmp[:, :], kkT[:, p, :], ACT.Square, K.last("dve"), K.last("pe"))
        for lo, n_ in ((0, 512), (512, 256)):
            b = bank()
            t = mm(b[:, 0:n_], C("h64"), tmp[:, lo:lo + n_], K.last("act"))
            t = act(tmp2[:, lo:lo + n_], b[:, 0:n_], ACT.Sqrt, t, K.last("dve"))
            give(b, t)
        ts(tmp2[:, :], tmp2[:, :], 1e-12, None, ALU.max, None, t)
        recip(tmp2[:, :], tmp2[:, :])
        tt(kkT[:, p, :], kkT[:, p, :], tmp2[:, :], ALU.mult)
    for q in range(4):
        p = q % 2
        ts(kd_[:, q, :], aT[:, q, :], -1.0, cc("ka", p), ALU.add, ALU.mult, K.last("act"))
        stt(kd_[:, q, :], kd_[:, q, :], 1.0, rwm[:, 2 + p, :], ALU.add, ALU.mult)
        tt(aT[:, q, :], aT[:, q, :], kkT[:, p, :], ALU.mult)
    dump("kd_", kd_[:, :, :])
    dump("lw", lw[:, :, :])
    K.barrier()
    s4 = ExitStack()
    big, scr, over = ring.take(12288)
    for e in ("dve", "act", "pool"):
        K.wait(e, over)
    spare = uT[:, :, :].rearrange("p k t -> p (k t)")[:, 4096:6144]
    Hr = sb("Hr", [128, 2, 2, 64], c=s4)
    t_H0 = memset(Hr[:, :, :, :], 0.0, e="dve")

    def rw_buffers(d):
        s_ = scr[:, 6144 * d:6144 * d + 6144]
        B = {n: s_[:, 512 * j:512 * j + 512].rearrange("p (h t) -> p h t", h=4)
             for j, n in enumerate(("ATm", "Aof", "Tm", "TT", "Xm", "BTm", "Abt", "Akt"))}
        B["OPC"] = s_[:, 4096:5120].rearrange("p (a q t) -> p a q t", a=4, q=2)
        B["OPT"] = s_[:, 5120:6144].rearrange("p (a c) -> p a c", a=4)
        B["E3"] = spare[:, 768 * d:768 * d + 768].rearrange("p (q a t) -> p q a t", q=2, a=3)
        B["BV"] = spare[:, 1536 + 256 * d:1792 + 256 * d]
        for n, w in (("U0", 256), ("SA", 256), ("TK", 256), ("Dt", 4)):
            B[n] = sb(f"{n}{d}", [128, w], c=s4)
        return B

    def v4(x):
        return x.rearrange("p (h t) -> p h t", h=4)

    def hp(h):
        return slice(64 * (h % 2), 64 * (h % 2) + 64), h // 2

    RB = [rw_buffers(d) for d in range(2)]
    r_end = [[t_H0], [t_H0]]
    yseen = set()

    def rw_unit(d, b6):
        B = RB[d]
        ATm, Aof, Tm, TT, Xm, BTm, Abt, Akt, OPC, OPT, E3, BV = (
            B[n] for n in ("ATm", "Aof", "Tm", "TT", "Xm", "BTm", "Abt", "Akt", "OPC", "OPT", "E3", "BV"))
        U0, SA = B["U0"], B["SA"]
        TK = B["TK"][:, :].rearrange("p (q t) -> p q t", q=2)
        Dt = B["Dt"][:, :].rearrange("p (c q) -> p c q", c=2)
        tok = slice(b6 * 128, (b6 + 1) * 128)
        isx = b6 >= 2
        K.wait("dve", r_end[d])
        K.wait("act", r_end[d])
        bd_ = bank()
        for p in range(2):
            l = lw[:, b6, 256 * d + 128 * p:256 * d + 128 * p + 128]
            b = bank()
            mm(b[:, 0:128], l, C(f"i64_{d}"))
            t = mm(b[:, 128:256], l, C(f"e64_{d}"))
            t2 = mm(bd_[:, 2 * p:2 * p + 2], l, C("ch64"))
            act(E3[:, p, 0:2, :].rearrange("p a b -> p (a b)"), b[:, 0:256], ACT.Exp, t, scale=-E05)
            t = act(E3[:, p, 2, :], b[:, 0:128], ACT.Exp, scale=E05)
            give(b, t)
            t_e = t
        t_D = act(Dt.rearrange("p c q -> p q c"), bd_[:, 0:4].rearrange("p (q c) -> p q c", q=2), ACT.Exp, t2, scale=-E05)
        give(bd_, t_D)
        yield
        tt(OPC[:, 1, :, :], kkT[:, :, tok], E3[:, :, 1, :], ALU.mult, t_e)
        t_c = tt(OPC[:, 2, :, :], aT[:, 2 * d:2 * d + 2, tok], E3[:, :, 2, :], ALU.mult)
        t_k = tt(OPC[:, 3, :, :], kd_[:, 2 * d:2 * d + 2, tok], E3[:, :, 2, :], ALU.mult)
        if isx:
            t_r = tt(OPC[:, 0, :, :], rwm[:, 0:2, tok], E3[:, :, 0, :], ALU.mult)
        yield

        def prod(i, j, *toks):
            b = bank()
            for h in (0, 2, 1, 3):
                ps_, q = hp(h)
                t = mm(b[:, h * 128:(h + 1) * 128], OPC[ps_, i, q, :], OPC[ps_, j, q, :], *toks, after=h == 1)
            return b, t

        def masked(bt, msk, dst):
            t = tt(dst[:, :, :], v4(bt[0][:, :]), bcm(C(msk), 4), ALU.mult, bt[1])
            give(bt[0], t)
            return t
        p1, p2 = prod(1, 2, t_c), prod(2, 1)
        masked(p1, f"l0_{1 - d}", Tm)
        stt(Tm[:, :, :], Tm[:, :, :], -1.0, bcm(ident, 4), ALU.mult, ALU.add)
        masked(p2, f"e64_{d}", ATm)
        tt(TT[:, :, :], ATm[:, :, :], bcm(C(f"l0_{d}"), 4), ALU.mult)
        t_T = stt(TT[:, :, :], TT[:, :, :], -1.0, bcm(ident, 4), ALU.mult, ALU.add)
        yield

        def side():
            nonlocal t_t, t_bv, t_A
            for a in range(2):
                b = bank()
                for q in range(2):
                    for p in range(2):
                        k = 2 * a + q
                        src = rwm[:, 4 + p, tok] if k == 0 else OPC[:, k, p, :]
                        t = tr(b[:, q * 256 + p * 128:q * 256 + (p + 1) * 128], src, ident, t_k)
                if a == 0:
                    act(OPT[:, 0, :], b[:, 0:256], ACT.Copy, t)
                    t_t = act(OPT[:, 1, :], b[:, 256:512], ACT.Copy, scale=-1.0)
                else:
                    t_t = act(OPT[:, 2:4, :].rearrange("p a b -> p (a b)"), b[:, :], ACT.Copy, t)
                give(b, t_t)
                yield
            t_B = masked(prod(3, 1, t_k), f"e64_{d}", BTm)
            yield
            b = bank()
            for h in range(4):
                t = mm(b[:, 64 * h:64 * h + 64], BTm[:, h, :], OPT[:, 0, 64 * h:64 * h + 64], t_B, t_t)
            t_bv = act(BV[:, :], b[:, 0:256], ACT.Copy, t, scale=-1.0)
            give(b, t_bv)
            yield
            if isx:
                masked(prod(2, 0, t_r), f"i64_{d}", Abt)
                t_A = masked(prod(3, 0), f"i64_{d}", Akt)
            yield
        t_t = t_bv = t_A = None
        beside = side()
        t_m = None
        for k in range(1, 6):
            t_a = tt(Aof[:, :, :], ATm[:, :, :], bcm(C(f"l{k}_{d}"), 4), ALU.mult, t_m)
            b = bank()
            for h in range(4):
                t_m = mm(b[:, h * 128:(h + 1) * 128], Aof[:, h, :], Tm[:, h, :], t_a, t_T)
            t_X = act(Xm[:, :, :], v4(b[:, :]), ACT.Copy, t_m)
            give(b, t_X)
            next(beside)
            yield
            b2 = bank()
            for h in range(4):
                t2 = mm(b2[:, h * 128:(h + 1) * 128], Xm[:, h, :], TT[:, h, :], t_X)
            if k < 5:
                b = bank()
                for h in range(4):
                    t1 = mm(b[:, h * 128:(h + 1) * 128], TT[:, h, :], Xm[:, h, :])
                t = tt(Tm[:, :, :], Tm[:, :, :], v4(b[:, :]), ALU.subtract, t1)
                give(b, t)
            t_T = tt(TT[:, :, :], TT[:, :, :], v4(b2[:, :]), ALU.subtract, t2)
            give(b2, t_T)
            t_m = [t_m, t2]
            yield
        b = bank()
        for h in range(4):
            t = mm(b[:, 64 * h:64 * h + 64], TT[:, h, :], BV[:, 64 * h:64 * h + 64], t_T, t_bv)
        for h in range(4):
            ps_, q = hp(h)
            t = mm(b[ps_, 256 + q * 128:384 + q * 128], OPT[:, 1, 64 * h:64 * h + 64], TT[:, h, :], t_t)
        act(U0[:, :], b[:, 0:256], ACT.Copy, t)
        t_u0 = act(TK.rearrange("p a b -> p (a b)"), b[:, 256:512], ACT.Copy)
        give(b, t_u0)
        yield
        by = bank() if isx else None
        t_H, t_y = r_end[d][0], None
        for ch in ((0, 1) if d == 0 else (1, 0)):
            cs = slice(64 * ch, 64 * ch + 64)
            b = bank()
            for h in (0, 2, 1, 3):
                ps_, q = hp(h)
                t = mm(b[cs, 64 * h:64 * h + 64], TK[ps_, q, cs], Hr[ps_, d, q, :], t_H, t_u0, after=h == 1)
            t_sa = tt(SA[cs, :], b[cs, 0:256], U0[cs, :], ALU.add, t)
            give(b, t_sa)
            b = bank()
            for h in range(4):
                ps_, q = hp(h)
                o = b[ps_, q * 64:q * 64 + 64]
                mm(o, OPT[cs, 3, 64 * h:64 * h + 64], OPT[cs, 0, 64 * h:64 * h + 64], start=True, stop=False)
                t = mm(o, OPT[cs, 2, 64 * h:64 * h + 64], SA[cs, 64 * h:64 * h + 64], t_sa, start=False, stop=True)
            if isx:
                for h in range(4):
                    ps_, q = hp(h)
                    o = by[ps_, q * 128 + 64 * ch:q * 128 + 64 * ch + 64]
                    mm(o, Hr[ps_, d, q, :], OPC[ps_, 0, q, cs], start=True, stop=False, after=True)
                    mm(o, SA[cs, 64 * h:64 * h + 64], Abt[cs, h, cs], t_sa, t_A, start=False, stop=False, after=True)
                    t_y = mm(o, OPT[cs, 0, 64 * h:64 * h + 64], Akt[cs, h, cs], start=False, stop=True)
            t = tt(Hr[:, d, :, :], Hr[:, d, :, :], b[:, 0:128].rearrange("p (q v) -> p q v", q=2), ALU.add, t, t_y, t_D)
            give(b, t)
            t_H = tt(Hr[:, d, :, :], Hr[:, d, :, :], bc(Dt[:, ch, :], 64), ALU.mult)
            yield
        r_end[d] = [t_H, t, t_y]
        if isx:
            o = yR[:, :, (b6 - 2) * 128:(b6 - 1) * 128]
            src = by[:, 0:256].rearrange("p (q t) -> p q t", q=2)
            t = tt(o, o, src, ALU.add, t_y) if b6 in yseen else copy(o, src, t_y)
            yseen.add(b6)
            give(by, t)

    def rw_strand(d):
        for b6 in ORD[d]:
            yield from rw_unit(d, b6)

    adaD = nc.dram_tensor("ada_rows", (4, D), F32, kind="Internal").ap()
    adaw = sb("adaw", [128, 1024], c=s4)
    ents_a = [[adaw[:, :], []], [rwm[:, 6:8, :].rearrange("p a b -> p (a b)")[:, 0:1024], []]]
    t_ada = []

    def ada_strand():
        mrow, brow = tmp[0:2, 0:512], tmp2[0:1, 0:512]
        t_st = t_pe = None
        for sec in range(2, 6):
            for h in range(2):
                w = sec * D + h * 512
                tb = K.dma("sp", lambda e, w=w: e.dma_start(brow, A["ada_b"][0:1, w:w + 512]), t_pe)

                def load(c, w=w):
                    buf, rd = ents_a[c % 2]
                    src = A["ada_w"][:, w + c * 128:w + c * 128 + 128].rearrange("(k p) n -> p k n", p=128)
                    return K.dma("sp", lambda e: e.dma_start(buf.rearrange("p (k n) -> p k n", k=8), src), rd)
                tk = [load(0), load(1)]
                yield
                b = bank()
                for c in range(4):
                    buf = ents_a[c % 2][0]
                    o = b[0:2, c * 128:(c + 1) * 128]
                    mm(o, C("ones")[0:1, 0:2], brow[:, c * 128:(c + 1) * 128], tb, tk[c], start=True, stop=False)
                    for k in range(8):
                        t_pe = mm(o, scv[:, k, :], buf[:, k * 128:(k + 1) * 128], start=False, stop=(k == 7))
                    ents_a[c % 2][1] = [t_pe]
                    if c < 2:
                        tk.append(load(c + 2))
                    yield
                    yield
                t = act(mrow, b[0:2, :], ACT.Identity, t_pe, t_st, bias=1.0 if sec == 4 else 0.0)
                give(b, t)
                t_st = K.dma("sp", lambda e, sec=sec, h=h: e.dma_start(adaD[sec - 2:sec - 1, h * 512:(h + 1) * 512], mrow[0:1, :]), t)
                t_ada.append(t_st)

    K.wait("sp", K.all())
    run(rw_strand(0), rw_strand(1), ada_strand())
    for e in ("act", "dve"):
        K.wait(e, t_ada)
    K.barrier()
    big[2] = K.all()
    s4.close()
    dump("yR", yR[:, :, :])
    t5 = tmp[:, 0:512]
    t6 = tmp2[:, 0:512]
    X = slice(256, 768)
    for p in range(2):
        y = yR[:, p, :]
        b = bank()
        t = mm(b[:, :], C("h64"), y, K.last("dve"))
        t = stt(y, b[:, :], -1.0 / 64, y, ALU.mult, ALU.add, t)
        give(b, t)
        t = act(t5, y, ACT.Square, t, K.last("pe"))
        b = bank()
        t = mm(b[:, :], C("h64"), t5, t)
        t = act(t6, b[:, :], ACT.Sqrt, t, bias=EPS64, scale=1.0 / 64)
        give(b, t)
        recip(t6, t6, t)
        tt(y, y, t6, ALU.mult)
        ts(y, y, cc("lnw", p), cc("lnb", p), ALU.mult, ALU.add)
        tt(t6, kd_[:, p, X], kd_[:, 2 + p, X], ALU.add)
        stt(t5, rwm[:, p, X], cc("rk", p), t6, ALU.mult, ALU.mult, K.last("pe"))
        b = bank()
        t = mm(b[:, :], C("h64"), t5, K.last("dve"))
        t = tt(t6, b[:, :], rwm[:, 4 + p, X], ALU.mult, t)
        give(b, t)
        tt(y, y, t6, ALU.add)
        if p == 0:
            t_s = act(aT[:, 0, 0:512], rwm[:, 8, X], ACT.Sigmoid, K.last("dve"))
        b = bank()
        t = mm(b[:, :], g2s[:, p * 128:(p + 1) * 128], aT[:, 0, 0:512], t_s)
        t = tt(ym[:, 4 + p, :], y, b[:, :], ALU.mult, t)
        give(b, t)
    dump("ym", ym[:, :, :])
    K.barrier()
    s3.close()
    m1.close()
    g12 = sb("g12", [128, 4, D], c=b1)
    K.wait("sp", K.all())
    for r, j in ((0, 0), (3, 1), (1, 2), (2, 3)):
        t_g12 = K.dma("sp", lambda e, r=r, j=j: e.dma_start(g12[:, j, :], adaD[r:r + 1, :].to_broadcast([128, D])), t_ada)
        if j == 0:
            K.wait("dve", t_g12)

    m2 = ExitStack()
    hD = nc.dram_tensor("h_rows", (512, D), F32, kind="Internal").ap()
    yD = nc.dram_tensor("y_rows", (4096, D), F32, kind="Internal").ap()
    t_hds = []
    hT = sb("hT", [128, 8, 512], c=m2)
    w8 = sb("w8", [128, 4, 8], c=m2)
    msk = sb("msk", [128, 4, 64], c=m2)
    idx = sb("idx", [128, 96, 2], I32, c=m2)
    ovi = sb("ovi", [1, 33], I32, c=m2)
    fac = sb("fac", [128, 4, D], c=m2)
    wtok = sb("wtok", [128, 4, 64], c=m2)
    m3 = ExitStack()
    lnr = sb("lnr", [128, 4, D], c=m3)
    xn = sb("xn2", [128, 2, D], c=m3)
    rwt = sb("rwt", [128, 8, 64], c=m3)
    rb = sb("rb", [128, 64], c=m3)
    sel = sb("sel", [128, 64], c=m3)
    sco = sb("sco", [128, 64], c=m3)
    m8 = sb("m8", [128, 8, 8], c=m3)
    gs = sb("gs", [128, 32], c=m3)
    K.wait("sp", K.all())
    tl = [rowload(lnr[:, 0, :], "ln1w"), rowload(lnr[:, 1, :], "ln1b"),
          K.dma("sp", lambda e: e.dma_start(rwt[:, :, :], A["router_w"].rearrange("(k p) n -> p k n", p=128))),
          rowload(rb[:, :], "rb")]

    ents = []
    for hf in range(2):
        ent, wap, tk = ring.load([(0, 4096, 8, A["w_out"][:, hf * 512:(hf + 1) * 512].rearrange("(k p) n -> p k n", p=128))], 4096)
        wv = wap.rearrange("p (k n) -> p k n", k=8)
        for i in range(4):
            b = bank()
            for k in range(8):
                t = mm(b[:, :], ym[:, k, i * 128:(i + 1) * 128], wv[:, k, :], tk, start=(k == 0), stop=(k == 7))
            hs = slice(hf * 512, (hf + 1) * 512)
            tmpv = xn[:, 0, hs]
            t = tt(tmpv, b[:, :], g12[:, 0, hs], ALU.mult, t)
            give(b, t)
            stt(xt[:, i, hs], xt[:, i, hs], ALPHA, tmpv, ALU.mult, ALU.add)
        ent[2] = K.last("pe")

    def layer_norm(x, w, bb, *toks):
        ln_stats(x, *toks)
        ts(x, x, mv[:, 0:1], rstd[:, 0:1], ALU.subtract, ALU.mult)
        tt(x, x, w, ALU.mult, *toks)
        return tt(x, x, bb, ALU.add)

    xnt = [None, None]
    for i in range(4):
        layer_norm(xt[:, i, :], lnr[:, 0, :], lnr[:, 1, :], *tl)
        ln_stats(xt[:, i, :])
        ts(xn[:, i % 2, :], xt[:, i, :], mv[:, 0:1], rstd[:, 0:1], ALU.subtract, ALU.mult, xnt[i % 2])
        tt(xn[:, i % 2, :], xn[:, i % 2, :], g12[:, 3, :], ALU.mult, t_g12)
        tn = tt(xn[:, i % 2, :], xn[:, i % 2, :], g12[:, 2, :], ALU.add)
        t_hd = K.dma("sp", lambda e, i=i, xn=xn: e.dma_start(hD[i * 128:(i + 1) * 128, :], xn[:, i % 2, :]), tn)
        t_hds.append(t_hd)
        for hf in range(2):
            b = bank()
            for k in range(4):
                t = tr(b[:, k * 128:(k + 1) * 128], xn[:, i % 2, (hf * 4 + k) * 128:(hf * 4 + k + 1) * 128], ident, tn)
            xnt[i % 2] = [t, t_hd]
            t2 = act(hT[:, hf * 4:hf * 4 + 4, i * 128:(i + 1) * 128], v4(b[:, :]), ACT.Copy, t)
            give(b, t2)
    t_h = K.last("act")
    dump("x1", xt[:, :, :])
    dump("hT", hT[:, :, :])
    for i in range(4):
        b = bank()
        for k in range(8):
            t = mm(b[:, 0:64], hT[:, k, i * 128:(i + 1) * 128], rwt[:, k, :], t_h, *tl, start=(k == 0), stop=(k == 7))
        t = act(sco[:, :], b[:, 0:64], ACT.Sigmoid, t, K.last("dve"))
        give(b, t)
        tt(sel[:, :], sco[:, :], rb[:, :], ALU.add, t, *tl)
        for g in range(8):
            max8(m8[:, g, :], sel[:, 8 * g:8 * g + 8])
        tt(gs[:, 0:8], m8[:, :, 0], m8[:, :, 1], ALU.add)
        max8(gs[:, 8:16], gs[:, 0:8])
        ts(gs[:, 16:24], gs[:, 0:8], gs[:, 11:12], None, ALU.is_ge, None)
        ts(gs[:, 24:32], gs[:, 16:24], -1.0, 1e30, ALU.add, ALU.mult)
        s3_ = sel[:, :].rearrange("p (g e) -> p g e", g=8)
        tt(s3_, s3_, bc(gs[:, 16:24], 8), ALU.mult)
        tt(s3_, s3_, bc(gs[:, 24:32], 8), ALU.add)
        max8(gs[:, 8:16], sel[:, :])
        strike(sel[:, :], gs[:, 8:16], sel[:, :])
        ts(msk[:, i, :], sel[:, :], -2e38, None, ALU.is_lt, None)
        tt(sel[:, :], msk[:, i, :], sco[:, :], ALU.mult)
        red(gs[:, 0:1], sel[:, :], ALU.add)
        recip(gs[:, 1:2], gs[:, 0:1])
        ts(wtok[:, i, :], sel[:, :], gs[:, 1:2], 2.5, ALU.mult, ALU.mult)
    dump("wtok", wtok[:, :, :])
    K.barrier()
    for e in K.sem:
        K.wait(e, t_hds)
    m3.close()

    hid = sb("hid", [128, 2, 512], c=m2)
    gsl = sb("gsl", [128, 2, 512], c=m2)
    sh_ent, sh_wap, sh_tk = ring.load([(0, 6144, 0, A["sw"])], 6144)
    first_w = [ring.load([(0, n, 0, A["ew"][0][:, lo:lo + n])], n) for lo, n in ((0, 4096), (4096, 2048))]

    def shared():
        wv = sh_wap[:, 0:4096].rearrange("p (k n) -> p k n", k=8)
        w2 = sh_wap[:, 4096:6144].rearrange("p (k n) -> p k n", k=2)
        for f in range(2):
            b = bank()
            for k in range(8):
                t = mm(b[:, :], wv[:, k, f * 128:(f + 1) * 128], hT[:, k, :], sh_tk, t_h, start=(k == 0), stop=(k == 7))
                if k % 2:
                    yield
            b2 = bank()
            for k in range(8):
                t2 = mm(b2[:, :], wv[:, k, 256 + f * 128:384 + f * 128], hT[:, k, :], start=(k == 0), stop=(k == 7))
                if k % 2:
                    yield
            t = act(gsl[:, f, :], b[:, :], ACT.Silu, t)
            give(b, t)
            t = tt(hid[:, f, :], gsl[:, f, :], b2[:, :], ALU.mult, t, t2)
            give(b2, t)
            yield
        t_h2 = t
        for i in range(4):
            for n_ in range(2):
                b = bank()
                for f in range(2):
                    t = mm(b[:, :], hid[:, f, i * 128:(i + 1) * 128], w2[:, f, n_ * 512:(n_ + 1) * 512], t_h2, start=(f == 0), stop=(f == 1))
                t = copy(fac[:, i, n_ * 512:(n_ + 1) * 512], b[:, :], t, e="act")
                give(b, t)
                yield
        sh_ent[2] = K.last("pe")

    BIG = 1048576.0
    m4 = ExitStack()
    BF = mybir.dt.bfloat16
    rk = sb("rk", [128, 4, 96], c=m4)
    jr = sb("jr", [128, 4, 64], c=m4)
    val = sb("val", [128, 4, 96, 4], BF, c=m4)
    eT = sb("eT", [64, 2, 512], c=m4)
    ot = sb("ot", [64, 3, 32], c=m4)
    nb = sb("nb", [64, 8], c=m4)
    Pm = sb("Pm", [128, 2, 4, 8, 128], BF, c=m4)
    ixf = sb("ixf", [128, 96, 2], c=m4)
    j8 = sb("j8", [128, 8, 64], c=m4)
    iota = C("iota")
    b = bank()
    for i in range(4):
        for i2 in range(i):
            mm(b[:, 64 * i:64 * i + 64], C("ones"), msk[:, i2, :], K.last("dve"), start=(i2 == 0), stop=False)
        t = mm(b[:, 64 * i:64 * i + 64], C("g128_1"), msk[:, i, :], K.last("dve"), start=(i == 0), stop=True)
    mf = msk[:, :, :]
    sh = shared()
    next(sh)
    ts(rk[:, :, 0:64], mf, -BIG, BIG, ALU.mult, ALU.add)
    t = tt(rk[:, :, 0:64], rk[:, :, 0:64], b[:, 0:256].rearrange("p (i e) -> p i e", i=4), ALU.add, t)
    give(b, t)
    for i in range(4):
        op("dve", lambda g, i=i: g.tensor_tensor_scan(jr[:, i, :], C("one8"), msk[:, i, :], 0.0, ALU.mult, ALU.add))
    tt(jr[:, :, :], jr[:, :, :], mf, ALU.subtract)
    for i in range(4):
        tt(j8[:, :, :], bcm(jr[:, i, :], 8), bc(iota[:, 0:8], 64), ALU.is_equal)
        tt(j8[:, :, :], j8[:, :, :], bcm(wtok[:, i, :], 8), ALU.mult)
        red(w8[:, i, :], j8[:, :, :], ALU.add)
    next(sh)
    b = bank()
    for i in range(4):
        t = mm(b[0:64, 0:1], msk[:, i, :], C("ones")[:, 0:1], start=(i == 0), stop=(i == 3))
    ts(nb[:, 0:1], b[0:64, 0:1], 128.5, None, ALU.is_gt, None, t)
    ts(nb[:, 1:2], b[0:64, 0:1], 256.5, None, ALU.is_gt, None)
    t = ts(nb[:, 2:3], b[0:64, 0:1], 384.5, None, ALU.is_gt, None)
    give(b, t)
    tt(nb[:, 3:4], nb[:, 0:1], nb[:, 1:2], ALU.add)
    t = tt(nb[:, 3:4], nb[:, 3:4], nb[:, 2:3], ALU.add)
    b = bank()
    t = mm(b[0:64, 0:1], C("tri64")[0:64, :], nb[:, 3:4], t)
    t = copy(nb[:, 4:5], b[0:64, 0:1], t)
    give(b, t)
    tt(nb[:, 5:6], nb[:, 4:5], nb[:, 3:4], ALU.add)
    O = ot[:, 0, :]
    i32_ = iota[0:64, 0:32]
    ts(O, i32_, nb[:, 4:5], None, ALU.is_ge, None)
    ts(ot[:, 1, :], i32_, nb[:, 5:6], None, ALU.is_lt, None)
    tt(O, O, ot[:, 1, :], ALU.mult)
    ts(ot[:, 1, :], i32_, nb[:, 4:5], 1.0, ALU.subtract, ALU.add)
    stt(ot[:, 1, :], ot[:, 1, :], -128.0, O, ALU.mult, ALU.mult)
    t_O = K.last("dve")
    b = bank()
    mm(b[0:1, 0:32], C("ii")[0:64, :], O, t_O)
    t = mm(b[0:1, 32:33], nb[:, 3:4], C("ones")[0:64, 0:1])
    t_ov = copy(ovi[0:1, :], b[0:1, 0:33], t)
    give(b, t_ov)
    for q, src in enumerate((rk[:, :, 0:64], jr[:, :, :])):
        b = bank()
        for i in range(4):
            t = tr(b[0:64, i * 128:(i + 1) * 128], src[:, i, :], ident, t_O)
        t = copy(eT[:, q, :], b[0:64, :], t, e="act")
        give(b, t)
    b = bank()
    for i in range(4):
        mm(b[:, 32 * i:32 * i + 32], eT[:, 0, i * 128:(i + 1) * 128], O, t, start=True, stop=False)
        t1 = mm(b[:, 32 * i:32 * i + 32], C("ones")[0:64, :], ot[:, 1, :], start=False, stop=True)
    for i in range(4):
        t2 = mm(b[:, 128 + 32 * i:160 + 32 * i], eT[:, 1, i * 128:(i + 1) * 128], O)
    copy(rk[:, :, 64:96], b[:, 0:128].rearrange("p (i e) -> p i e", i=4), t2)
    copy(val[:, :, 64:96, 2], b[:, 128:256].rearrange("p (i e) -> p i e", i=4))
    copy(val[:, :, 0:64, 2], jr[:, :, :])
    t = K.last("dve")
    give(b, t)
    memset(val[:, :, :, 3], 1.0, e="dve")
    for i in range(4):
        memset(val[:, i, :, 0], float(i), e="dve")
        ts(val[:, i, :, 1], iota[:, 0:96], 0.0, C("ii"), ALU.mult, ALU.add)
    t_val = K.last("dve")
    bi_ = bank()
    pmr = [None] * 2
    for n0 in range(0, 96, 8):
        q = n0 // 8 % 2
        for i in range(4):
            t_p = tt(Pm[:, q, i, :, :], bcm(iota, 8), bc(rk[:, i, n0:n0 + 8], 128), ALU.is_equal, pmr[q])
            if n0:
                next(sh, None)
        for n_ in range(n0, n0 + 8):
            for i in range(4):
                t = mm(bi_[:, 4 * n_:4 * n_ + 4], Pm[:, q, i, n_ - n0, :], val[:, i, n_, :], t_p, t_val, start=(i == 0), stop=(i == 3))
        pmr[q] = t
    for _ in sh:
        pass
    R4 = bi_[:, 0:384].rearrange("p (b c) -> p b c", c=4)
    off = sb("off", [128, 96], c=m4)
    cvi = sb("cvi", [128, 96, 4], c=m4)
    t = copy(cvi[:, :, :], R4, t)
    give(bi_, t)
    ts(off[:, :], cvi[:, :, 3], -BIG, BIG, ALU.mult, ALU.add)
    stt(ixf[:, :, 0], cvi[:, :, 0], 128.0, cvi[:, :, 1], ALU.mult, ALU.add)
    stt(ixf[:, :, 1], ixf[:, :, 0], 8.0, cvi[:, :, 2], ALU.mult, ALU.add)
    tt(ixf[:, :, :], ixf[:, :, :], bc(off[:, :], 2), ALU.add)
    t_ix = copy(idx[:, :, :], ixf[:, :, :])
    dump("idx", ixf[:, :, :])
    K.barrier()
    m4.close()

    m4 = ExitStack()
    hg = sb("hg", [128, 3, D], c=m4)
    hgT = sb("hgT", [128, 2, 8, 128], c=m4)
    hd2 = sb("hd2", [128, 2, 256], c=m4)
    hdT = sb("hdT", [128, 2, 2, 128], c=m4)
    sl = sb("sl", [128, 2, 256], c=m4)
    yb = sb("yb", [128, 3, D], c=m4)
    t_hg = memset(hg[:, :, :], 0.0)
    K.wait("pool", t_hds, t_ix, t_hg)

    def block(n_, load_w, st):
        g3, g2 = n_ % 3, n_ % 2
        t_g = K.dma("pool", lambda e: e.indirect_dma_start(
            out=hg[:, g3, :], out_offset=None, in_=hD, in_offset=bass.IndirectOffsetOnAxis(ap=idx[:, n_, 0:1], axis=0),
            bounds_check=511, oob_is_err=False), st["hg"][g3])
        yield
        for q in range(2):
            b = bank()
            for k in range(4):
                t = tr(b[:, k * 128:(k + 1) * 128], hg[:, g3, (q * 4 + k) * 128:(q * 4 + k + 1) * 128], ident, t_g, t_hg)
            t2 = copy(hgT[:, g2, 4 * q:4 * q + 4, :], v4(b[:, :]), t, st["hgT"][g2], e="act" if q else "dve")
            if q == 0:
                ta = t2
            give(b, t2)
        st["hg"][g3] = t
        yield
        e1, wa, tk1 = load_w(0, 4096)
        wv = wa.rearrange("p (k n) -> p k n", k=8)
        b = bank()
        for k in range(8):
            t = mm(b[:, :], hgT[:, g2, k, :], wv[:, k, :], ta, t2, tk1, start=(k == 0), stop=(k == 7))
        e1[2] = t
        st["hgT"][g2] = t
        t3 = act(sl[:, g2, :], b[:, 0:256], ACT.Silu, t, st["sl"][g2])
        t4 = tt(hd2[:, g2, :], sl[:, g2, :], b[:, 256:512], ALU.mult, t3, st["hd2"][g2])
        st["sl"][g2] = t4
        give(b, t4)
        yield
        b = bank()
        for q in range(2):
            t = tr(b[:, q * 128:(q + 1) * 128], hd2[:, g2, q * 128:(q + 1) * 128], ident, t4)
        st["hd2"][g2] = t
        t = act(hdT[:, g2, :, :], b[:, 0:256].rearrange("p (q s) -> p q s", q=2), ACT.Copy, t, st["hdT"][g2])
        give(b, t)
        yield
        e2, wb, tk2 = load_w(4096, 2048)
        w2 = wb.rearrange("p (k n) -> p k n", k=2)
        te = []
        for q in range(2):
            b = bank()
            for k in range(2):
                t5 = mm(b[:, :], hdT[:, g2, k, :], w2[:, k, q * 512:(q + 1) * 512], t, tk2, start=(k == 0), stop=(k == 1))
            t6 = copy(yb[:, g3, q * 512:(q + 1) * 512], b[:, :], t5, st["yb"][g3], e="act" if q else "dve")
            te.append(t6)
            give(b, t6)
        e2[2] = t5
        st["hdT"][g2] = t5
        t_s = K.dma("pool", lambda e: e.indirect_dma_start(
            out=yD, out_offset=bass.IndirectOffsetOnAxis(ap=idx[:, n_, 1:2], axis=0), in_=yb[:, g3, :], in_offset=None,
            bounds_check=4095, oob_is_err=False), *te)
        st["yb"][g3] = t_s
        st["all"].append(t_s)
        yield

    def fresh():
        return {"hg": [None] * 3, "hgT": [None] * 2, "sl": [None] * 2, "hd2": [None] * 2, "hdT": [None] * 2,
                "yb": [None] * 3, "all": []}

    def static_w(e):
        return lambda lo, n: first_w.pop(0) if e == 0 else ring.load([(0, n, 0, A["ew"][e][:, lo:lo + n])], n)

    st = fresh()
    live = []
    for n_ in range(64 + 4):
        for g in list(live):
            if next(g, "end") == "end":
                live.remove(g)
        if n_ < 64:
            g = block(n_, static_w(n_), st)
            next(g)
            live.append(g)
    for g in live:
        for _ in g:
            pass
    K.barrier(("pe", "act", "dve", "pool", "sp"))
    for e in K.q:
        K.wait(e, t_ov, st["all"])
    nreg = {}

    def load_n(e):
        def f(eng):
            nreg[e] = eng.alloc_register("over_" + e)
            eng.reg_load(nreg[e], ovi[0:1, 32:33])
        K.q[e].append(f)
    for e in K.q:
        load_n(e)
    ent, scr, over = ring.take(6144)
    K.wait("sp", over)
    mfree = free[:]
    for i in range(32):
        K.part("ov")
        free[:] = [(b, None) for b in banks]

        def dyn_w(lo, n, i=i, scr=scr):
            def f(eng):
                v = eng.value_load(ovi[0:1, i:i + 1], min_val=0, max_val=63)
                return eng.dma_start(scr[:, lo:lo + n], A["ew"][bass.ds(v, 1), :, lo:lo + n].rearrange("o p n -> p (o n)"))
            return [0, 0, None], scr[:, lo:lo + n], [K.dma("sp", f)]
        so = fresh()
        for _ in block(64 + i, dyn_w, so):
            pass
        for e in K.q:
            K.wait(e, K.all(), so["all"])
        K.part_end(lambda e, eng, i=i: eng.If_cmp(nreg[e], i, "IS_GT"))
    free[:] = mfree
    ent[2] = K.all()
    K.barrier()
    m4.close()
    m4 = ExitStack()
    yr = sb("yr", [128, 2, 4, D], c=m4)
    yv = yD.rearrange("(i p j) d -> i p j d", p=128, j=8)
    yt = [None, None]
    for i in range(4):
        for q in range(2):
            t = K.dma("sp", lambda e, i=i, q=q: e.dma_start(yr[:, q, :, :], yv[i, :, 4 * q:4 * q + 4, :]), yt[q])
            for j in range(4):
                t2 = stt(fac[:, i, :], yr[:, q, j, :], w8[:, i, 4 * q + j:4 * q + j + 1], fac[:, i, :], ALU.mult, ALU.add, t)
            yt[q] = t2
    dump("fac", fac[:, :, :])
    K.barrier()
    m4.close()
    m5 = ExitStack()
    lnr = sb("lnr2", [128, 2, D], c=m5)
    tl = [rowload(lnr[:, 0, :], "ln2w", K.all()), rowload(lnr[:, 1, :], "ln2b", K.all())]
    for i in range(4):
        tt(fac[:, i, :], fac[:, i, :], g12[:, 1, :], ALU.mult)
        stt(xt[:, i, :], xt[:, i, :], ALPHA, fac[:, i, :], ALU.mult, ALU.add)
        layer_norm(xt[:, i, :], lnr[:, 0, :], lnr[:, 1, :], *tl)
    dump("x2", xt[:, :, :])
    K.barrier()
    m5.close()
    m2.close()

    b1.close()
    m6 = ExitStack()
    xn = sb("xn3", [128, D], c=m6)
    lamr = sb("lamr", [128, 512], c=m6)
    lms = sb("lms", [128, 8], c=m6)
    t_lam = rowload(lamr[:, :], "lam", K.all())
    gsc = sb("gsc", [128, 2], c=m6)
    for l in range(2):
        t = ts(gsc[:, l:l + 1], cc("g_sub", l), 1.0 - (0.8 - 0.6 * float(np.exp(-0.3 * l))), None, ALU.mult, None)
    K.wait("act", t)
    for l in range(2):
        for q in range(2):
            a = lamr[:, l * 256 + q * 128:l * 256 + q * 128 + 64]
            b_ = lamr[:, l * 256 + q * 128 + 64:l * 256 + q * 128 + 128]
            tt(a, a, b_, ALU.mult, t_lam)
            red(lms[:, 2 * q:2 * q + 1], a, ALU.add)
        act(lms[:, 4:5], lms[:, 0:1], ACT.Exp, K.last("dve"))
        act(lms[:, 5:6], lms[:, 2:3], ACT.Exp)
        li = 0.8 - 0.6 * float(np.exp(-0.3 * l))
        tt(lms[:, 6 + l:7 + l], lms[:, 5:6], lms[:, 4:5], ALU.subtract, K.last("act"))
        ts(lms[:, 6 + l:7 + l], lms[:, 6 + l:7 + l], -li, None, ALU.add, None)

    def rms_rows(x, *toks):
        act(xn[:, :], x, ACT.Square, K.last("dve"), K.last("pe"), *toks, accum=mv[:, 0:1])
        act(rstd[:, 1:2], mv[:, 0:1], ACT.Sqrt, bias=EPS6, scale=1.0 / D)
        return recip(rstd[:, 0:1], rstd[:, 1:2], K.last("act"))

    R32 = mybir.dt.float32r

    def f(ap):
        return ap.bitcast(F32)

    def split(h, lo, x, *toks, gain=None):
        kw = {} if gain is None else {"scale": gain}
        t = act(h, x, ACT.Copy, *toks, **kw)
        if gain is None:
            return tt(lo, x, f(h), ALU.subtract, t, *toks)
        return stt(lo, x, gain, f(h), ALU.mult, ALU.subtract, t, *toks)

    def mm3(o, l, r, *toks, start=True, stop=True):
        mm(o, l[0], r[0], *toks, start=start, stop=False)
        mm(o, l[0], r[1], start=False, stop=False)
        return mm(o, l[1], r[0], start=False, stop=stop)

    def split_w(wr, wv, tk):
        k, n_ = wv.shape[1:]
        e2, ap, over = wr.take(2 * k * n_)
        v = [ap[:, j * k * n_:(j + 1) * k * n_].rearrange("p (k n) -> p k n", k=k) for j in range(2)]
        t = split(v[0], v[1], wv, tk, over)
        return e2, v, t

    def split_items(wr, loads):
        for load, views in loads:
            box = []
            for n_, view in enumerate(views):
                def item(load=load, view=view, box=box, last=(n_ == len(views) - 1)):
                    if not box:
                        box.append(load())
                    ent, wap, tk = box[0]
                    e2, w2_, tw_ = split_w(wr, view(wap), tk)
                    if last:
                        ent[2] = tw_
                    return e2, w2_, tw_
                yield item

    def rms_T(gname, l, hT, xb):
        xs = [xn[:, :], xb]
        rd = [None, None]
        t_in = [K.last("dve"), K.last("pe")]
        tns = []

        def norm(i):
            x, q = xs[i % 2], i % 2
            act(x, xt[:, i, :], ACT.Square, rd[q], t_in, accum=mv[:, q:q + 1])
            t = act(rstd[:, 2 + q:3 + q], mv[:, q:q + 1], ACT.Sqrt, bias=EPS6, scale=1.0 / D)
            t = recip(rstd[:, q:q + 1], rstd[:, 2 + q:3 + q], t)
            tns.append(ts(x, xt[:, i, :], rstd[:, q:q + 1], None, ALU.mult, None))

        norm(0)
        for i in range(4):
            x, qs = xs[i % 2], slice(i * 128, (i + 1) * 128)
            bs = []
            for hf in range(2):
                b = bank()
                for k in range(4):
                    t = tr(b[:, k * 128:(k + 1) * 128], x[:, (hf * 4 + k) * 128:(hf * 4 + k + 1) * 128], ident, tns[i])
                bs.append((b, t))
            rd[i % 2] = t
            if i < 3:
                norm(i + 1)
            for hf, (b, t) in enumerate(bs):
                for k in range(4):
                    kk = hf * 4 + k
                    t1 = act(hT[0][:, kk, qs], b[:, k * 128:(k + 1) * 128], ACT.Copy, t, scale=cc(gname, l * 8 + kk))
                for k in range(4):
                    kk = hf * 4 + k
                    t2 = stt(hT[1][:, kk, qs], b[:, k * 128:(k + 1) * 128], cc(gname, l * 8 + kk), f(hT[0][:, kk, qs]),
                             ALU.mult, ALU.subtract, t1)
                give(b, t2)
        return K.last("dve")

    for l in range(2):
        at = ExitStack()
        qT = sb(f"qT{l}", [128, 16, 512], c=at)
        iT = sb(f"iT{l}", [128, 3, 512], c=at)
        vt = sb(f"vt{l}", [128, 4, 1024], c=at)
        iw = sb(f"iw{l}", [128, 4, 8], c=at)
        r1 = sb(f"r1{l}", [128, 2, 512], c=at)
        a1 = ExitStack()
        rope = sb(f"rope{l}", [128, 4, 512], c=a1)
        t_rope = K.dma("sp", lambda e, rope=rope: e.dma_start(rope[:, :, :], A["rope"]), K.all())
        hT = [sb(f"hT{l}{q}", [128, 8, 512], R32, c=a1) for q in "hl"]
        r2 = sb(f"r2{l}", [128, 2, 512], c=a1)
        wr = Ring(K, sb(f"wr{l}", [128, 4096], R32, c=a1), 4096)
        W2 = A["w_in_2"][l]

        def wl2(c0, n_):
            def load():
                ent, wap, tk = ring.load([(0, 8 * n_, 8, W2[:, c0:c0 + n_].rearrange("(k p) n -> p k n", p=128))], 8 * n_)
                return ent, wap.rearrange("p (k n) -> p k n", k=8), tk
            return load

        def cut(j):
            return lambda v: v[:, :, j * 128:(j + 1) * 128]

        def rows2(k):
            return lambda v: v[:, 2 * k:2 * k + 2, :]

        loads = [(wl2(c0, w), [cut(j) for j in range(w // 128)])
                 for c0, w in ((0, 512), (512, 512), (1024, 512), (1536, 512), (2048, 384))]
        loads += [(wl2(2432 + 512 * q, 512), [rows2(kp) for kp in range(4)]) for q in range(2)]
        loads += [(wl2(3456, 8), [lambda v: v])]
        pre = Ahead(split_items(wr, loads), 2)
        t_h = rms_T("g_mix", l, hT, r1[:, :, :].rearrange("p a b -> p (a b)"))
        t_r1 = K.last("pe")
        rr = [t_r1, t_r1]
        pend = None

        def rope_part(n_, t):
            r = r1[:, n_ % 2, :]
            dst = qT[:, n_, :] if n_ < 16 else iT[:, n_ - 16, :]
            ct, sn, swp = (rope[:, 0, :], rope[:, 1, :], "sw64") if n_ < 16 else (rope[:, 2, :], rope[:, 3, :], "sw32")
            b = bank()
            t2 = mm(b[:, :], C(swp), r, t)
            tt(dst, r, ct, ALU.mult, t, t_rope)
            rr2 = r2[:, n_ % 2, :]
            t3 = tt(rr2, b[:, :], sn, ALU.mult, t2)
            give(b, t3)
            rr[n_ % 2] = [t2, t3]
            tt(dst, dst, rr2, ALU.add)

        for n_ in range(19):
            e2, w2_, tw_ = pre.next()
            b = bank()
            for k in range(8):
                t = mm3(b[:, :], [x[:, k, :] for x in w2_], [x[:, k, :] for x in hT], t_h, tw_, start=(k == 0), stop=(k == 7))
            e2[2] = t
            t = act(r1[:, n_ % 2, :], b[:, :], ACT.Copy, t, rr[n_ % 2])
            give(b, t)
            if pend:
                rope_part(*pend)
            pend = (n_, t)
        for q in range(2):
            bs = [bank() for _ in range(4)]
            for kp in range(4):
                e2, w2_, tw_ = pre.next()
                for i in range(4):
                    for k in range(2):
                        kk = 2 * kp + k
                        t = mm3(bs[i][:, :], [x[:, kk, i * 128:(i + 1) * 128] for x in hT], [x[:, k, :] for x in w2_], tw_,
                                start=(kk == 0), stop=(kk == 7))
                e2[2] = t
                if pend:
                    rope_part(*pend)
                    pend = None
            for i in range(4):
                t2 = act(vt[:, i, q * 512:(q + 1) * 512], bs[i][:, :], ACT.Copy, t)
                give(bs[i], t2)
        e2, w2_, tw_ = pre.next()
        b = bank()
        for i in range(4):
            for k in range(8):
                t = mm3(b[:, 8 * i:8 * i + 8], [x[:, k, i * 128:(i + 1) * 128] for x in hT], [x[:, k, :] for x in w2_], tw_,
                        start=(k == 0), stop=(k == 7))
        t = ts(iw[:, :, :].rearrange("p a b -> p (a b)"), b[:, 0:32], float(32 ** -0.5 * 8 ** -0.5), None, ALU.mult, None, t)
        give(b, t)
        dump(f"qT{l}", qT[:, :, :])
        K.barrier()
        a1.close()

        NW = 3
        sc, wk, zb = (sb(f"{n}{l}", [128, 512], c=at) for n in ("sc", "wk", "zb"))
        big, scr, over = ring.take(4096 + 2048 * NW)
        ym = scr[:, 2048 * NW:2048 * NW + 4096].rearrange("p (k t) -> p k t", k=8)
        for e in ("dve", "act", "pool"):
            K.wait(e, over)
        P = scr[:, 0:1024 * NW].rearrange("p (w a b) -> p w a b", w=NW, a=2)
        PT = scr[:, 1024 * NW:2048 * NW].rearrange("p (w a b c) -> p w a b c", w=NW, a=2, b=4)
        bi, ob = (sb(f"{n}{l}", [128, 4, 512], c=at) for n in ("bi", "ob"))
        m8b = sb(f"m8b{l}", [128, 8], c=at)
        st = sb(f"st{l}", [128, NW, 8], c=at)
        nrm = sb(f"nrm{l}", [128, 2, 16], c=at)
        K.barrier()
        memset(zb[:, :], 0.0, e="dve")
        t_zb = memset(zb[0:64, 448:512], -1e30, e="dve")
        btok = [t_zb, None, None, None]

        def indexer():
            for i in range(1, 4):
                qs = slice(i * 128, (i + 1) * 128)
                ns = 128 * (i + 1)
                S_, W_, B_ = sc[:, 0:ns], wk[:, 0:ns], bi[:, i, 0:ns]
                tr1 = [None, None]
                for h in range(8):
                    hs = slice(32 * (h % 4), 32 * (h % 4) + 32)
                    b = bank()
                    t = mm(b[:, 0:ns], iT[hs, h // 4, qs], iT[hs, 2, 0:ns])
                    t2 = act(r1[:, h % 2, 0:ns], b[:, 0:ns], ACT.Relu, t, tr1[h % 2])
                    give(b, t2)
                    yield
                    if h == 0:
                        tr1[0] = ts(S_, r1[:, 0, 0:ns], iw[:, i, 0:1], None, ALU.mult, None, t2)
                    else:
                        tr1[h % 2] = stt(S_, r1[:, h % 2, 0:ns], iw[:, i, h:h + 1], S_, ALU.mult, ALU.add, t2)
                memset(sc[0:64, ns - 64:ns], -1e30, e="dve")
                src = S_
                for r in range(16):
                    max8(m8b[:, :], src)
                    strike(W_, m8b[:, :], src)
                    src = W_
                    if r % 2:
                        yield
                ts(B_, W_, -2e38, -1.0, ALU.is_lt, ALU.add)
                ts(B_, B_, 1e30, None, ALU.mult, None)
                btok[i] = memset(bi[0:64, i, ns - 64:ns], -1e30, e="dve")
                yield

        ptr_ = [[None, None] for _ in range(NW)]

        def unit(w, i, h, diff):
            qs = slice(i * 128, (i + 1) * 128)
            ns = 128 * (i + 1)
            if diff or i == 0:
                bias, t_b = zb[:, 512 - ns:512], t_zb
            else:
                while btok[i] is None:
                    yield
                bias, t_b = bi[:, i, 0:ns], btok[i]
            o = 8 if diff else 0
            tq = []
            for c in range(2):
                ps_ = slice(64 * c, 64 * c + 64)
                b = bank()
                t = mm(b[:, 0:ns], qT[ps_, o + h, qs], qT[ps_, o + 4 + h, 0:ns])
                tq.append((b, t))
            yield
            s_ = st[:, w, :]
            te = []
            for c in range(2):
                b, t = tq[c]
                t = ttr(P[:, w, c, 0:ns], b[:, 0:ns], bias, 0.125, -3e38, ALU.add, ALU.max, s_[:, c:c + 1], t, t_b, ptr_[w][c])
                give(b, t)
            t = ts(s_[:, 2:4], s_[:, 0:2], -1.0, None, ALU.mult, None)
            for c in range(2):
                t2 = act(P[:, w, c, 0:ns], P[:, w, c, 0:ns], ACT.Exp, t, bias=s_[:, 2 + c:3 + c], accum=s_[:, 4 + c:5 + c])
            yield
            recip(s_[:, 6:8], s_[:, 4:6], t2)
            if diff:
                tt(s_[:, 7:8], s_[:, 7:8], lms[:, 6 + l:7 + l], ALU.mult)
                ts(P[:, w, 0, 0:ns], P[:, w, 0, 0:ns], s_[:, 6:7], None, ALU.mult, None)
                t = stt(P[:, w, 0, 0:ns], P[:, w, 1, 0:ns], s_[:, 7:8], P[:, w, 0, 0:ns], ALU.mult, ALU.add)
            else:
                for c in range(2):
                    t = ts(P[:, w, c, 0:ns], P[:, w, c, 0:ns], s_[:, 6 + c:7 + c], None, ALU.mult, None)
            yield
            tq = []
            for c in range(1 if diff else 2):
                b = bank()
                for j in range(i + 1):
                    t2 = tr(b[:, j * 128:(j + 1) * 128], P[:, w, c, j * 128:(j + 1) * 128], ident, t)
                ptr_[w][c] = t2
                tq.append((b, t2))
            yield
            tp = []
            for c, (b, t2) in enumerate(tq):
                t = copy(PT[:, w, c, 0:i + 1, :].rearrange("p a b -> p (a b)"), b[:, 0:ns], t2, ptv[w][c], e="act")
                give(b, t)
                tp.append(t)
            yield
            bo = bank()
            if diff:
                for j in range(i + 1):
                    t = mm(bo[:, 0:128], PT[:, w, 0, j, :], vt[:, j, 512 + 128 * h:640 + 128 * h], tp[0], start=(j == 0), stop=(j == i))
                ptv[w][0] = t
                yield
                t = act(ob[:, i, 128 * h:128 * h + 128], bo[:, 0:128], ACT.Copy, t)
            else:
                for c in range(2):
                    ps_ = slice(64 * c, 64 * c + 64)
                    for j in range(i + 1):
                        t = mm(bo[ps_, 0:128], vt[:, j, 128 * h + 64 * c:128 * h + 64 * c + 64], PT[:, w, c, j, :], tp[c],
                               start=(j == 0), stop=(j == i))
                    ptv[w][c] = t
                yield
                t = act(ym[:, h, qs], bo[:, 0:128], ACT.Copy, t)
            give(bo, t)

        ptv = [[None, None] for _ in range(NW)]
        todo = [(0, h, d) for d in (0, 1) for h in range(4)] + [(1, h, 1) for h in range(4)] + \
               [(2, h, 1) for h in range(4)] + [(1, h, 0) for h in range(4)] + [(3, h, 1) for h in range(4)] + \
               [(2, h, 0) for h in range(4)] + [(3, h, 0) for h in range(4)]

        def worker(w):
            while todo:
                i, h, d = todo.pop(0)
                yield from unit(w, i, h, d)
                yield

        run(indexer(), *[worker(w) for w in range(NW)])
        t0 = K.last("act")
        for i in range(4):
            for h in range(4):
                o_ = ob[:, i, 128 * h:128 * h + 128]
                ttr(r1[:, 0, 0:128], o_, o_, 1.0, 0.0, ALU.mult, ALU.add, nrm[:, 0, 4 * i + h:4 * i + h + 1], t0)
        t = act(nrm[:, 1, :], nrm[:, 0, :], ACT.Sqrt, K.last("dve"), bias=EPS6, scale=1.0 / 128)
        recip(nrm[:, 0, :], nrm[:, 1, :], t)
        li = 0.8 - 0.6 * float(np.exp(-0.3 * l))
        for i in range(4):
            t = tt(v4(ob[:, i, :]), v4(ob[:, i, :]), bc(nrm[:, 0, 4 * i:4 * i + 4], 128), ALU.mult)
            b = bank()
            for h in range(4):
                t2 = tr(b[:, h * 128:(h + 1) * 128], ob[:, i, h * 128:(h + 1) * 128], ident, t)
            t = act(ym[:, 4:8, i * 128:(i + 1) * 128], v4(b[:, :]), ACT.Copy, t2, scale=gsc[:, l:l + 1])
            give(b, t)
        dump(f"ymb{l}", ym[:, :, :])
        K.barrier()
        at.close()
        po = ExitStack()
        yh = [sb(f"ys{l}{q}", [128, 8, 512], R32, c=po) for q in "hl"]
        wr = Ring(K, sb(f"wo{l}", [128, 8192], R32, c=po), 8192)
        def wlo(hf):
            def load():
                ent, wap, tk = ring.load([(0, 4096, 8, A["w_out_2"][l][:, hf * 512:(hf + 1) * 512].rearrange("(k p) n -> p k n", p=128))], 4096)
                return ent, wap.rearrange("p (k n) -> p k n", k=8), tk
            return load

        t_ys = [split(yh[0][:, k, :], yh[1][:, k, :], ym[:, k, :]) for k in range(8)]
        big[2] = t_ys[7]
        pre = Ahead(split_items(wr, [(wlo(hf), [rows2(kp) for kp in range(4)]) for hf in range(2)]), 3)
        for hf in range(2):
            bs = [bank() for _ in range(4)]
            for kp in range(4):
                e2, w2_, tw_ = pre.next()
                for i in range(4):
                    for k in range(2):
                        kk = 2 * kp + k
                        t = mm3(bs[i][:, :], [x[:, kk, i * 128:(i + 1) * 128] for x in yh], [x[:, k, :] for x in w2_], tw_, t_ys[kk],
                                start=(kk == 0), stop=(kk == 7))
                e2[2] = t
            for i in range(4):
                hs = slice(hf * 512, (hf + 1) * 512)
                t2 = tt(xt[:, i, hs], xt[:, i, hs], bs[i][:, :], ALU.add, t)
                give(bs[i], t2)
        K.barrier()
        po.close()
        dump(f"xa{l}", xt[:, :, :])
        ff = ExitStack()
        hT = [sb(f"hU{l}{q}", [128, 8, 512], R32, c=ff) for q in "hl"]
        hh = [sb(f"hf{l}{q}", [128, 11, 512], R32, c=ff) for q in "hl"]
        gsl = sb(f"gsl{l}", [128, 2, 512], c=ff)
        wr = Ring(K, sb(f"wf{l}", [128, 8192], R32, c=ff), 8192)
        def wlg(c0, w_):
            def load():
                ws = [A[n_][l][:, c0:c0 + w_].rearrange("(k p) n -> p k n", p=128) for n_ in ("w_gate", "w_up")]
                ent, wap, tk = ring.load([(q * 8 * w_, 8 * w_, 8, ws[q]) for q in range(2)], 16 * w_)
                return ent, wap.rearrange("p (q k n) -> p q k n", q=2, k=8), tk
            return load

        def wld(r0, nf, hf):
            def load():
                src = A["w_down"][l][r0:r0 + nf * 128, hf * 512:(hf + 1) * 512].rearrange("(k p) n -> p k n", p=128)
                ent, wap, tk = ring.load([(0, nf * 512, nf, src)], nf * 512)
                return ent, wap.rearrange("p (k n) -> p k n", k=nf), tk
            return load

        def part(q, f_):
            return lambda v: v[:, q, :, f_ * 128:(f_ + 1) * 128]

        def rows_(k0, k1):
            return lambda v: v[:, k0:k1, :]

        loads = []
        for grp in range(2):
            for f0 in range(0, 11, 2):
                nf = min(2, 11 - f0)
                loads.append((wlg((grp * 11 + f0) * 128, nf * 128), [part(q, f_) for f_ in range(nf) for q in range(2)]))
            for hf in range(2):
                for f0 in range(0, 11, 4):
                    nf = min(4, 11 - f0)
                    loads.append((wld((grp * 11 + f0) * 128, nf, hf), [rows_(k, min(k + 2, nf)) for k in range(0, nf, 2)]))
        pre = Ahead(split_items(wr, loads), 3)
        t_h = rms_T("g_ffn", l, hT, gsl[:, :, :].rearrange("p a b -> p (a b)"))
        t_dn = None
        gr = [K.last("pe")] * 2
        for grp in range(2):
            for f0 in range(11):
                pr = []
                for q in range(2):
                    e2, w2_, tw_ = pre.next()
                    b = bank()
                    for k in range(8):
                        t = mm3(b[:, :], [x[:, k, :] for x in w2_], [x[:, k, :] for x in hT], t_h, tw_, start=(k == 0), stop=(k == 7))
                    e2[2] = t
                    pr.append((b, t))
                g_ = gsl[:, f0 % 2, :]
                t = act(g_, pr[0][0][:, :], ACT.Silu, pr[0][1], gr[f0 % 2])
                give(pr[0][0], t)
                t = tt(g_, g_, pr[1][0][:, :], ALU.mult, t, pr[1][1])
                give(pr[1][0], t)
                gr[f0 % 2] = split(hh[0][:, f0, :], hh[1][:, f0, :], g_, t, t_dn)
            t_hf = K.last("dve")
            for hf in range(2):
                bs = [bank() for _ in range(4)]
                for f0 in range(0, 11, 2):
                    e2, w2_, tw_ = pre.next()
                    for i in range(4):
                        for q in range(min(2, 11 - f0)):
                            t = mm3(bs[i][:, :], [x[:, f0 + q, i * 128:(i + 1) * 128] for x in hh], [x[:, q, :] for x in w2_], tw_, t_hf,
                                    start=(f0 + q == 0), stop=(f0 + q == 10))
                    e2[2] = t
                t_dn = t
                for i in range(4):
                    hs = slice(hf * 512, (hf + 1) * 512)
                    t2 = tt(xt[:, i, hs], xt[:, i, hs], bs[i][:, :], ALU.add, t)
                    give(bs[i], t2)
        K.barrier()
        ff.close()
        dump(f"xf{l}", xt[:, :, :])
    gfr = sb("gfr", [128, D], c=m6)[:, :]
    t_gf = rowload(gfr, "gfin", K.all())
    od = out.rearrange("(b p) d -> p b d", p=128)
    for i in range(4):
        rms_rows(xt[:, i, :])
        t = stt(xt[:, i, :], xt[:, i, :], rstd[:, 0:1], gfr, ALU.mult, ALU.mult, t_gf)
        t_o = K.dma("sp", lambda e, i=i: e.dma_start(od[:, i, :], xt[:, i, :]), t)
        K.wait("sp", t_o)
    for i in range(len(K.dn)):
        if K.dn[i]:
            K.wait("sp", (f"d{i}", K.dsem[i], K.dn[i]))
    m6.close()
    K.emit()


def _layout(I):
    a = {k: np.asarray(v) for k, v in I.items()}

    def colp(v):
        return v.reshape(-1, 128).T

    cols = {
        "conv_w": colp(a["ssd_conv_w"][0]), "conv_b": colp(a["ssd_conv_b"][0]), "mu": colp(a["rwkv_mu"][0]),
        "a0": colp(a["rwkv_a0"][0]), "kk": colp(a["rwkv_kk"][0]), "ka": colp(a["rwkv_ka"][0]),
        "rk": colp(a["rwkv_rk"][0]), "lnw": colp(a["rwkv_lnx_w"][0]), "lnb": colp(a["rwkv_lnx_b"][0]),
        "c": colp(a["c"][0]), "cc": colp(a["c_ctx"]), "g_mix": colp(a["g_mix_2"]), "g_ffn": colp(a["g_ffn_2"]),
        "g_sub": colp(a["g_subln_2"]), "gla_w": colp(a["gla_norm_w"][0]), "ssd_w": colp(a["ssd_norm_w"][0]),
    }
    rows = {
        "dtb": a["ssd_dt_bias"], "alog": a["ssd_a_log"], "ssd_d": a["ssd_d"], "w0": a["rwkv_w0"], "gb": a["gla_gb"],
        "ln1w": a["ln1_w"], "ln1b": a["ln1_b"], "ln2w": a["ln2_w"], "ln2b": a["ln2_b"], "rb": a["router_b"],
        "gfin": a["g_final_2"],
        "lam": np.stack([a["lam_q1_2"], a["lam_k1_2"], a["lam_q2_2"], a["lam_k2_2"]], 1),
    }

    def bdiag(x, n):
        k, m = x.shape[1:]
        o = np.zeros((n, 2 * m), x.dtype)
        for i in range(2):
            o[i * k:(i + 1) * k, i * m:(i + 1) * m] = x[i]
        return o

    def expert(w1, w3, w2):
        n = w1.shape[0]
        f = lambda w, k: w.reshape(n, k, 128, -1).transpose(0, 2, 1, 3).reshape(n, 128, -1)
        w13 = np.concatenate([w1.reshape(n, 8, 128, -1), w3.reshape(n, 8, 128, -1)], 3)
        return np.concatenate([w13.transpose(0, 2, 1, 3).reshape(n, 128, -1), f(w2, 2)], 2)

    W = a["w_in_2"]
    ik = W[:, :, 1792:1824]
    w_in_2 = np.concatenate([W[:, :, 0:1024], W[:, :, 1832:2856], W[:, :, 1536:1792], ik, ik, ik, ik,
                             W[:, :, 1024:1536], W[:, :, 2856:3368], W[:, :, 1824:1832]], 2)
    out = {
        "x": a["x"][0], "ctx": a["ctx"][0], "ada_w": a["ada_w"][0], "ada_b": a["ada_b"], "w_in": a["w_in"][0],
        "cst": _const_mats()[1], "rope": _rope_tables(),
        "cols": np.concatenate([cols[n] for n, _ in COLS], 1),
        "rows": np.concatenate([rows[n].reshape(1, -1) for n, _ in ROWS], 1),
        "gux": bdiag(a["gla_gu"][0], 32), "w2x": bdiag(a["rwkv_w2"][0], 128), "a2x": bdiag(a["rwkv_a2"][0], 128),
        "g2": a["rwkv_g2"][0], "w_out": a["w_out"][0], "router_w": a["router_w"][0],
        "ew": expert(a["exp_w1"][0], a["exp_w3"][0], a["exp_w2"][0]),
        "sw": expert(a["sh_w1"], a["sh_w3"], a["sh_w2"])[0],
        "w_in_2": w_in_2, "w_out_2": a["w_out_2"], "w_gate": a["w_gate_2"], "w_up": a["w_up_2"], "w_down": a["w_down_2"],
    }
    return {k: np.ascontiguousarray(v) for k, v in out.items()}


def _declare(nc, arrays):
    return {k: nc.dram_tensor("in_" + k, v.shape, mybir.dt.from_np(v.dtype), kind="ExternalInput").ap()
            for k, v in arrays.items()}


def kernel(**inputs):
    import concourse.bacc as _bacc
    from concourse.bass_utils import run_bass_kernel_spmd as _run

    nc = _bacc.Bacc("TRN2", target_bir_lowering=False, num_devices=1)
    arrays = _layout(inputs)
    A = _declare(nc, arrays)
    out = nc.dram_tensor("out", (512, 1024), F32, kind="ExternalOutput").ap()
    build(nc, A, out)
    r = _run(nc, [{"in_" + k: v for k, v in arrays.items()}], core_ids=[0])
    return r.results[0]["out"].reshape(1, 512, 1024)
```
